# Optimizing a Trainium2 kernel written in Bass

```python
import math
import jax, jax.numpy as jnp
from jax import lax
import numpy as np

D_MODEL = 1024
BATCH = 1
SEQ = 512
DEPTH = 2

MLA_HEADS = 8
MLA_NOPE_DIM = 128
MLA_ROPE_DIM = 64
MLA_V_DIM = 128
MLA_Q_RANK = 384
MLA_KV_RANK = 256
ROPE_THETA = 10000.0
SWA_Q_HEADS = 16
SWA_KV_HEADS = 4
SWA_HEAD_DIM = 64
WINDOW = 128
REL_BUCKETS = 32
REL_MAX_DIST = 128
D_FF = 4 * D_MODEL
BLOCK = 128
LN_EPS = 1e-5
RMS_EPS = 1e-6


def _layernorm(x, g, b):
    xf = x.astype(jnp.float32)
    mu = xf.mean(-1, keepdims=True)
    var = jnp.square(xf - mu).mean(-1, keepdims=True)
    return ((xf - mu) * lax.rsqrt(var + LN_EPS) * g + b).astype(x.dtype)

def _rmsnorm(x, g):
    xf = x.astype(jnp.float32)
    return (xf * lax.rsqrt(jnp.mean(xf * xf, -1, keepdims=True) + RMS_EPS) * g).astype(x.dtype)

def _rope(x, pos):
    half = x.shape[-1] // 2
    inv = ROPE_THETA ** (-jnp.arange(half, dtype=jnp.float32) / half)
    ang = pos.astype(jnp.float32)[:, None] * inv[None, :]
    ang = ang.reshape(ang.shape[:1] + (1,) * (x.ndim - 3) + ang.shape[1:])
    cos, sin = jnp.cos(ang), jnp.sin(ang)
    xf = x.astype(jnp.float32)
    x1, x2 = xf[..., :half], xf[..., half:]
    return jnp.concatenate([x1 * cos - x2 * sin, x1 * sin + x2 * cos], -1).astype(x.dtype)

def _t5_bucket(dist):
    n = jnp.maximum(dist, 0)
    max_exact = REL_BUCKETS // 2
    nf = jnp.maximum(n, 1).astype(jnp.float32)
    large = max_exact + (jnp.log(nf / max_exact) / math.log(REL_MAX_DIST / max_exact)
                         * (REL_BUCKETS - max_exact)).astype(jnp.int32)
    large = jnp.minimum(large, REL_BUCKETS - 1)
    return jnp.where(n < max_exact, n, large)

def _to_blocks(t, nb):
    return t.reshape((t.shape[0], nb, BLOCK) + t.shape[2:]).swapaxes(0, 1)

def _mla(x, w_in, g_q, g_kv, w_uq, w_uk, w_uv, w_o, pos):
    B, S, _ = x.shape
    nb = S // BLOCK
    h = x @ w_in
    c_q = _rmsnorm(h[..., :MLA_Q_RANK], g_q)
    c_kv = _rmsnorm(h[..., MLA_Q_RANK:MLA_Q_RANK + MLA_KV_RANK], g_kv)
    k_r = _rope(h[..., MLA_Q_RANK + MLA_KV_RANK:], pos)
    q = jnp.einsum('bsr,rhd->bshd', c_q, w_uq)
    q_n = q[..., :MLA_NOPE_DIM]
    q_r = _rope(q[..., MLA_NOPE_DIM:], pos)
    q_lat = jnp.einsum('bshn,chn->bshc', q_n, w_uk)
    scale = (MLA_NOPE_DIM + MLA_ROPE_DIM) ** -0.5
    kpos = jnp.arange(S)

    def block(args):
        ql, qr, i = args
        s = (jnp.einsum('bqhc,bkc->bhqk', ql, c_kv)
             + jnp.einsum('bqhr,bkr->bhqk', qr, k_r)).astype(jnp.float32) * scale
        qpos = i * BLOCK + jnp.arange(BLOCK)
        s = jnp.where(kpos[None, :] <= qpos[:, None], s, -jnp.inf)
        p = jax.nn.softmax(s, axis=-1).astype(x.dtype)
        return jnp.einsum('bhqk,bkc->bqhc', p, c_kv)

    o_lat = lax.map(block, (_to_blocks(q_lat, nb), _to_blocks(q_r, nb), jnp.arange(nb)))
    o_lat = o_lat.swapaxes(0, 1).reshape(B, S, MLA_HEADS, MLA_KV_RANK)
    o = jnp.einsum('bshc,chv->bshv', o_lat, w_uv).reshape(B, S, MLA_HEADS * MLA_V_DIM)
    return o @ w_o

def _shared_kv(x, w_kv):
    B, S, _ = x.shape
    nb = S // BLOCK
    kv = (x @ w_kv).reshape(B, nb, BLOCK, 2, SWA_KV_HEADS, SWA_HEAD_DIM)
    k, v = kv[:, :, :, 0], kv[:, :, :, 1]

    def band(t):
        prev = jnp.pad(t, ((0, 0), (1, 0), (0, 0), (0, 0), (0, 0)))[:, :-1]
        return jnp.concatenate([prev, t], axis=2)

    return band(k), band(v)

def _swa(x, w_q, sinks, w_o, k_band, v_band, rel_bias):
    B, S, _ = x.shape
    nb = S // BLOCK
    G = SWA_Q_HEADS // SWA_KV_HEADS
    q = (x @ w_q).reshape(B, nb, BLOCK, SWA_KV_HEADS, G, SWA_HEAD_DIM)
    s = jnp.einsum('bnqkgd,bnjkd->bnkgqj', q, k_band).astype(jnp.float32) * SWA_HEAD_DIM ** -0.5
    i = jnp.arange(BLOCK)
    j = jnp.arange(2 * BLOCK)
    dist = i[:, None] + BLOCK - j[None, :]
    bias = rel_bias[_t5_bucket(dist)].astype(jnp.float32)
    bias = bias.transpose(2, 0, 1).reshape(SWA_KV_HEADS, G, BLOCK, 2 * BLOCK)
    kpos = jnp.arange(nb)[:, None] * BLOCK - BLOCK + j[None, :]
    valid = (dist >= 0) & (dist < WINDOW)
    mask = valid[None] & (kpos >= 0)[:, None, :]
    s = jnp.where(mask[None, :, None, None], s + bias, -jnp.inf)
    sink = sinks.astype(jnp.float32).reshape(SWA_KV_HEADS, G)[..., None]
    m = jnp.maximum(s.max(-1), sink)
    p = jnp.exp(s - m[..., None])
    denom = p.sum(-1) + jnp.exp(sink - m)
    p = (p / denom[..., None]).astype(x.dtype)
    o = jnp.einsum('bnkgqj,bnjkd->bnqkgd', p, v_band).reshape(B, S, SWA_Q_HEADS * SWA_HEAD_DIM)
    return o @ w_o

def _mlp(x, w_up, w_down):
    h = jax.nn.relu(x @ w_up)
    return (h * h) @ w_down

def first_inputs(seed: int = 0) -> dict:
    key = jax.random.key(seed)
    ks = jax.random.split(key, 20)
    n_a = DEPTH // 2
    n_b = DEPTH - n_a
    beta = (8 * DEPTH) ** -0.25
    f32 = jnp.float32

    def nrm(k, shape, fan_in, gain=1.0):
        return jax.random.normal(k, shape, f32) * (gain * fan_in ** -0.5)

    in_w = MLA_Q_RANK + MLA_KV_RANK + MLA_ROPE_DIM
    kv_k = nrm(ks[8], (D_MODEL, 1, SWA_KV_HEADS * SWA_HEAD_DIM), D_MODEL)
    kv_v = nrm(ks[9], (D_MODEL, 1, SWA_KV_HEADS * SWA_HEAD_DIM), D_MODEL, beta)
    return {
        'x': jax.random.normal(ks[0], (BATCH, SEQ, D_MODEL), f32),
        'mla_w_in': nrm(ks[1], (n_a, D_MODEL, in_w), D_MODEL),
        'mla_g_q': 1.0 + 0.05 * jax.random.normal(ks[2], (n_a, MLA_Q_RANK), f32),
        'mla_g_kv': 1.0 + 0.05 * jax.random.normal(ks[3], (n_a, MLA_KV_RANK), f32),
        'mla_w_uq': nrm(ks[4], (n_a, MLA_Q_RANK, MLA_HEADS, MLA_NOPE_DIM + MLA_ROPE_DIM), MLA_Q_RANK),
        'mla_w_uk': nrm(ks[5], (n_a, MLA_KV_RANK, MLA_HEADS, MLA_NOPE_DIM), MLA_KV_RANK),
        'mla_w_uv': nrm(ks[6], (n_a, MLA_KV_RANK, MLA_HEADS, MLA_V_DIM), MLA_KV_RANK, beta),
        'mla_w_o': nrm(ks[7], (n_a, MLA_HEADS * MLA_V_DIM, D_MODEL), MLA_HEADS * MLA_V_DIM, beta),
        'kv_w_shared': jnp.concatenate([kv_k, kv_v], axis=1).reshape(D_MODEL, 2 * SWA_KV_HEADS * SWA_HEAD_DIM),
        'swa_w_q': nrm(ks[10], (n_b, D_MODEL, SWA_Q_HEADS * SWA_HEAD_DIM), D_MODEL),
        'swa_sinks': 0.5 * jax.random.normal(ks[11], (n_b, SWA_Q_HEADS), f32),
        'swa_w_o': nrm(ks[12], (n_b, SWA_Q_HEADS * SWA_HEAD_DIM, D_MODEL), SWA_Q_HEADS * SWA_HEAD_DIM, beta),
        'rel_bias': 0.5 * jax.random.normal(ks[13], (REL_BUCKETS, SWA_Q_HEADS), f32),
        'mlp_w_up': nrm(ks[14], (DEPTH, D_MODEL, D_FF), D_MODEL),
        'mlp_w_down': nrm(ks[15], (DEPTH, D_FF, D_MODEL), D_FF, beta),
        'ln_mix_g': 1.0 + 0.05 * jax.random.normal(ks[16], (DEPTH, D_MODEL), f32),
        'ln_mix_b': 0.02 * jax.random.normal(ks[17], (DEPTH, D_MODEL), f32),
        'ln_mlp_g': 1.0 + 0.05 * jax.random.normal(ks[18], (DEPTH, D_MODEL), f32),
        'ln_mlp_b': 0.02 * jax.random.normal(ks[19], (DEPTH, D_MODEL), f32),
    }

def first_block(x, mla_w_in, mla_g_q, mla_g_kv, mla_w_uq, mla_w_uk, mla_w_uv, mla_w_o,
              kv_w_shared, swa_w_q, swa_sinks, swa_w_o, rel_bias,
              mlp_w_up, mlp_w_down, ln_mix_g, ln_mix_b, ln_mlp_g, ln_mlp_b):
    alpha = (2 * DEPTH) ** 0.25
    n_a = DEPTH // 2
    pos = jnp.arange(x.shape[1])
    k_band = v_band = None
    for l in range(DEPTH):
        if l < n_a:
            y = _mla(x, mla_w_in[l], mla_g_q[l], mla_g_kv[l], mla_w_uq[l], mla_w_uk[l],
                     mla_w_uv[l], mla_w_o[l], pos)
        else:
            if l == n_a:
                k_band, v_band = _shared_kv(x, kv_w_shared)
            b = l - n_a
            y = _swa(x, swa_w_q[b], swa_sinks[b], swa_w_o[b], k_band, v_band, rel_bias)
        x = _layernorm(alpha * x + y, ln_mix_g[l], ln_mix_b[l])
        x = _layernorm(alpha * x + _mlp(x, mlp_w_up[l], mlp_w_down[l]), ln_mlp_g[l], ln_mlp_b[l])
    return x


DEPTH_2 = 1

CHUNK = 64
Q_BLOCK = 128
EPS = 1e-6

MLSTM_HEADS = 4
MLSTM_HD = D_MODEL // MLSTM_HEADS
MLSTM_W = MLSTM_HEADS * MLSTM_HD
CONV_K = 4

DIFF_HEADS = 8
DIFF_HD = D_MODEL // (2 * DIFF_HEADS)
DIFF_W = DIFF_HEADS * 2 * DIFF_HD

RET_HEADS = 4
RET_HD = D_MODEL // RET_HEADS
RET_W = RET_HEADS * RET_HD

FFN_HIDDEN = -(-8 * D_MODEL // (3 * 256)) * 256

IN_SIZES = (MLSTM_W, MLSTM_W, MLSTM_W, MLSTM_W, MLSTM_HEADS, MLSTM_HEADS,
            DIFF_W, DIFF_W, DIFF_W,
            RET_W, RET_W, RET_W, RET_W,
            3 * D_MODEL)
N_IN = sum(IN_SIZES)


def rmsnorm(x, g):
    x32 = x.astype(jnp.float32)
    y = x32 * lax.rsqrt(jnp.mean(x32 * x32, axis=-1, keepdims=True) + EPS)
    return (y * g.astype(jnp.float32)).astype(x.dtype)

def head_rms(x):
    x32 = x.astype(jnp.float32)
    return x32 * lax.rsqrt(jnp.mean(x32 * x32, axis=-1, keepdims=True) + EPS)

def causal_dwconv(x, w):
    K = w.shape[0]
    S = x.shape[1]
    xp = jnp.pad(x, ((0, 0), (K - 1, 0), (0, 0)))
    out = xp[:, 0:S] * w[0]
    for j in range(1, K):
        out = out + xp[:, j:j + S] * w[j]
    return out

def to_chunks(a):
    B, S = a.shape[0], a.shape[1]
    return jnp.moveaxis(a.reshape(B, S // CHUNK, CHUNK, *a.shape[2:]), 1, 0)

def from_chunks(a):
    a = jnp.moveaxis(a, 0, 1)
    return a.reshape(a.shape[0], a.shape[1] * a.shape[2], *a.shape[3:])

def mlstm(q, k, v, i_pre, f_pre):
    B, S, H, dh = q.shape
    f32 = jnp.float32
    q = q.astype(f32)
    k = k.astype(f32) * (dh ** -0.5)
    v = v.astype(f32)
    logf = jax.nn.log_sigmoid(f_pre.astype(f32))
    ig = i_pre.astype(f32)
    causal = jnp.tril(jnp.ones((CHUNK, CHUNK), dtype=bool))

    def step(carry, inp):
        C, n, m = carry
        qj, kj, vj, lf, igj = inp
        b = jnp.cumsum(lf, axis=1).transpose(0, 2, 1)
        igT = igj.transpose(0, 2, 1)
        g = b[..., -1]
        d_intra = b[..., :, None] - b[..., None, :] + igT[..., None, :]
        d_intra = jnp.where(causal, d_intra, -jnp.inf)
        d_inter = b + m[..., None]
        m_row = jnp.maximum(jnp.max(d_intra, axis=-1), d_inter)
        w_intra = jnp.exp(d_intra - m_row[..., None])
        w_inter = jnp.exp(d_inter - m_row)
        s = jnp.einsum('blhd,bshd->bhls', qj, kj) * w_intra
        w_int_t = w_inter.transpose(0, 2, 1)[..., None]
        num = (jnp.einsum('bhls,bshe->blhe', s, vj)
               + jnp.einsum('blhd,bhde->blhe', qj, C) * w_int_t)
        den = jnp.sum(s, axis=-1) + jnp.einsum('blhd,bhd->bhl', qj, n) * w_inter
        den = jnp.maximum(jnp.abs(den), jnp.exp(-m_row))
        h = num / den.transpose(0, 2, 1)[..., None]
        a = g[..., None] - b + igT
        m_new = jnp.maximum(g + m, jnp.max(a, axis=-1))
        w_old = jnp.exp(g + m - m_new)
        w_k = jnp.exp(a - m_new[..., None])
        C_new = w_old[..., None, None] * C + jnp.einsum('bhs,bshd,bshe->bhde', w_k, kj, vj)
        n_new = w_old[..., None] * n + jnp.einsum('bhs,bshd->bhd', w_k, kj)
        return (C_new, n_new, m_new), h

    init = (jnp.zeros((B, H, dh, dh), f32), jnp.zeros((B, H, dh), f32), jnp.zeros((B, H), f32))
    xs = (to_chunks(q), to_chunks(k), to_chunks(v), to_chunks(logf), to_chunks(ig))
    _, hs = lax.scan(step, init, xs)
    return from_chunks(hs)

def retention(q, k, v):
    B, S, H, dh = q.shape
    f32 = jnp.float32
    q = q.astype(f32)
    k = k.astype(f32) * (dh ** -0.5)
    v = v.astype(f32)
    log_gamma = jnp.log(1.0 - 2.0 ** (-5.0 - jnp.arange(H, dtype=f32)))
    pos = jnp.arange(CHUNK, dtype=f32)
    rel = pos[:, None] - pos[None, :]
    dmask = jnp.where(rel[None] >= 0, jnp.exp(log_gamma[:, None, None] * jnp.maximum(rel, 0.0)[None]), 0.0)
    xi = jnp.exp(log_gamma[None, :] * (pos[:, None] + 1.0))
    zeta = jnp.exp(log_gamma[:, None] * (CHUNK - 1.0 - pos[None, :]))
    chunk_decay = jnp.exp(log_gamma * CHUNK)

    def step(R, inp):
        qj, kj, vj = inp
        s = jnp.einsum('blhd,bshd->bhls', qj, kj) * dmask[None]
        o = (jnp.einsum('bhls,bshe->blhe', s, vj)
             + jnp.einsum('blhd,bhde->blhe', qj, R) * xi[None, :, :, None])
        R_new = chunk_decay[None, :, None, None] * R + jnp.einsum('hs,bshd,bshe->bhde', zeta, kj, vj)
        return R_new, o

    R0 = jnp.zeros((B, H, dh, dh), f32)
    _, os_ = lax.scan(step, R0, (to_chunks(q), to_chunks(k), to_chunks(v)))
    return from_chunks(os_)

def diff_attention(q, k, v, lam):
    B, S, H, _, dh = q.shape
    f32 = jnp.float32
    q = q.astype(f32) * (dh ** -0.5)
    k = k.astype(f32)
    v = v.astype(f32)
    slopes = 2.0 ** (-8.0 * (jnp.arange(H, dtype=f32) + 1.0) / H)
    outs = []
    for blk in range(S // Q_BLOCK):
        q0 = blk * Q_BLOCK
        kend = q0 + Q_BLOCK
        qb = q[:, q0:kend]
        kb = k[:, :kend]
        vb = v[:, :kend]
        s = jnp.einsum('bqhcd,bkhcd->bhcqk', qb, kb)
        tq = jnp.arange(q0, kend)
        tk = jnp.arange(kend)
        dist = jnp.abs(tq[:, None] - tk[None, :]).astype(f32)
        allowed = (tk // CHUNK)[None, :] <= (tq // CHUNK)[:, None]
        bias = -slopes[:, None, None] * dist[None]
        s = jnp.where(allowed, s + bias[None, :, None], -jnp.inf)
        p = jax.nn.softmax(s, axis=-1)
        a = p[:, :, 0] - lam * p[:, :, 1]
        outs.append(jnp.einsum('bhqk,bkhe->bqhe', a, vb))
    return jnp.concatenate(outs, axis=1)

def split_in(proj):
    idx = np.cumsum(np.array(IN_SIZES))[:-1].tolist()
    return jnp.split(proj, idx, axis=-1)

def second_inputs(seed: int = 0) -> dict:
    key = jax.random.key(seed)
    ks = jax.random.split(key, 16)
    f32 = jnp.float32

    def nrm(kk, shape, scale):
        return jax.random.normal(kk, shape, f32) * scale

    x = nrm(ks[0], (BATCH, SEQ, D_MODEL), 1.0)
    norm_gains = 1.0 + nrm(ks[1], (DEPTH_2, 4, D_MODEL), 0.05)
    w_in = nrm(ks[2], (DEPTH_2, D_MODEL, N_IN), D_MODEL ** -0.5)
    mlstm_conv = nrm(ks[3], (DEPTH_2, CONV_K, 2 * MLSTM_W), CONV_K ** -0.5)
    f_bias = jnp.broadcast_to(jnp.linspace(3.0, 6.0, MLSTM_HEADS, dtype=f32), (DEPTH_2, MLSTM_HEADS))
    i_bias = jnp.zeros((DEPTH_2, MLSTM_HEADS), f32)
    mlstm_gate_bias = jnp.stack([i_bias, f_bias], axis=1) + nrm(ks[4], (DEPTH_2, 2, MLSTM_HEADS), 0.1)
    diff_lambda = nrm(ks[5], (DEPTH_2, 4, DIFF_HD), 0.1)
    diff_subln = 1.0 + nrm(ks[6], (DEPTH_2, 2 * DIFF_HD), 0.05)
    w_mlstm_out = nrm(ks[7], (DEPTH_2, MLSTM_W, D_MODEL), MLSTM_W ** -0.5)
    w_diff_out = nrm(ks[8], (DEPTH_2, DIFF_W, D_MODEL), DIFF_W ** -0.5)
    w_ret_out = nrm(ks[9], (DEPTH_2, RET_W, D_MODEL), RET_W ** -0.5)
    w_out = nrm(ks[10], (DEPTH_2, D_MODEL, D_MODEL), D_MODEL ** -0.5)
    w_ffn_in = nrm(ks[11], (DEPTH_2, D_MODEL, 2 * FFN_HIDDEN), D_MODEL ** -0.5)
    w_ffn_out = nrm(ks[12], (DEPTH_2, FFN_HIDDEN, D_MODEL), FFN_HIDDEN ** -0.5)
    return {"x": x, "norm_gains": norm_gains, "w_in": w_in, "mlstm_conv": mlstm_conv,
            "mlstm_gate_bias": mlstm_gate_bias, "diff_lambda": diff_lambda,
            "diff_subln": diff_subln, "w_mlstm_out": w_mlstm_out, "w_diff_out": w_diff_out,
            "w_ret_out": w_ret_out, "w_out": w_out, "w_ffn_in": w_ffn_in,
            "w_ffn_out": w_ffn_out}

def second_block(x, norm_gains, w_in, mlstm_conv, mlstm_gate_bias, diff_lambda, diff_subln,
              w_mlstm_out, w_diff_out, w_ret_out, w_out, w_ffn_in, w_ffn_out):
    B, S, _ = x.shape
    f32 = jnp.float32
    for l in range(DEPTH_2):
        g = norm_gains[l]
        h = rmsnorm(x, g[0])
        proj = h @ w_in[l]
        (mq, mk, mv, mo, mi, mf, dq, dk, dv, rq, rk, rv, rg, gates) = split_in(proj)

        qk = jax.nn.silu(causal_dwconv(jnp.concatenate([mq, mk], axis=-1), mlstm_conv[l]))
        mq_c, mk_c = jnp.split(qk, 2, axis=-1)
        hm = mlstm(mq_c.reshape(B, S, MLSTM_HEADS, MLSTM_HD),
                   mk_c.reshape(B, S, MLSTM_HEADS, MLSTM_HD),
                   mv.reshape(B, S, MLSTM_HEADS, MLSTM_HD),
                   mi + mlstm_gate_bias[l, 0],
                   mf + mlstm_gate_bias[l, 1])
        hm = jax.nn.sigmoid(mo.astype(f32)) * head_rms(hm).reshape(B, S, MLSTM_W)

        lam_init = 0.8 - 0.6 * math.exp(-0.3 * l)
        lmb = diff_lambda[l].astype(f32)
        lam = jnp.exp(jnp.sum(lmb[0] * lmb[1])) - jnp.exp(jnp.sum(lmb[2] * lmb[3])) + lam_init
        hd = diff_attention(dq.reshape(B, S, DIFF_HEADS, 2, DIFF_HD),
                            dk.reshape(B, S, DIFF_HEADS, 2, DIFF_HD),
                            dv.reshape(B, S, DIFF_HEADS, 2 * DIFF_HD), lam)
        hd = (rmsnorm(hd, diff_subln[l]) * (1.0 - lam_init)).reshape(B, S, DIFF_W)

        hr = retention(rq.reshape(B, S, RET_HEADS, RET_HD),
                       rk.reshape(B, S, RET_HEADS, RET_HD),
                       rv.reshape(B, S, RET_HEADS, RET_HD))
        hr = jax.nn.silu(rg.astype(f32)) * head_rms(hr).reshape(B, S, RET_W)

        gm, gd, gr = jnp.split(jax.nn.sigmoid(gates), 3, axis=-1)
        y = (gm * (hm.astype(x.dtype) @ w_mlstm_out[l])
             + gd * (hd.astype(x.dtype) @ w_diff_out[l])
             + gr * (hr.astype(x.dtype) @ w_ret_out[l]))
        y = y @ w_out[l]
        x = x + rmsnorm(y, g[1])

        h2 = rmsnorm(x, g[2])
        a, u = jnp.split(h2 @ w_ffn_in[l], 2, axis=-1)
        f = (jax.nn.silu(a) * u) @ w_ffn_out[l]
        x = x + rmsnorm(f, g[3])
    return x


def setup_inputs(seed=0):
    out = dict(first_inputs(seed))
    for name, value in second_inputs(seed + 1).items():
        if name != "x":
            out[name + "_2"] = value
    return out


def reference(
    x, mla_w_in, mla_g_q, mla_g_kv, mla_w_uq, mla_w_uk, mla_w_uv, mla_w_o, kv_w_shared, swa_w_q,
    swa_sinks, swa_w_o, rel_bias, mlp_w_up, mlp_w_down, ln_mix_g, ln_mix_b, ln_mlp_g, ln_mlp_b,
    norm_gains_2, w_in_2, mlstm_conv_2, mlstm_gate_bias_2, diff_lambda_2, diff_subln_2,
    w_mlstm_out_2, w_diff_out_2, w_ret_out_2, w_out_2, w_ffn_in_2, w_ffn_out_2,
):
    x = first_block(
        x, mla_w_in, mla_g_q, mla_g_kv, mla_w_uq, mla_w_uk, mla_w_uv, mla_w_o, kv_w_shared,
        swa_w_q, swa_sinks, swa_w_o, rel_bias, mlp_w_up, mlp_w_down, ln_mix_g, ln_mix_b,
        ln_mlp_g, ln_mlp_b,
    )
    return second_block(
        x, norm_gains_2, w_in_2, mlstm_conv_2, mlstm_gate_bias_2, diff_lambda_2, diff_subln_2,
        w_mlstm_out_2, w_diff_out_2, w_ret_out_2, w_out_2, w_ffn_in_2, w_ffn_out_2,
    )


_drawn_inputs = setup_inputs


def setup_inputs(seed=0):
    import zlib

    import numpy as np

    out = dict(_drawn_inputs(seed))
    spreads = {}
    factors = {'mla_g_q': 8.0,
     'mla_g_kv': 8.0,
     'swa_sinks': 8.0,
     'rel_bias': 2.801,
     'diff_lambda_2': 4.661}
    for name, (base, spread) in spreads.items():
        noise = np.random.default_rng([zlib.crc32(name.encode()), seed]).standard_normal(out[name].shape)
        drawn = base * np.exp(spread * noise) if base else spread * noise
        out[name] = __import__('jax').numpy.asarray(drawn.astype(out[name].dtype))
    for name, factor in factors.items():
        out[name] = (out[name] * factor).astype(out[name].dtype)
    return out
```

```python
import numpy as np
from contextlib import ExitStack

P = 128
S = 512
T = S // P
D = 1024
KD = D // P
CH = 2048

MLA_HEADS, NOPE, ROPE, VDIM, QR, KVR = 8, 128, 64, 128, 384, 256
SWA_KV, SWA_DH, WINDOW, BUCKETS = 4, 64, 128, 32
SWA_G = 4
D_FF = 4 * D
FFN = 2816
FT = FFN // P
ALPHA = 4 ** 0.25
LN_EPS, RMS_EPS = 1e-5, 1e-6
MLA_SCALE = (NOPE + ROPE) ** -0.5
BIG = float(2.0 ** 100)
DIFF_SCALE = 64 ** -0.5
LAM_INIT = 0.2

PLAN = [
    ("xt", 0, 0, 0, 8, 0, 0),
    ("in", 4, 2, 2, 5, 1, 0),
    ("pair", 8, 12, 32, 32, 4, 0),
    ("wo0", 4, 2, 0, 8, 2, 0),
    ("mlp0", 32, 8, 32, 8, 8, 16),
    ("kv", 3, 1, 4, 0, 1, 2),
    ("swa", 4, 8, 24, 32, 0, 4),
    ("ot", 0, 0, 0, 8, 0, 0),
    ("wo1", 4, 2, 0, 8, 2, 0),
    ("mlp1", 32, 8, 32, 0, 8, 16),
    ("pre", 0, 0, 0, 8, 0, 0),
    ("if", 1, 0, 2, 2, 0, 1),
    ("ml", 16, 16, 32, 8, 8, 8),
    ("mix0", 8, 4, 0, 0, 4, 0),
    ("ret", 16, 12, 32, 8, 8, 8),
    ("mix1", 8, 4, 0, 0, 4, 0),
    ("dv", 4, 2, 0, 0, 2, 0),
    ("diff", 8, 16, 24, 40, 0, 8),
    ("mix2", 8, 4, 0, 0, 4, 0),
    ("yt", 0, 0, 0, 8, 0, 0),
    ("wout", 4, 2, 0, 8, 2, 0),
    ("ffn", 34, 6, 44, 0, 6, 22),
]
BASE, _at = {}, [0] * 6
for _name, *_n in PLAN:
    BASE[_name] = tuple(_at)
    _at = [a + b for a, b in zip(_at, _n)]
CHUNKS = _at[0]


def constants():
    f = np.float32
    i, j = np.arange(P)[:, None], np.arange(P)[None, :]
    half = ROPE // 2
    inv = (f(10000.0) ** (-np.arange(half, dtype=f) / f(half))).astype(f)
    ang = (np.arange(S, dtype=f)[:, None] * inv[None, :]).astype(f).astype(np.float64)
    freq = np.arange(P) % half
    sign = np.where(np.arange(P) % ROPE < half, -1.0, 1.0)
    jj = np.arange(S)[None, :] - (S - P)
    alibi = -np.abs(i - jj).astype(np.float64)
    alibi = np.where((jj >= 0) & (jj // 64 > i // 64), -BIG, alibi)
    h = np.arange(4, dtype=np.float64)
    log_gamma = np.log(1.0 - 2.0 ** (-5.0 - h))
    rel = np.arange(S)[None, :] - i
    decay = np.where(rel[None] >= 0, np.exp(log_gamma[:, None, None] * np.maximum(rel, 0)[None]), 0.0) / 16.0
    dist = 255 - np.arange(3 * P)
    ok = (dist >= 0) & (dist < WINDOW)
    n = np.clip(dist, 0, None)
    nf = np.maximum(n, 1).astype(f)
    large = 16 + (np.log(nf / f(16)) / f(np.log(8.0)) * f(16)).astype(np.int32)
    bucket = np.where(n < 16, n, np.minimum(large, BUCKETS - 1))
    onehot = (ok[None, :] & (bucket[None, :] == np.arange(BUCKETS)[:, None]))
    return {
        "c_ident": np.eye(P, dtype=f),
        "c_causal": np.where(j > i, -BIG, 0.0).astype(f),
        "c_future": np.where(j < i, BIG, 0.0).astype(f),
        "c_cos": np.cos(ang).T[freq].astype(f),
        "c_sin": (np.sin(ang).T[freq] * sign[:, None]).astype(f),
        "c_alibi": alibi.astype(f),
        "c_slope": np.broadcast_to(2.0 ** -np.arange(1.0, 9.0), (P, 8)).astype(f).copy(),
        "c_decay": np.ascontiguousarray(decay.transpose(1, 0, 2)).astype(f),
        "c_onehot": onehot.astype(f),
        "c_window": np.broadcast_to(np.where(ok, 0.0, -BIG), (16, 3 * P)).astype(f).copy(),
    }


class Tally:

    def __init__(self, sem):
        self.sem, self.base, self.k, self.i, self.per = sem, 0, 0, 0, 0

    def enter(self, i, per):
        self.base, self.k, self.i, self.per = self.base + self.k, 0, i, per

    def leave(self, n):
        assert self.k == self.per, (self.k, self.per)
        self.base, self.k, self.i, self.per = self.base + n * self.per, 0, 0, 0

    def value(self):
        return self.base + self.k + self.i * self.per

    def then(self, engine, instruction):
        self.k += 1
        instruction.then_inc(self.sem, 1)
        engine.wait_ge(self.sem, self.value())


def build(nc, a, out):
    import concourse.bass as bass
    from concourse import mybir

    F32, F32R = mybir.dt.float32, mybir.dt.float32r
    ALU, ACT, AX = mybir.AluOpType, mybir.ActivationFunctionType, mybir.AxisListType
    ds = bass.ds
    ctx = ExitStack()

    def sb(name, shape, dt=F32):
        return ctx.enter_context(nc.sbuf_tensor(name, shape, dt))

    def sem(name):
        return ctx.enter_context(nc.semaphore(name))

    X = sb("X", [P, T, D])
    Y = sb("Y", [P, T, D])
    XH, XL = sb("XH", [P, KD, S], F32R), sb("XL", [P, KD, S], F32R)
    YH, YL = sb("YH", [P, KD, S], F32R), sb("YL", [P, KD, S], F32R)
    RAW = [sb(f"RAW{s}", [P, CH]) for s in range(2)]
    WH = [sb(f"WH{s}", [P, CH], F32R) for s in range(2)]
    WL = [sb(f"WL{s}", [P, CH], F32R) for s in range(2)]
    GB = sb("GB", [P, 2, D])
    ident, identR = sb("ident", [P, P]), sb("identR", [P, P], F32R)
    ones = sb("ones", [P, P])
    causalR, futureR = sb("causalR", [P, P], F32R), sb("futureR", [P, P], F32R)
    cosT, sinT = sb("cosT", [P, S]), sb("sinT", [P, S])
    vec = sb("vec", [P, 160])
    st = sb("st", [P, 256])
    xtmp = sb("xtmp", [P, 2, S])
    ar = sb("ar", [P, 10240])
    slopeR = sb("slopeR", [P, S], F32R)
    scr = nc.dram_tensor("toeplitz", (16, P, 3 * P), F32, kind="Internal").ap()

    A = [ctx.enter_context(nc.psum_tensor(f"A{t}", [P, S], F32)) for t in range(4)]
    B = [ctx.enter_context(nc.psum_tensor(f"B{m}", [P, S], F32)) for m in range(2)]
    C = [ctx.enter_context(nc.psum_tensor(f"C{m}", [P, S], F32)) for m in range(2)]

    def cut(at, *shape):
        n = int(np.prod(shape))
        assert at + n <= 10240
        v = ar[:, at:at + n]
        if len(shape) == 2:
            v = v.rearrange("p (a b) -> p a b", a=shape[0])
        if len(shape) == 3:
            v = v.rearrange("p (a b c) -> p a b c", a=shape[0], b=shape[1])
        return v

    def grid(t, k, n, at=0):
        return t[:, at:at + k * n].rearrange("p (k n) -> p k n", k=k)

    def f32(ap):
        return ap.bitcast(F32)

    def tok(t):
        return slice(t * P, (t + 1) * P)

    def ln_g(n):
        return 16 * n

    def ln_b(n):
        return 16 * n + 8
    NG0, NG2, GQ, GKV, SUBLN, CONV = 64, 72, 80, 83, 85, 88
    GATEB = st[:, 184:186]

    raw_in = [sem(f"raw_in{s}") for s in range(2)]
    raw_more = [sem(f"raw_more{s}") for s in range(2)]
    hi_ready, lo_ready = sem("hi_ready"), sem("lo_ready")
    chunk_done = sem("chunk_done")
    tok_done = sem("tok_done")
    feat_done = sem("feat_done")
    a_free = [sem(f"a_free{t}") for t in range(4)]
    b_free = [sem(f"b_free{m}") for m in range(2)]
    c_free = [sem(f"c_free{m}") for m in range(2)]
    act_step, dve_step, pool_step = sem("act_step"), sem("dve_step"), sem("pool_step")
    x_in, consts_in, rows_in, rows_zero = sem("x_in"), sem("consts_in"), sem("rows_in"), sem("rows_zero")
    consts_done, masks_done = sem("consts_done"), sem("masks_done")
    gb_in = sem("gb_in")
    stage_sems = {}

    def s_(name):
        if name not in stage_sems:
            stage_sems[name] = sem(name)
        return stage_sems[name]

    def slot(c):
        return c % 2

    def c_all_free(pe, n):
        pe.wait_ge(c_free[0], (n + 1) // 2)
        pe.wait_ge(c_free[1], n // 2)

    def wait_tok(e, t, g, c):
        if t < 3:
            e.wait_ge(tok_done, 3 * g + t + 1)
        else:
            e.wait_ge(chunk_done, c + 1)

    def wait_feat(e, m, f, c):
        if m == 0:
            e.wait_ge(feat_done, f + 1)
        else:
            e.wait_ge(chunk_done, c + 1)

    RELB, ONEHOT, WINDOW_T, HEADS_T = (ar[0:32, 4300:4316], ar[0:32, 4320:4704], ar[0:16, 4704:5088], Y[0:16, T - 1, 0:3 * P])
    CAUSAL_T, FUTURE_T, SINK_T, LAMB_T = cut(5500, P), cut(5628, P), cut(5760, 16), cut(5780, 4, 64)
    ROWS_T, LAMP_T = cut(4000, 2, P), cut(6040, 2, 64)
    M_QN, M_KN, M_QR, M_V = cut(0, 2, S), cut(1024, 2, S), cut(2048, S), cut(2560, T, 256)
    M_P, M_PT, M_T, M_KR = cut(3584, 2, 1280), cut(6144, T, S), cut(8192, 2, S), cut(9216, S)
    C_N = cut(0, T, QR + KVR)
    R_T, SQ_T = cut(0, 2, S), cut(1024, 2, S)
    W_K, W_V, W_Q, W_B = cut(0, 4 * S), cut(2048, T, 256), cut(3072, 2, S), cut(4096, 2, 4, 256)
    W_S, W_PT, W_KG = cut(6144, 2, 4, 256), cut(8192, 2, S), cut(9216, S)
    G_I, G_F, G_T, G_L = cut(0, S), cut(512, S), cut(1024, S), cut(1536, S)
    G_B, G_U, G_EM, G_0, G_M = cut(2048, S), cut(2560, S), cut(3072, S), cut(3584, S), cut(9232, S)
    L_Q, L_K, L_V, L_A = cut(0, 2, S), cut(1024, 2, S), cut(2048, T, 258), cut(3080, T, S)
    L_H, L_O, L_M = cut(5128, T, 256), cut(6152, T, 256), cut(7176, S)
    L_PRE, L_ACC, DECAY = cut(7688, 2, 516), cut(8720, S), cut(7176, 4, S)
    F_V, F_Q, F_K, F_A = cut(0, T, D), cut(4096, 2, S), cut(5120, 2, S), cut(6144, 2, S)
    F_P, F_PT, F_H, ALIBI = cut(7168, 2, S), cut(8192, T, S), xtmp[:, 0, :], xtmp[:, 1, :]
    GATE = cut(5128, T, S)
    SQUARES = cut(4096, T, D)
    SILU_T, PROD_T = cut(0, 2, S), cut(1024, 2, S)
    SS, RS, MV, ST6, NMR = 0, 8, 16, 24, 72
    NM, SUM, RINV = 76, 84, 92
    W_MAX, W_NEG, W_SUM, W_ES, W_DEN, W_INV, NEGSINK, LAM = 100, 108, 116, 124, 132, 140, 148, 164
    NEGHALF, EPSILON, PER_DIM = 168, 172, 176
    U_COL, EM_COL, H_DEN, H_INV, H_SS, H_R, SLOPE = 192, 208, 224, 228, 232, 236, 240

    def stat(at, n=1):
        return st[:, at:at + n]

    CONSTS_N, ROWS_N = 12, 14

    block = ctx.enter_context(nc.Block())

    @block.sync
    def _(sp):
        sp.dma_start(X[:], a["x"][0].rearrange("(t p) d -> p t d", p=P)).then_inc(x_in, 16)

        def load(c, s, *pieces):
            if not isinstance(c, int) or c >= 2:
                sp.wait_ge(lo_ready, c - 1)
            for dst, src in pieces[:-1]:
                sp.dma_start(dst, src).then_inc(raw_more[s], 16)
            dst, src = pieces[-1]
            sp.dma_start(dst, src).then_inc(raw_in[s], 16)

        def rows(w):
            return w.rearrange("(k p) n -> p k n", p=P)

        def load_tokens(c0, w, halves=2):
            for h in range(halves):
                for kh in range(2):
                    c = c0 + 2 * h + kh
                    load(c, slot(c), (grid(RAW[slot(c)], 4, 512), rows(w)[:, 4 * kh:4 * kh + 4, 512 * h:512 * h + 512]))

        def load_mlp(c0, up, down):
            with sp.Fori(0, 4) as i:
                for j in range(4):
                    s = slot(c0 + j)
                    load(c0 + j + 8 * i, s, (grid(RAW[s], 8, 256), rows(up)[:, :, ds(i * 1024 + 256 * j, 256)]))
                for j in range(4, 8):
                    h, kh, s = (j - 4) // 2, j % 2, slot(c0 + j)
                    load(c0 + j + 8 * i, s, (grid(RAW[s], 4, 512), rows(down)[:, ds(i * 8 + 4 * kh, 4), 512 * h:512 * h + 512]))

        w_in = rows(a["mla_w_in"][0])
        for kh in range(2):
            load(kh, slot(kh), (grid(RAW[kh], 4, QR), w_in[:, 4 * kh:4 * kh + 4, 0:QR]))
        for kh in range(2):
            g, w, r0 = grid(RAW[kh], 4, 512), w_in[:, 4 * kh:4 * kh + 4, :], QR + KVR
            half = ROPE // 2
            load(2 + kh, slot(2 + kh),
                 (g[:, :, 256:320], w[:, :, r0:r0 + ROPE]), (g[:, :, 320:384], w[:, :, r0:r0 + ROPE]),
                 *[(g[:, :, 384 + half * q:384 + half * q + half],
                    w[:, :, r0 + half * (1 - q % 2):r0 + half * (1 - q % 2) + half]) for q in range(4)],
                 (g[:, :, 0:KVR], w[:, :, QR:QR + KVR]))
        c0 = BASE["pair"][0]
        w_uv = a["mla_w_uv"][0].rearrange("(k p) h v -> p k (h v)", p=P)
        w_uk = a["mla_w_uk"][0].rearrange("(k p) h v -> p k (h v)", p=P)
        w_uq = a["mla_w_uq"][0].rearrange("(k p) h v -> p k (h v)", p=P)
        with sp.Fori(0, 4) as i:
            s = slot(c0)
            load(c0 + 2 * i, s, (grid(RAW[s], 2, 256), w_uv[:, :, ds(i * 256, 256)]))
            s = slot(c0 + 1)
            g, hw, half = grid(RAW[s], 3, 512), NOPE + ROPE, ROPE // 2
            load(c0 + 1 + 2 * i, s,
                 *[(g[:, :, 128 * h:128 * h + 128], w_uq[:, :, ds(i * (2 * hw) + hw * h, NOPE)]) for h in range(2)],
                 *[(g[:, :, 256 + 64 * h:256 + 64 * h + 64], w_uq[:, :, ds(i * (2 * hw) + hw * h + NOPE, ROPE)]) for h in range(2)],
                 *[(g[:, :, 384 + 64 * h + half * q:384 + 64 * h + half * q + half],
                    w_uq[:, :, ds(i * (2 * hw) + hw * h + NOPE + half * (1 - q), half)]) for h in range(2) for q in range(2)],
                 (grid(RAW[s], 2, 256, 1536), w_uk[:, :, ds(i * 256, 256)]))
        load_tokens(BASE["wo0"][0], a["mla_w_o"][0])
        load_mlp(BASE["mlp0"][0], a["mlp_w_up"][0], a["mlp_w_down"][0])
        c0, w_kv = BASE["kv"][0], rows(a["kv_w_shared"])
        s = slot(c0)
        load(c0, s, (grid(RAW[s], 8, 256), w_kv[:, :, 0:256]))
        s = slot(c0 + 1)
        g = grid(RAW[s], 8, 256)
        load(c0 + 1, s, *[(g[:, :, 128 * j + 64 * e:128 * j + 64 * e + 64],
                           w_kv[:, :, 128 * j + 64 * (1 - e):128 * j + 64 * (1 - e) + 64]) for j in range(2) for e in range(2)])
        s = slot(c0 + 2)
        load(c0 + 2, s, (grid(RAW[s], 8, 256), w_kv[:, :, 256:512]))
        c0 = BASE["swa"][0]
        with sp.Fori(0, 2) as i:
            for u in range(2):
                s = slot(c0 + u)
                load(c0 + u + 2 * i, s, (grid(RAW[s], 8, 256), rows(a["swa_w_q"][0])[:, :, ds(i * 512 + 256 * u, 256)]))
        load_tokens(BASE["wo1"][0], a["swa_w_o"][0])
        load_mlp(BASE["mlp1"][0], a["mlp_w_up"][1], a["mlp_w_down"][1])
        w = rows(a["w_in_2"][0])
        OFF = dict(mq=0, mk=D, mv=2 * D, mo=3 * D, gate_if=4 * D, dq=4 * D + 8, dk=5 * D + 8, dv=6 * D + 8,
                   rq=7 * D + 8, rk=8 * D + 8, rv=9 * D + 8, rg=10 * D + 8, gates=11 * D + 8)
        c0 = BASE["if"][0]
        load(c0, slot(c0), (grid(RAW[slot(c0)], 8, 256), w[:, :, OFF["gate_if"]:OFF["gate_if"] + 256]))

        def load_heads(c0, names):
            with sp.Fori(0, 4) as i:
                for j, name in enumerate(names):
                    s = slot(c0 + j)
                    load(c0 + j + 4 * i, s, (grid(RAW[s], 8, 256), w[:, :, ds(i * 256 + OFF[name], 256)]))

        def load_mix(c0, n, w_o):
            for h in range(2):
                for kh in range(2):
                    c = c0 + 4 * h + kh
                    at = OFF["gates"] + n * D + 512 * h
                    load(c, slot(c), (grid(RAW[slot(c)], 4, 512), w[:, 4 * kh:4 * kh + 4, at:at + 512]))
                for kh in range(2):
                    c = c0 + 4 * h + 2 + kh
                    load(c, slot(c), (grid(RAW[slot(c)], 4, 512), rows(w_o)[:, 4 * kh:4 * kh + 4, 512 * h:512 * h + 512]))

        load_heads(BASE["ml"][0], ("mq", "mk", "mv", "mo"))
        load_mix(BASE["mix0"][0], 0, a["w_mlstm_out_2"][0])
        load_heads(BASE["ret"][0], ("rq", "rk", "rv", "rg"))
        load_mix(BASE["mix1"][0], 2, a["w_ret_out_2"][0])
        load_tokens(BASE["dv"][0], a["w_in_2"][0][:, OFF["dv"]:OFF["dv"] + D])
        c0 = BASE["diff"][0]
        with sp.Fori(0, 4) as i:
            for u, name in enumerate(("dq", "dk")):
                s = slot(c0 + u)
                load(c0 + u + 2 * i, s, (grid(RAW[s], 8, 256), w[:, :, ds(i * 256 + OFF[name], 256)]))
        load_mix(BASE["mix2"][0], 1, a["w_diff_out_2"][0])
        load_tokens(BASE["wout"][0], a["w_out_2"][0])
        c0, w_up, w_down = BASE["ffn"][0], rows(a["w_ffn_in_2"][0]), rows(a["w_ffn_out_2"][0])

        def load_down(c0, k0, nk):
            for h in range(2):
                for kh in range(2):
                    c, n = c0 + 2 * h + kh, min(4, nk - 4 * kh)
                    load(c, slot(c), (grid(RAW[slot(c)], n, 512), w_down[:, k0 + 4 * kh:k0 + 4 * kh + n, 512 * h:512 * h + 512]))

        for n, tiles in enumerate((8, 8, 6)):
            c = c0 + 12 * n
            with sp.Fori(0, tiles // 2) as i:
                for u in range(2):
                    load(c + u + 2 * i, slot(c + u),
                         (grid(RAW[slot(c + u)], 8, 256), w_up[:, :, ds(i * 256 + (8 * n * P + FFN * u), 256)]))
            load_down(c + tiles, 8 * n, tiles)
        for t in range(T):
            sp.wait_ge(s_("fin_x"), t + 1)
            sp.dma_start(out[0, tok(t), :], X[:, t, :]).then_inc(s_("stored"), 16)
        sp.wait_ge(s_("stored"), 16 * T)

    @block.tensor
    def _(pe):
        def mm(dst, l, r, first, last):
            return nc.tensor.matmul(dst, l, r, start=first, stop=last)

        def mm3(dst, lh, ll, rh, rl, first, last):
            mm(dst, lh, rh, first, False)
            mm(dst, lh, rl, False, False)
            return mm(dst, ll, rh, False, last)

        def tokens(c, s, xh, xl, k0, nk, n, rnd, first=True, last=True, done=None):
            pe.wait_ge(lo_ready, c + 1)
            wh, wl = grid(WH[s], nk, n), grid(WL[s], nk, n)
            for t in range(T):
                if first and rnd is not None:
                    pe.wait_ge(a_free[t], rnd)
                for j in range(nk):
                    k = k0 + j
                    m = mm3(A[t][:, 0:n], xh[:, k, tok(t)], xl[:, k, tok(t)], wh[:, j, :], wl[:, j, :],
                            first and j == 0, last and j == nk - 1)
                if t == T - 1:
                    m.then_inc(chunk_done, 1)
                elif last:
                    m.then_inc(tok_done, 1)

        def tokens_full(c0, r0, xh, xl):
            for h in range(2):
                for kh in range(2):
                    c = c0 + 2 * h + kh
                    tokens(c, slot(c), xh, xl, 4 * kh, 4, 512, r0 + h, kh == 0, kh == 1)

        def features(c, s, xh, xl, use):
            pe.wait_ge(lo_ready, c + 1)
            wh, wl = grid(WH[s], KD, 256), grid(WL[s], KD, 256)
            for m in range(2):
                pe.wait_ge(b_free[m], use)
                for k in range(KD):
                    r = mm3(B[m][:], wh[:, k, tok(m)], wl[:, k, tok(m)], xh[:, k, :], xl[:, k, :], k == 0, k == KD - 1)
                r.then_inc(feat_done if m == 0 else chunk_done, 1)

        def transposed(name, n0, src):
            for k in range(KD):
                b = (n0 + k) % 2
                if n0 + k >= 2:
                    pe.wait_ge(c_free[b], (n0 + k) // 2)
                for t in range(T):
                    r = nc.tensor.transpose(C[b][:, tok(t)], src[:, t, tok(k)], ident[:])
                r.then_inc(s_(name + "_t"), 1)

        pe.wait_ge(rows_in, ROWS_N * 16)
        pe.wait_ge(consts_in, CONSTS_N * 16)
        for m in range(2):
            nc.tensor.transpose(A[m][:, 0:P], ROWS_T[:, m, :], ident[:])
        mm(A[2][0:16, 0:3 * P], RELB, ONEHOT, True, True).then_inc(s_("vec_t"), 1)
        pe.wait_ge(consts_done, 1)
        pe.wait_ge(masks_done, 1)
        pe.wait_ge(x_in, 16)
        transposed("xt", BASE["xt"][3], X)
        c_all_free(pe, BASE["in"][3])
        for kh in range(2):
            tokens(kh, slot(kh), XH, XL, 4 * kh, 4, QR, None, kh == 0, kh == 1)
        for kh in range(2):
            c, s = 2 + kh, slot(2 + kh)
            pe.wait_ge(lo_ready, c + 1)
            wh, wl = grid(WH[s], 4, 512), grid(WL[s], 4, 512)
            for t in range(T):
                if kh == 0:
                    pe.wait_ge(a_free[t], 1)
                for j in range(4):
                    k = 4 * kh + j
                    r = mm3(A[t][:, 0:KVR], XH[:, k, tok(t)], XL[:, k, tok(t)], wh[:, j, 0:KVR], wl[:, j, 0:KVR],
                            k == 0, k == 7)
                if kh == 1:
                    r.then_inc(s_("in_kv"), 1)
            for m in range(2):
                for j in range(4):
                    k, cols = 4 * kh + j, slice(256 + P * m, 384 + P * m)
                    r = mm3(B[m][:], wh[:, j, cols], wl[:, j, cols], XH[:, k, :], XL[:, k, :], k == 0, k == 7)
                if m == 1:
                    r.then_inc(chunk_done, 1)
                elif kh == 1:
                    r.then_inc(s_("in_kv"), 1)
        n0, cn = BASE["in"][3], cut(0, T, QR + KVR)
        for k in range(5):
            b = (n0 + k) % 2
            pe.wait_ge(c_free[b], (n0 + k) // 2)
            for t in range(T):
                pe.wait_ge(a_free[t], 1 if k < 3 else 2)
                r = nc.tensor.transpose(C[b][:, tok(t)], cn[:, t, tok(k)], ident[:])
            r.then_inc(s_("in_t"), 1)
        c_all_free(pe, n0 + 5)
        c0, ra, rb, n0, _, _ = BASE["pair"]
        pe.wait_ge(s_("kr_ready"), 1)
        with pe.Fori(0, 4) as i:
            c = c0 + 2 * i
            tokens(c, slot(c0), YH, YL, 3, 2, 256, ra + 3 * i)
            s = slot(c0 + 1)
            pe.wait_ge(lo_ready, c + 2)
            qh, ql = grid(WH[s], 3, 512), grid(WL[s], 3, 512)
            kh, kl = grid(WH[s], 2, 256, 1536), grid(WL[s], 2, 256, 1536)
            for u, (wh, wl, at, x0, nk) in enumerate((
                    (qh, ql, 0, 0, 3), (qh, ql, 128, 0, 3), (kh, kl, 0, 3, 2), (kh, kl, 128, 3, 2),
                    (qh, ql, 256, 0, 3), (qh, ql, 384, 0, 3))):
                b = u % 2
                pe.wait_ge(b_free[b], (rb + u) // 2 + 4 * i)
                for k in range(nk):
                    r = mm3(B[b][:], wh[:, k, at:at + P], wl[:, k, at:at + P], YH[:, x0 + k, :], YL[:, x0 + k, :], k == 0, k == nk - 1)
                r.then_inc(chunk_done if u == 5 else s_("pair_f"), 1)
            for b in range(2):
                pe.wait_ge(b_free[b], rb // 2 + 4 * i + 3)
            pe.wait_ge(s_("qr_ready"), i + 1)
            for h in range(2):
                for q in range(T):
                    n, rows = (q + 1) * P, slice(64 * h, 64 * h + 64)
                    pe.wait_ge(a_free[q], ra + 3 * i + 1 + h)
                    mm(A[q][:, 0:n], M_QN[:, h, tok(q)], M_KN[:, h, 0:n], True, False)
                    mm(A[q][:, n - P:n], identR[:], causalR[:], False, False)
                    mm(A[q][:, 0:n], M_QR[rows, tok(q)], M_KR[rows, 0:n], False, True).then_inc(s_("pair_s"), 1)
            for h in range(2):
                for q in range(T):
                    u = n0 + 4 * h + q
                    pe.wait_ge(c_free[u % 2], u // 2 + 4 * i)
                    pe.wait_ge(s_("pair_p"), 8 * i + 4 * h + q + 1)
                    for k in range(q + 1):
                        at = q * (q + 1) // 2 * P + k * P
                        r = nc.tensor.transpose(C[u % 2][:, tok(k)], M_P[:, h, at:at + P], ident[:])
                    r.then_inc(s_("pair_t"), 1)
                for b in range(2):
                    pe.wait_ge(c_free[b], (n0 + 4 * h + 4 + 1 - b) // 2 + 4 * i)
                pe.wait_ge(b_free[h], rb // 2 + 4 * i + 3)
                for k in range(T):
                    r = mm(B[h][:, k * P:S], M_V[:, k, tok(h)], M_PT[:, k, k * P:S], k == 0, k == T - 1)
                r.then_inc(s_("pair_o"), 1)

        def b_all_free(n):
            pe.wait_ge(b_free[0], (n + 1) // 2)
            pe.wait_ge(b_free[1], n // 2)

        b_all_free(BASE["mlp0"][2])
        tokens_full(BASE["wo0"][0], BASE["wo0"][1], XH, XL)

        def norm_transposed(name, n0):
            pe.wait_ge(s_(name + "_n"), T)
            transposed(name, n0, Y)
            c_all_free(pe, n0 + KD)

        norm_transposed("ln0", BASE["wo0"][3])

        def mlp(name):
            c0, ra, rb, _, _, _ = BASE[name]
            with pe.Fori(0, 4) as i:
                c = c0 + 8 * i
                for j in range(4):
                    features(c + j, slot(c0 + j), XH, XL, rb // 2 + 4 * i + j)
                for h in range(2):
                    for kh in range(2):
                        j = 4 + 2 * h + kh
                        pe.wait_ge(s_(name + "_y"), 8 * i + 4 * kh + 4)
                        tokens(c + j, slot(c0 + j), YH, YL, 4 * kh, 4, 512, ra + 2 * i + h, kh == 0, kh == 1)

        mlp("mlp0")
        norm_transposed("ln1", BASE["mlp0"][3])
        c0, ra, rb, _, _, _ = BASE["kv"]
        for u in range(2):
            features(c0 + u, slot(c0 + u), XH, XL, rb // 2 + u)
        tokens(c0 + 2, slot(c0 + 2), XH, XL, 0, 8, 256, ra)
        c0, ra, rb, n0, _, _ = BASE["swa"]
        for t in range(T):
            pe.wait_ge(a_free[t], BASE["kv"][1] + 1)
        with pe.Fori(0, 2) as i:
            for u in range(2):
                features(c0 + u + 2 * i, slot(c0 + u), XH, XL, rb // 2 + 3 * u + 6 * i)
                for b in range(2):
                    pe.wait_ge(b_free[b], rb // 2 + 3 * u + 1 + 6 * i)
                pe.wait_ge(s_("swa_k"), 2 * i + u + 1)
                for n in range(T):
                    w = P if n == 0 else 2 * P
                    bank = 2 * (n % 2)
                    for e in range(2):
                        pe.wait_ge(a_free[bank + e], ra + 2 * u + n // 2 + 4 * i)
                    for q in range(2):
                        for e in range(2):
                            rows = slice(64 * e, 64 * e + 64)
                            k_at = (n - 1) * P if n else 0
                            keys = W_KG[rows, k_at:k_at + w]
                            r = mm(A[bank + e][:, 256 * q:256 * q + w], W_Q[rows, q, tok(n)], keys, True, True)
                            if q == 1:
                                r.then_inc(s_("swa_s"), 1)
                    pe.wait_ge(s_("swa_p"), 4 * (u + 2 * i) + n + 1)
                    for kb in range(2):
                        x = n0 + 8 * u + 2 * n + kb
                        pe.wait_ge(c_free[x % 2], x // 2 + 8 * i)
                        todo = [(h, kb) for h in range(4)] if n else [(2 * kb, 0), (2 * kb + 1, 0)]
                        for z, (h, blk) in enumerate(todo):
                            r = nc.tensor.transpose(C[x % 2][:, tok(z)], W_S[:, n % 2, h, blk * P:blk * P + P], ident[:])
                        r.then_inc(s_("swa_t"), 1)
                    for kb in range(2):
                        x = n0 + 8 * u + 2 * n + kb
                        pe.wait_ge(c_free[x % 2], x // 2 + 1 + 8 * i)
                    pe.wait_ge(b_free[n % 2], rb // 2 + 3 * u + 1 + n // 2 + 6 * i)
                    blocks = (0, 1) if n else (1,)
                    for h in range(4):
                        for kb in blocks:
                            r = mm(B[n % 2][:, 64 * h:64 * h + 64], W_PT[:, kb, tok(h)],
                                   W_V[:, n - 1 + kb, ds(i * 128 + 64 * u, 64)], kb == blocks[0], kb == 1)
                    r.then_inc(s_("swa_o"), 1)
        b_all_free(BASE["mlp1"][2])
        transposed("ot", BASE["ot"][3], Y)
        c_all_free(pe, BASE["wo1"][3])
        tokens_full(BASE["wo1"][0], BASE["wo1"][1], YH, YL)
        norm_transposed("ln2", BASE["wo1"][3])
        mlp("mlp1")
        norm_transposed("pre", BASE["pre"][3])
        c0, _, rb, n0, _, _ = BASE["if"]
        s = slot(c0)
        pe.wait_ge(lo_ready, c0 + 1)
        wh, wl = grid(WH[s], KD, 256), grid(WL[s], KD, 256)
        for m in range(2):
            pe.wait_ge(b_free[m], rb // 2)
            for k in range(KD):
                cols = slice(4 * m, 4 * m + P)
                r = mm3(B[m][:], wh[:, k, cols], wl[:, k, cols], XH[:, k, :], XL[:, k, :], k == 0, k == KD - 1)
            r.then_inc(feat_done if m == 0 else chunk_done, 1)
        for m, src in enumerate((G_U, G_EM)):
            b = (n0 + m) % 2
            pe.wait_ge(c_free[b], (n0 + m) // 2)
            pe.wait_ge(s_("if_g"), 1)
            for t in range(T):
                r = nc.tensor.transpose(C[b][:, tok(t)], src[:, tok(t)], ident[:])
            r.then_inc(s_("if_t"), 1)
        c_all_free(pe, n0 + 2)

        def head_transposed(name, i, n0, src):
            pe.wait_ge(s_(name + "_h"), T * i + T)
            for m in range(2):
                b = (n0 + m) % 2
                pe.wait_ge(c_free[b], (n0 + m) // 2 + i)
                for t in range(T):
                    r = nc.tensor.transpose(C[b][:, tok(t)], src[:, t, tok(m)], ident[:])
                r.then_inc(s_(name + "_t"), 1)

        def decayed_values(name, i, rounds, rb, at, v, width):
            for t in range(T):
                pe.wait_ge(a_free[t], rounds)
                b, u = t % 2, rb + 4 + t
                pe.wait_ge(b_free[b], u // 2 + 4 * i)
                for j in range(t + 1):
                    r = mm(B[b][:, 0:width], at[:, j, (t - j) * P:(t - j) * P + P], v[:, j, 0:width], j == 0, j == t)
                r.then_inc(s_(name + "_o"), 1)

        def scores(name, i, r, q, k):
            for j in range(T):
                n = S - j * P
                pe.wait_ge(a_free[j], r)
                for m in range(2):
                    x = mm(A[j][:, 0:n], k[:, m, tok(j)], q[:, m, j * P:S], m == 0, m == 1)
                x.then_inc(s_(name + "_s"), 1)

        c0, ra, rb, n0, _, _ = BASE["ml"]
        with pe.Fori(0, 4) as i:
            c = c0 + 4 * i
            for j in range(2):
                features(c + j, slot(c0 + j), XH, XL, rb // 2 + 4 * i + j)
            for j in range(2):
                tokens(c + 2 + j, slot(c0 + 2 + j), XH, XL, 0, KD, 256, ra + 4 * i + j)
            pe.wait_ge(s_("ml_m"), i + 1)
            for j in range(T):
                n = S - j * P
                pe.wait_ge(a_free[j], ra + 4 * i + 2)
                if n > P:
                    mm(A[j][:, P:n], ones[:], L_M[:, (j + 1) * P:S], True, True)
                mm(A[j][:, 0:P], ones[:], L_M[:, tok(j)], True, False)
                mm(A[j][:, 0:P], identR[:], futureR[:], False, True).then_inc(s_("ml_w"), 1)
            pe.wait_ge(s_("ml_qk"), 4 * i + 4)
            scores("ml", i, ra + 4 * i + 3, L_Q, L_K)
            decayed_values("ml", i, ra + 4 * i + 4, rb, L_A, L_V, 257)
            head_transposed("ml", i, n0, L_H)

        def mix(name):
            c0, ra, _, n0, _, _ = BASE[name]
            c_all_free(pe, n0)
            for h in range(2):
                for kh in range(2):
                    c = c0 + 4 * h + kh
                    tokens(c, slot(c), XH, XL, 4 * kh, 4, 512, ra + 2 * h, kh == 0, kh == 1)
                for kh in range(2):
                    c = c0 + 4 * h + 2 + kh
                    tokens(c, slot(c), YH, YL, 4 * kh, 4, 512, ra + 2 * h + 1, kh == 0, kh == 1)

        mix("mix0")
        c0, ra, rb, n0, _, _ = BASE["ret"]
        with pe.Fori(0, 4) as i:
            c = c0 + 4 * i
            for j in range(2):
                features(c + j, slot(c0 + j), XH, XL, rb // 2 + 4 * i + j)
            for j in range(2):
                tokens(c + 2 + j, slot(c0 + 2 + j), XH, XL, 0, KD, 256, ra + 3 * i + j)
            for b in range(2):
                pe.wait_ge(b_free[b], rb // 2 + 4 * i + 2)
            scores("ret", i, ra + 3 * i + 2, L_Q, L_K)
            decayed_values("ret", i, ra + 3 * i + 3, rb, L_A, L_V, 256)
            head_transposed("ret", i, n0, L_H)
        mix("mix1")
        tokens_full(BASE["dv"][0], BASE["dv"][1], XH, XL)
        c0, ra, rb, n0, _, _ = BASE["diff"]
        for t in range(T):
            pe.wait_ge(a_free[t], BASE["dv"][1] + 2)
        with pe.Fori(0, 4) as i:
            for j in range(2):
                features(c0 + j + 2 * i, slot(c0 + j), XH, XL, rb // 2 + 3 * i + j)
            for b in range(2):
                pe.wait_ge(b_free[b], rb // 2 + 3 * i + 2)
            for h in range(2):
                pe.wait_ge(s_("diff_b"), 2 * i + h + 1)
                for q in range(T):
                    n = (q + 1) * P
                    for e in range(2):
                        u, rows = 2 * q + e, slice(64 * e, 64 * e + 64)
                        pe.wait_ge(a_free[u % 4], ra + 2 * h + u // 4 + 4 * i)
                        mm(A[u % 4][:, 0:n], identR[:], slopeR[:, S - n:S], True, False)
                        mm(A[u % 4][:, 0:n], F_Q[rows, h, tok(q)], F_K[rows, h, 0:n], False, True).then_inc(s_("diff_s"), 1)
                for q in range(T):
                    u = n0 + 5 * h + q
                    pe.wait_ge(c_free[u % 2], u // 2 + 5 * i)
                    pe.wait_ge(s_("diff_p"), 8 * i + 4 * h + q + 1)
                    for k in range(q + 1):
                        r = nc.tensor.transpose(C[u % 2][:, tok(k)], F_A[:, q % 2, tok(k)], ident[:])
                    r.then_inc(s_("diff_t"), 1)
                for b in range(2):
                    pe.wait_ge(c_free[b], (n0 + 5 * h + 4 + 1 - b) // 2 + 5 * i)
                u = rb + 4 + h
                pe.wait_ge(b_free[u % 2], u // 2 + 3 * i)
                for q in range(T):
                    for k in range(q + 1):
                        r = mm(B[u % 2][:, tok(q)], F_PT[:, k, tok(q)], F_V[:, k, ds(i * 256 + P * h, P)], k == 0, k == q)
                r.then_inc(s_("diff_o"), 1)
                u = n0 + 5 * h + 4
                pe.wait_ge(b_free[h], (rb + 4 + h) // 2 + 1 + 3 * i)
                pe.wait_ge(c_free[u % 2], u // 2 + 5 * i)
                for t in range(T):
                    r = nc.tensor.transpose(C[u % 2][:, tok(t)], F_H[:, tok(t)], ident[:])
                r.then_inc(s_("diff_ht"), 1)
        mix("mix2")
        pe.wait_ge(s_("mixed"), 16)
        transposed("yt", BASE["yt"][3], Y)
        c_all_free(pe, BASE["wout"][3])
        tokens_full(BASE["wout"][0], BASE["wout"][1], XH, XL)
        norm_transposed("post", BASE["wout"][3])
        c, ra, rb, _, _, _ = BASE["ffn"]
        use, done = rb // 2, 0
        for n, tiles in enumerate((8, 8, 6)):
            with pe.Fori(0, tiles // 2) as i:
                for j in range(2):
                    features(c + j + 2 * i, slot(c + j), XH, XL, use + j + 2 * i)
            c, use, done = c + tiles, use + tiles, done + tiles
            for h in range(2):
                for kh in range(2):
                    nk = min(4, tiles - 4 * kh)
                    pe.wait_ge(s_("ffn_y"), done - tiles + 4 * kh + nk)
                    tokens(c, slot(c), YH, YL, 4 * kh, nk, 512, ra + 2 * n + h, kh == 0, kh == 1)
                    c += 1

    @block.scalar
    def _(act):
        def split(c, per=0, i=0, more=None):
            if c >= CHUNKS:
                return
            s = slot(c)
            act.wait_ge(raw_in[s], 16 * (c // 2 + 1) + i * (16 * (per // 2)))
            if more is not None:
                act.wait_ge(raw_more[s], more)
            if c >= 2:
                act.wait_ge(chunk_done, c - 1 + i * per)
            n = 4 * QR if c < 2 else CH
            nc.scalar.activation(WH[s][:, 0:n], RAW[s][:, 0:n], ACT.Copy).then_inc(hi_ready, 1)

        def copy(dst, src, scale=1.0):
            return nc.scalar.activation(dst, src, ACT.Copy, scale=scale)

        def hi_transposed(name, n0, dst, g=None, b=None):
            for k in range(KD):
                act.wait_ge(s_(name + "_t"), k + 1)
                src = C[(n0 + k) % 2][:]
                if g is None:
                    x = copy(dst[:, k, :], src)
                else:
                    x = nc.scalar.activation(dst[:, k, :], src, ACT.Identity, scale=vec[:, g + k:g + k + 1],
                                             bias=0.0 if b is None else vec[:, b + k:b + k + 1])
                x.then_inc(s_(name + "_hi"), 1)

        act.wait_ge(consts_in, CONSTS_N * 16)
        copy(identR[:], ident[:]).then_inc(masks_done, 1)
        act.wait_ge(s_("lam_dot"), 1)
        nc.scalar.activation(stat(LAM, 2), stat(LAM, 2), ACT.Exp).then_inc(s_("lam_exp"), 1)
        split(0)
        hi_transposed("xt", BASE["xt"][3], XH)
        split(1)
        split(2, more=16 * 6)

        def latents(n, wait, at, width):
            for t in range(T):
                wait(t)
                nc.scalar.activation(C_N[:, t, at:at + width], A[t][:, 0:width], ACT.Square,
                                     accum_out=stat(SS + 4 * n + t)).then_inc(s_("in_ss"), 1)
            for t in range(T):
                act.wait_ge(s_("in_r"), 4 * n + t + 1)
                nc.scalar.activation(C_N[:, t, at:at + width], A[t][:, 0:width], ACT.Copy,
                                     scale=stat(RS + 4 * n + t)).then_inc(a_free[t], 1)

        latents(0, lambda t: wait_tok(act, t, 0, 1), 0, QR)
        split(3, more=16 * 6)
        split(4)
        latents(1, lambda t: act.wait_ge(s_("in_kv"), t + 1), QR, KVR)
        for k in range(5):
            act.wait_ge(s_("in_t"), k + 1)
            g = (GQ + k) if k < 3 else (GKV + k - 3)
            nc.scalar.activation(YH[:, k, :], C[(BASE["in"][3] + k) % 2][:], ACT.Copy,
                                 scale=vec[:, g:g + 1]).then_inc(s_("in_hi"), 1)
        c0, ra, rb, n0, g0, _ = BASE["pair"]
        with act.Fori(0, 4) as i:
            split(c0 + 1, 2, i, more=16 * 6 + 128 + i * 128)
            for t in range(T):
                if t < 3:
                    act.wait_ge(tok_done, 3 * g0 + t + 1 + i * 3)
                else:
                    act.wait_ge(chunk_done, c0 + 1 + i * 2)
                copy(M_V[:, t, :], A[t][:, 0:256]).then_inc(a_free[t], 1)
            split(c0 + 2, 2, i)
            act.wait_ge(s_("pair_f"), 5 * i + 1)
            copy(M_QN[:, 0, :], B[0][:]).then_inc(b_free[0], 1)
            act.wait_ge(s_("pair_f"), 5 * i + 3)
            copy(M_KN[:, 0, :], B[0][:], MLA_SCALE).then_inc(b_free[0], 1)
            for h in range(2):
                for q in range(T):
                    n, at = (q + 1) * P, q * (q + 1) // 2 * P
                    act.wait_ge(s_("pair_m"), 8 * i + 4 * h + q + 1)
                    nc.scalar.activation(M_P[:, h, at:at + n], A[q][:, 0:n], ACT.Exp, bias=stat(NM + 4 * h + q),
                                         accum_out=stat(SUM + 4 * h + q)).then_inc(a_free[q], 1)
            for h in range(2):
                for q in range(T):
                    u = (n0 + 4 * h + q) % 2
                    act.wait_ge(s_("pair_t"), 8 * i + 4 * h + q + 1)
                    copy(M_PT[:, 0:q + 1, tok(q)], C[u][:, 0:(q + 1) * P].rearrange("p (k n) -> p k n", n=P)).then_inc(c_free[u], 1)
                act.wait_ge(s_("pair_o"), 2 * i + h + 1)
                copy(XH[:, ds(i * 2 + h, 1), :].rearrange("p a n -> p (a n)"), B[h][:]).then_inc(s_("pair_hi"), 1)

        def splits(c0, n):
            for c in range(c0, c0 + n):
                split(c + 1)

        def normalize(name):
            for t in range(T):
                act.wait_ge(s_(name + "_r"), t + 1)
                nc.scalar.activation(Y[:, t, :], Y[:, t, :], ACT.Identity, scale=stat(RS + t),
                                     bias=stat(NMR + t)).then_inc(s_(name + "_n"), 1)

        splits(BASE["wo0"][0], 4)
        normalize("ln0")
        hi_transposed("ln0", BASE["wo0"][3], XH, ln_g(0), ln_b(0))

        def mlp(name):
            c0, _, _, _, _, f0 = BASE[name]
            with act.Fori(0, 4) as i:
                for j in range(4):
                    split(c0 + j + 1, 8, i)
                    for m in range(2):
                        if m == 0:
                            act.wait_ge(feat_done, f0 + j + 1 + i * 4)
                        else:
                            act.wait_ge(chunk_done, c0 + j + 1 + i * 8)
                        nc.scalar.activation(R_T[:, m, :], B[m][:], ACT.Relu).then_inc(b_free[m], 1)
                        act.wait_ge(s_(name + "_sq"), 8 * i + 2 * j + m + 1)
                        copy(YH[:, 2 * j + m, :], SQ_T[:, m, :]).then_inc(s_(name + "_hi"), 1)
                for j in range(4, 8):
                    split(c0 + j + 1, 8, i)

        mlp("mlp0")
        normalize("ln1")
        hi_transposed("ln1", BASE["mlp0"][3], XH, ln_g(1), ln_b(1))
        c0, _, _, _, g0, f0 = BASE["kv"]
        for u in range(2):
            split(c0 + u + 1, more=16 * 6 + 512 + 48 if u == 0 else None)
            wait_feat(act, 0, f0 + u, c0 + u)
            copy(W_K[:, 2 * S * u:2 * S * u + S], B[0][:]).then_inc(b_free[0], 1)
        split(c0 + 3)
        for t in range(T):
            wait_tok(act, t, g0, c0 + 2)
            copy(W_V[:, t, :], A[t][:, 0:256]).then_inc(a_free[t], 1)
        c0, ra, rb, n0, _, f0 = BASE["swa"]
        with act.Fori(0, 2) as i:
            for u in range(2):
                split(c0 + u + 1, 2, i)
                act.wait_ge(feat_done, f0 + u + 1 + i * 2)
                copy(W_Q[:, 0, :], B[0][:], SWA_DH ** -0.5).then_inc(b_free[0], 1)
                for n in range(T):
                    w, z = (P if n == 0 else 2 * P), n % 2
                    act.wait_ge(s_("swa_m"), 4 * (2 * i + u) + n + 1)
                    for h in range(4):
                        nc.scalar.activation(W_S[:, z, h, 0:w], W_S[:, z, h, 0:w], ACT.Exp, bias=stat(W_NEG + 4 * z + h),
                                             accum_out=stat(W_SUM + 4 * z + h))
                    nc.scalar.activation(stat(W_ES + 4 * z, 4), stat(W_ES + 4 * z, 4), ACT.Exp).then_inc(s_("swa_p"), 1)
                    x = n0 + 8 * u + 2 * n
                    act.wait_ge(s_("swa_t"), 8 * (2 * i + u) + 2 * n + 1)
                    dst = W_PT[:, 0, :] if n else W_PT[:, 1, 0:256]
                    copy(dst, C[x % 2][:, 0:512 if n else 256]).then_inc(c_free[x % 2], 1)
        hi_transposed("ot", BASE["ot"][3], YH)
        splits(BASE["wo1"][0], 4)
        normalize("ln2")
        hi_transposed("ln2", BASE["wo1"][3], XH, ln_g(2), ln_b(2))
        mlp("mlp1")
        normalize("ln3")

        def scale_norm(name):
            for t in range(T):
                act.wait_ge(s_(name + "_x"), t + 1)
                nc.scalar.activation(Y[:, t, :], X[:, t, :], ACT.Square, accum_out=stat(SS + t)).then_inc(s_(name + "_ss"), 1)
            for t in range(T):
                act.wait_ge(s_(name + "_r"), t + 1)
                copy(Y[:, t, :], X[:, t, :], stat(RS + t)).then_inc(s_(name + "_n"), 1)

        scale_norm("pre")
        hi_transposed("pre", BASE["pre"][3], XH, NG0)
        split(BASE["if"][0] + 1)
        act.wait_ge(s_("if_abs"), 1)
        nc.scalar.activation(G_L, G_T, ACT.Exp, scale=-1.0).then_inc(s_("if_e"), 1)
        act.wait_ge(s_("if_e"), 1)
        nc.scalar.activation(G_L, G_L, ACT.Ln, bias=1.0).then_inc(s_("if_l"), 1)
        act.wait_ge(s_("if_m"), 1)
        nc.scalar.activation(G_EM, G_EM, ACT.Exp, scale=-1.0).then_inc(s_("if_g"), 1)
        c0, ra, rb, n0, g0, f0 = BASE["ml"]

        def head_rms(name, i, inv):
            for t in range(T):
                if inv:
                    act.wait_ge(s_(name + "_d"), T * i + t + 1)
                    nc.scalar.activation(L_H[:, t, :], B[t % 2][:, 0:256], ACT.Copy, scale=stat(H_INV + t)).then_inc(b_free[t % 2], 1)
                else:
                    act.wait_ge(s_(name + "_o"), T * i + t + 1)
                    copy(L_H[:, t, :], B[t % 2][:, 0:256]).then_inc(b_free[t % 2], 1)
                u = BASE[name][2] + 4 + t
                act.wait_ge(b_free[t % 2], u // 2 + 1 + i * 4)
                nc.scalar.activation(xtmp[:, t // 2, 256 * (t % 2):256 * (t % 2) + 256], L_H[:, t, :], ACT.Square, scale=256 ** -0.5,
                                     accum_out=stat(H_SS + t)).then_inc(s_(name + "_ss"), 1)

        def head_hi(name, i, n0):
            for m in range(2):
                act.wait_ge(s_(name + "_t"), 2 * i + m + 1)
                copy(YH[:, ds(i * 2 + m, 1), :].rearrange("p a n -> p (a n)"), C[(n0 + m) % 2][:]).then_inc(s_(name + "_hi"), 1)

        def head_tokens(name, i, j, gi, dst, func):
            for t in range(T):
                if t < 3:
                    act.wait_ge(tok_done, 3 * (g0 + gi) + t + 1 + i * 6)
                else:
                    act.wait_ge(chunk_done, c0 + j + 1 + i * 4)
                nc.scalar.activation(dst[:, t, 0:256], A[t][:, 0:256], func).then_inc(a_free[t], 1)

        act.wait_ge(s_("ml_m"), 1)
        with act.Fori(0, 4) as i:
            for j in range(2):
                split(c0 + j + 1, 4, i)
                for m in range(2):
                    if m == 0:
                        act.wait_ge(feat_done, f0 + j + 1 + i * 2)
                    else:
                        act.wait_ge(chunk_done, c0 + j + 1 + i * 4)
                    copy(L_PRE[:, m, 3:3 + S], B[m][:]).then_inc(b_free[m], 1)
                for m in range(2):
                    act.wait_ge(s_("ml_conv"), 4 * i + 2 * j + m + 1)
                    nc.scalar.activation((L_Q, L_K)[j][:, m, :], L_ACC, ACT.Silu).then_inc(s_("ml_qk"), 1)
            split(c0 + 3, 4, i)
            head_tokens("ml", i, 2, 0, L_V, ACT.Copy)
            split(c0 + 4, 4, i)
            head_tokens("ml", i, 3, 1, L_O, ACT.Sigmoid)
            for j in range(T):
                n = S - j * P
                act.wait_ge(s_("ml_w"), T * i + j + 1)
                nc.scalar.activation(L_A[:, j, 0:n], A[j][:, 0:n], ACT.Exp, scale=-1.0,
                                     bias=st[:, ds(i + (U_COL + 4 * j), 1)]).then_inc(a_free[j], 1)
            head_rms("ml", i, True)
            head_hi("ml", i, n0)

        def mix(name):
            c0, _, _, _, g0, _ = BASE[name]
            for h in range(2):
                for kh in range(4):
                    c = c0 + 4 * h + kh
                    split(c + 1)
                    if kh == 1:
                        for t in range(T):
                            wait_tok(act, t, g0 + 2 * h, c)
                            nc.scalar.activation(GATE[:, t, :], A[t][:], ACT.Sigmoid).then_inc(a_free[t], 1)

        mix("mix0")
        c0, ra, rb, n0, g0, f0 = BASE["ret"]
        with act.Fori(0, 4) as i:
            for j in range(2):
                split(c0 + j + 1, 4, i)
                act.wait_ge(feat_done, f0 + j + 1 + i * 2)
                copy((L_Q, L_K)[j][:, 0, :], B[0][:]).then_inc(b_free[0], 1)
            split(c0 + 3, 4, i)
            head_tokens("ret", i, 2, 0, L_V, ACT.Copy)
            split(c0 + 4, 4, i)
            head_tokens("ret", i, 3, 1, L_O, ACT.Silu)
            head_rms("ret", i, False)
            head_hi("ret", i, n0)
        mix("mix1")
        c0, _, _, _, g0, _ = BASE["dv"]
        for h in range(2):
            split(c0 + 2 * h + 1)
            split(c0 + 2 * h + 2)
            for t in range(T):
                wait_tok(act, t, g0 + h, c0 + 2 * h + 1)
                copy(F_V[:, t, 512 * h:512 * h + 512], A[t][:]).then_inc(a_free[t], 1)
        c0, ra, rb, n0, _, f0 = BASE["diff"]

        def transposed_out(i, h, q):
            u = (n0 + 5 * h + q) % 2
            act.wait_ge(s_("diff_t"), 8 * i + 4 * h + q + 1)
            copy(F_PT[:, 0:q + 1, tok(q)], C[u][:, 0:(q + 1) * P].rearrange("p (k n) -> p k n", n=P)).then_inc(c_free[u], 1)

        with act.Fori(0, 4) as i:
            for j in range(2):
                split(c0 + j + 1, 2, i)
                act.wait_ge(feat_done, f0 + j + 1 + i * 2)
                copy((F_Q, F_K)[j][:, 0, :], B[0][:], DIFF_SCALE if j == 0 else 1.0).then_inc(b_free[0], 1)
            for h in range(2):
                for q in range(T):
                    n = (q + 1) * P
                    if h or q:
                        act.wait_ge(s_("diff_p"), 8 * i + 4 * h + q)
                    for e in range(2):
                        u = 2 * q + e
                        act.wait_ge(s_("diff_m"), 16 * i + 8 * h + u + 1)
                        nc.scalar.activation(F_P[:, e, 0:n], A[u % 4][:, 0:n], ACT.Exp, bias=stat(NM + u),
                                             accum_out=stat(SUM + u)).then_inc(a_free[u % 4], 1)
                    if q:
                        transposed_out(i, h, q - 1)
                transposed_out(i, h, T - 1)
                act.wait_ge(s_("diff_o"), 2 * i + h + 1)
                b = (rb + h) % 2
                for q in range(T):
                    x = nc.scalar.activation(F_A[:, 0, tok(q)], B[b][:, tok(q)], ACT.Square, accum_out=stat(H_SS + q))
                x.then_inc(s_("diff_ss"), 1)
                act.wait_ge(s_("diff_ht"), 2 * i + h + 1)
                u = (n0 + 5 * h + 4) % 2
                nc.scalar.activation(YH[:, ds(i * 2 + h, 1), :].rearrange("p a n -> p (a n)"), C[u][:], ACT.Copy,
                                     scale=vec[:, SUBLN:SUBLN + 1]).then_inc(s_("diff_hi"), 1)
        mix("mix2")
        hi_transposed("yt", BASE["yt"][3], XH)
        c0, ra, _, _, g0, _ = BASE["wout"]
        for h in range(2):
            split(c0 + 2 * h + 1)
            split(c0 + 2 * h + 2)
            for t in range(T):
                wait_tok(act, t, g0 + h, c0 + 2 * h + 1)
                copy(Y[:, t, 512 * h:512 * h + 512], A[t][:]).then_inc(a_free[t], 1)
        def sums_of_squares(name, wait):
            for t in range(T):
                wait(t)
                nc.scalar.activation(SQUARES[:, t, :], Y[:, t, :], ACT.Square,
                                     accum_out=stat(SS + t)).then_inc(s_(name + "_ss"), 1)

        sums_of_squares("out", lambda t: act.wait_ge(a_free[t], ra + 2))
        scale_norm("post")
        hi_transposed("post", BASE["wout"][3], XH, NG2)
        c, ra, rb, _, _, f0 = BASE["ffn"]
        use = rb // 2
        for n, tiles in enumerate((8, 8, 6)):
            with act.Fori(0, tiles // 2) as i:
                split(c + 1, 2, i)
                for m in range(2):
                    if m == 0:
                        act.wait_ge(feat_done, f0 + 1 + i * 2)
                    else:
                        act.wait_ge(chunk_done, c + 1 + i * 2)
                    nc.scalar.activation(SILU_T[:, m, :], B[m][:], ACT.Silu).then_inc(b_free[m], 1)
                split(c + 2, 2, i)
                for m in range(2):
                    act.wait_ge(b_free[m], use + 2 + i * 2)
                    copy(YH[:, ds(i * 2 + m, 1), :].rearrange("p a n -> p (a n)"), PROD_T[:, m, :]).then_inc(s_("ffn_hi"), 1)
            c, f0, use = c + tiles, f0 + tiles, use + tiles
            for j in range(4):
                split(c + 1)
                c += 1
        sums_of_squares("fin", lambda t: act.wait_ge(a_free[t], ra + 6))

    @block.vector
    def _(dve):
        step = Tally(dve_step)
        tt, stt, ts = nc.vector.tensor_tensor, nc.vector.scalar_tensor_tensor, nc.vector.tensor_scalar

        def then(x):
            step.then(dve, x)

        def split(c, per=0, i=0):
            if c >= CHUNKS:
                return
            s = slot(c)
            dve.wait_ge(hi_ready, c + 1 + i * per)
            n = 4 * QR if c < 2 else CH
            tt(WL[s][:, 0:n], RAW[s][:, 0:n], f32(WH[s][:, 0:n]), ALU.subtract).then_inc(lo_ready, 1)

        def lo_transposed(name, n0, hi, lo, g=None, b=None):
            for k in range(KD):
                u = (n0 + k) % 2
                dve.wait_ge(s_(name + "_hi"), k + 1)
                if g is None:
                    x = tt(lo[:, k, :], C[u][:], f32(hi[:, k, :]), ALU.subtract)
                elif b is None:
                    x = stt(lo[:, k, :], C[u][:], vec[:, g + k:g + k + 1], f32(hi[:, k, :]), ALU.mult, ALU.subtract)
                else:
                    then(ts(xtmp[:, u, :], C[u][:], vec[:, g + k:g + k + 1], vec[:, b + k:b + k + 1], ALU.mult, ALU.add))
                    x = tt(lo[:, k, :], xtmp[:, u, :], f32(hi[:, k, :]), ALU.subtract)
                x.then_inc(c_free[u], 1)

        nc.vector.memset(ROWS_T, 0.0).then_inc(rows_zero, 1)
        nc.vector.memset(ones[:], 1.0)
        dve.wait_ge(consts_in, CONSTS_N * 16)
        nc.vector.tensor_copy(causalR[:], CAUSAL_T)
        nc.vector.tensor_copy(futureR[:], FUTURE_T)
        for g in range(SWA_KV):
            ts(stat(NEGSINK + 4 * g, 4).rearrange("p (e q) -> p e q", e=2),
               SINK_T[:, 4 * g:4 * g + 4].rearrange("p (q e) -> p e q", e=2), -1.0, None, ALU.mult)
        then(tt(LAMP_T, LAMB_T.rearrange("p (a b) n -> p a b n", b=2)[:, :, 0, :],
                LAMB_T.rearrange("p (a b) n -> p a b n", b=2)[:, :, 1, :], ALU.mult))
        nc.vector.tensor_reduce(stat(LAM, 2), LAMP_T, AX.X, ALU.add).then_inc(s_("lam_dot"), 1)
        dve.wait_ge(s_("lam_exp"), 1)
        then(tt(stat(LAM + 2), stat(LAM + 1), stat(LAM), ALU.subtract))
        then(ts(stat(LAM + 2), stat(LAM + 2), -LAM_INIT, None, ALU.add))
        dve.wait_ge(s_("vec_t"), 1)
        nc.vector.tensor_copy(vec[:, 0:88], A[0][:, 0:88])
        then(tt(HEADS_T, A[2][0:16, 0:3 * P], WINDOW_T, ALU.add))
        then(ts(vec[:, SUBLN:SUBLN + 1], vec[:, SUBLN:SUBLN + 1], 1.0 - LAM_INIT, None, ALU.mult))
        nc.vector.tensor_copy(vec[:, CONV:CONV + 64], A[1][:, 0:64]).then_inc(consts_done, 1)
        split(0)
        lo_transposed("xt", BASE["xt"][3], XH, XL)
        split(1)
        split(2)
        split(3)
        split(4)
        for m, table in enumerate((cosT, sinT)):
            if m == 0:
                dve.wait_ge(s_("in_kv"), 5)
            else:
                dve.wait_ge(chunk_done, 4)
            x = stt(M_T[:, m, :], B[m][:], MLA_SCALE, table[:], ALU.mult, ALU.mult)
            x.then_inc(b_free[m], 1)
        for m in range(2):
            dve.wait_ge(b_free[m], 1)
        tt(M_KR, M_T[:, 0, :], M_T[:, 1, :], ALU.add).then_inc(s_("kr_ready"), 1)
        for k in range(5):
            u = (BASE["in"][3] + k) % 2
            g = (GQ + k) if k < 3 else (GKV + k - 3)
            dve.wait_ge(s_("in_hi"), k + 1)
            stt(YL[:, k, :], C[u][:], vec[:, g:g + 1], f32(YH[:, k, :]), ALU.mult, ALU.subtract).then_inc(c_free[u], 1)
        c0, ra, rb, n0, _, _ = BASE["pair"]
        with dve.Fori(0, 4) as i:
            step.enter(i, 8)
            split(c0 + 1, 2, i)
            split(c0 + 2, 2, i)
            dve.wait_ge(s_("pair_f"), 5 * i + 2)
            nc.vector.tensor_copy(M_QN[:, 1, :], B[1][:]).then_inc(b_free[1], 1)
            dve.wait_ge(s_("pair_f"), 5 * i + 4)
            ts(M_KN[:, 1, :], B[1][:], MLA_SCALE, None, ALU.mult).then_inc(b_free[1], 1)
            dve.wait_ge(s_("pair_f"), 5 * i + 5)
            tt(M_T[:, 0, :], B[0][:], cosT[:], ALU.mult).then_inc(b_free[0], 1)
            dve.wait_ge(chunk_done, c0 + 2 + 2 * i)
            tt(M_T[:, 1, :], B[1][:], sinT[:], ALU.mult).then_inc(b_free[1], 1)
            for m in range(2):
                dve.wait_ge(b_free[m], rb // 2 + 3 + 4 * i)
            tt(M_QR, M_T[:, 0, :], M_T[:, 1, :], ALU.add).then_inc(s_("qr_ready"), 1)

            def row_max(h, q):
                dve.wait_ge(s_("pair_s"), 8 * i + 4 * h + q + 1)
                nc.vector.tensor_reduce(stat(NM + 4 * h + q), A[q][:, 0:(q + 1) * P], AX.X, ALU.max,
                                        negate=True).then_inc(s_("pair_m"), 1)

            def normalized(h, q):
                n, at = (q + 1) * P, q * (q + 1) // 2 * P
                dve.wait_ge(a_free[q], ra + 2 + h + 3 * i)
                then(nc.vector.reciprocal(stat(RINV + 4 * h + q), stat(SUM + 4 * h + q)))
                ts(M_P[:, h, at:at + n], M_P[:, h, at:at + n], stat(RINV + 4 * h + q), None, ALU.mult).then_inc(s_("pair_p"), 1)

            for q in range(T):
                row_max(0, q)
            for q in range(T):
                normalized(0, q)
                row_max(1, q)
            for q in range(T):
                normalized(1, q)
            for h in range(2):
                dve.wait_ge(s_("pair_hi"), 2 * i + h + 1)
                tt(XL[:, ds(i * 2 + h, 1), :].rearrange("p a n -> p (a n)"), B[h][:],
                   f32(XH[:, ds(i * 2 + h, 1), :]).rearrange("p a n -> p (a n)"), ALU.subtract).then_inc(b_free[h], 1)
        step.leave(4)

        def moments(name, t):
            nc.vector.bn_stats(st[:, ST6 + 12 * t:ST6 + 12 * t + 6], Y[:, t, 0:512])
            then(nc.vector.bn_stats(st[:, ST6 + 12 * t + 6:ST6 + 12 * t + 12], Y[:, t, 512:1024]))
            nc.vector.bn_aggr(stat(MV + 2 * t, 2), stat(ST6 + 12 * t, 12)).then_inc(s_(name + "_st"), 1)

        def residual(name, ln):
            c0, ra, _, _, g0, _ = BASE[name]
            for h in range(2):
                split(c0 + 2 * h + 1)
                split(c0 + 2 * h + 2)
                for t in range(T):
                    wait_tok(dve, t, g0 + h, c0 + 2 * h + 1)
                    stt(Y[:, t, 512 * h:512 * h + 512], X[:, t, 512 * h:512 * h + 512], ALPHA, A[t][:], ALU.mult, ALU.add).then_inc(a_free[t], 1)
                    if h == 1:
                        dve.wait_ge(a_free[t], ra + 2)
                        moments(ln, t)

        dve.wait_ge(s_("toeplitz_out"), 16)
        residual("wo0", "ln0")
        lo_transposed("ln0", BASE["wo0"][3], XH, XL, ln_g(0), ln_b(0))

        def mlp(name, before, ln):
            c0, ra, rb, _, g0, f0 = BASE[name]
            for t in range(T):
                dve.wait_ge(s_(before + "_y"), t + 1)
            with dve.Fori(0, 4) as i:
                for j in range(4):
                    split(c0 + j + 1, 8, i)
                    for m in range(2):
                        n = 8 * i + 2 * j + m
                        dve.wait_ge(b_free[m], rb // 2 + j + 1 + i * 4)
                        tt(SQ_T[:, m, :], R_T[:, m, :], R_T[:, m, :], ALU.mult).then_inc(s_(name + "_sq"), 1)
                        dve.wait_ge(s_(name + "_hi"), n + 1)
                        tt(YL[:, 2 * j + m, :], SQ_T[:, m, :], f32(YH[:, 2 * j + m, :]), ALU.subtract).then_inc(s_(name + "_y"), 1)
                for h in range(2):
                    split(c0 + 4 + 2 * h + 1, 8, i)
                    split(c0 + 4 + 2 * h + 2, 8, i)
                    for t in range(T):
                        if t < 3:
                            dve.wait_ge(tok_done, 3 * (g0 + h) + t + 1 + i * 6)
                        else:
                            dve.wait_ge(chunk_done, c0 + 6 + 2 * h + i * 8)
                        y = Y[:, t, 512 * h:512 * h + 512]
                        tt(y, y, A[t][:], ALU.add).then_inc(a_free[t], 1)
            for t in range(T):
                dve.wait_ge(a_free[t], ra + 8)
                moments(ln, t)

        mlp("mlp0", "ln0", "ln1")
        lo_transposed("ln1", BASE["mlp0"][3], XH, XL, ln_g(1), ln_b(1))
        c0, _, _, _, _, f0 = BASE["kv"]
        for u in range(2):
            split(c0 + u + 1)
            wait_feat(dve, 1, f0 + u, c0 + u)
            nc.vector.tensor_copy(W_K[:, 2 * S * u + S:2 * S * u + 2 * S], B[1][:]).then_inc(b_free[1], 1)
        split(c0 + 3)
        c0, ra, rb, n0, _, f0 = BASE["swa"]
        for m in range(2):
            dve.wait_ge(b_free[m], rb // 2)
        for t in range(T):
            dve.wait_ge(s_("ln1_x"), t + 1)
        with dve.Fori(0, 2) as i:
            step.enter(i, 2 * 4 * 4)
            for u in range(2):
                g = 2 * i + u
                split(c0 + u + 1, 2, i)
                dve.wait_ge(chunk_done, c0 + u + 1 + i * 2)
                ts(W_Q[:, 1, :], B[1][:], SWA_DH ** -0.5, None, ALU.mult).then_inc(b_free[1], 1)
                for e in range(2):
                    rows = slice(64 * e, 64 * e + 64)
                    x = nc.vector.tensor_copy(W_KG[rows, :], W_K[rows, ds(i * S + (0 if e == u else 2 * S), S)])
                x.then_inc(s_("swa_k"), 1)
                dve.wait_ge(s_("bias_in%d" % u), 32 * i + 32)
                for n in range(T):
                    w, z, bank = (P if n == 0 else 2 * P), n % 2, 2 * (n % 2)
                    for e in range(2):
                        dve.wait_ge(s_("swa_s"), 8 * g + 2 * n + e + 1)
                        tt(W_S[:, z, 2 * e:2 * e + 2, 0:w],
                           A[bank + e][:].rearrange("p (q n) -> p q n", q=2)[:, :, 0:w],
                           W_B[:, u, 2 * e:2 * e + 2, 256 - w:256], ALU.add).then_inc(a_free[bank + e], 1)
                    for e in range(2):
                        dve.wait_ge(a_free[bank + e], ra + 2 * u + n // 2 + 1 + 4 * i)
                    then(nc.vector.tensor_reduce(stat(W_MAX + 4 * z, 4), W_S[:, z, :, 0:w], AX.X, ALU.max, negate=True))
                    sink = st[:, ds(i * 8 + (NEGSINK + 4 * u), 4)]
                    then(tt(stat(W_NEG + 4 * z, 4), stat(W_MAX + 4 * z, 4), sink, ALU.min))
                    tt(stat(W_ES + 4 * z, 4), stat(W_NEG + 4 * z, 4), sink, ALU.subtract).then_inc(s_("swa_m"), 1)
                    dve.wait_ge(s_("swa_p"), 4 * g + n + 1)
                    then(tt(stat(W_DEN + 4 * z, 4), stat(W_SUM + 4 * z, 4), stat(W_ES + 4 * z, 4), ALU.add))
                    then(nc.vector.reciprocal(stat(W_INV + 4 * z, 4), stat(W_DEN + 4 * z, 4)))
                    x = n0 + 8 * u + 2 * n + 1
                    dve.wait_ge(s_("swa_t"), 8 * g + 2 * n + 2)
                    dst = W_PT[:, 1, :] if n else W_PT[:, 1, 256:512]
                    nc.vector.tensor_copy(dst, C[x % 2][:, 0:512 if n else 256]).then_inc(c_free[x % 2], 1)
                    dve.wait_ge(s_("swa_o"), 4 * g + n + 1)
                    y = Y[:, n, ds(i * 512 + 256 * u, 256)].rearrange("p (q e d) -> p e q d", q=2, e=2)
                    inv = stat(W_INV + 4 * z, 4).rearrange("p (e q) -> p e q", e=2).unsqueeze(3).broadcast_to([P, 2, 2, 64])
                    tt(y, B[n % 2][:, 0:256].rearrange("p (e q d) -> p e q d", e=2, q=2), inv, ALU.mult).then_inc(b_free[n % 2], 1)
        step.leave(2)
        lo_transposed("ot", BASE["ot"][3], YH, YL)
        residual("wo1", "ln2")
        lo_transposed("ln2", BASE["wo1"][3], XH, XL, ln_g(2), ln_b(2))
        mlp("mlp1", "ln2", "ln3")
        for t in range(T):
            dve.wait_ge(s_("ln3_n"), t + 1)
            if t == 0:
                dve.wait_ge(gb_in, 4 * 32)
            then(tt(X[:, t, :], Y[:, t, :], GB[:, 0, :], ALU.mult))
            tt(X[:, t, :], X[:, t, :], GB[:, 1, :], ALU.add).then_inc(s_("pre_x"), 1)
        lo_transposed("pre", BASE["pre"][3], XH, XL, NG0)
        c0, _, _, _, _, f0 = BASE["if"]
        split(c0 + 1)
        then(nc.vector.memset(G_0, 0.0))
        wait_feat(dve, 0, f0, c0)
        ts(G_I, B[0][:], GATEB[:, 0:1], None, ALU.add).then_inc(b_free[0], 1)
        wait_feat(dve, 1, f0, c0)
        ts(G_F, B[1][:], GATEB[:, 1:2], None, ALU.add).then_inc(b_free[1], 1)
        dve.wait_ge(b_free[1], BASE["if"][2] // 2 + 1)
        stt(G_T, G_F, -1.0, G_F, ALU.mult, ALU.max).then_inc(s_("if_abs"), 1)
        dve.wait_ge(s_("if_l"), 1)
        then(stt(G_F, G_F, 0.0, G_L, ALU.min, ALU.subtract))
        then(nc.vector.tensor_tensor_scan(G_B, G_F, G_0, 0.0, ALU.add, ALU.add))
        dve.wait_ge(b_free[0], BASE["if"][2] // 2 + 1)
        then(tt(G_U, G_I, G_B, ALU.subtract))
        then(nc.vector.tensor_tensor_scan(G_M, G_U, G_U, 0.0, ALU.max, ALU.max))
        tt(G_EM, G_B, G_M, ALU.add).then_inc(s_("if_m"), 1)
        n0 = BASE["if"][3]
        for m, at in enumerate((U_COL, EM_COL)):
            u = (n0 + m) % 2
            dve.wait_ge(s_("if_t"), m + 1)
            nc.vector.tensor_copy(stat(at, 16).rearrange("p (t h) -> p t h", t=T),
                                  C[u][:].rearrange("p (t n) -> p t n", t=T)[:, :, 0:4]).then_inc(c_free[u], 1)
        then(nc.vector.memset(L_PRE, 0.0))
        then(nc.vector.memset(L_V[:, :, 256:258], 1.0))

        def values_by_token(name, i):
            for t in range(T):
                dve.wait_ge(s_(name + "_r"), T * i + t + 1)
                stt(L_H[:, t, :], L_H[:, t, :], stat(H_R + t), L_O[:, t, :], ALU.mult, ALU.mult).then_inc(s_(name + "_h"), 1)

        def head_lo(name, i, n0):
            for m in range(2):
                u = (n0 + m) % 2
                dve.wait_ge(s_(name + "_hi"), 2 * i + m + 1)
                tt(YL[:, ds(i * 2 + m, 1), :].rearrange("p a n -> p (a n)"), C[u][:],
                   f32(YH[:, ds(i * 2 + m, 1), :]).rearrange("p a n -> p (a n)"), ALU.subtract).then_inc(c_free[u], 1)

        c0, ra, rb, n0, _, f0 = BASE["ml"]
        with dve.Fori(0, 4) as i:
            step.enter(i, 4 * 3 + 4 * 3)
            ts(L_M, G_M, ident[:, ds(i, 1)], None, ALU.mult).then_inc(s_("ml_m"), 1)
            for j in range(2):
                split(c0 + j + 1, 4, i)
                for m in range(2):
                    dve.wait_ge(b_free[m], rb // 2 + 1 + j + 4 * i)
                    if j or m:
                        dve.wait_ge(s_("ml_qk"), 4 * i + 2 * j + m)
                    tap = [vec[:, ds(i * 2 + (CONV + 16 * q + 8 * j + m), 1)] for q in range(4)]
                    then(ts(L_ACC, L_PRE[:, m, 0:S], tap[0], None, ALU.mult))
                    then(stt(L_ACC, L_PRE[:, m, 1:1 + S], tap[1], L_ACC, ALU.mult, ALU.add))
                    then(stt(L_ACC, L_PRE[:, m, 2:2 + S], tap[2], L_ACC, ALU.mult, ALU.add))
                    stt(L_ACC, L_PRE[:, m, 3:3 + S], tap[3], L_ACC, ALU.mult, ALU.add).then_inc(s_("ml_conv"), 1)
            split(c0 + 3, 4, i)
            split(c0 + 4, 4, i)
            for j in range(T):
                n = S - j * P
                dve.wait_ge(s_("ml_s"), T * i + j + 1)
                dve.wait_ge(a_free[j], ra + 3 + 4 * i)
                stt(L_A[:, j, 0:n], A[j][:, 0:n], 1.0 / 16.0, L_A[:, j, 0:n], ALU.mult, ALU.mult).then_inc(a_free[j], 1)
            for t in range(T):
                dve.wait_ge(s_("ml_o"), T * i + t + 1)
                den = stat(H_DEN + t)
                then(nc.vector.tensor_copy(den, B[t % 2][:, 256:257]))
                then(stt(den, den, -1.0, den, ALU.mult, ALU.max))
                then(ts(den, den, st[:, ds(i + (EM_COL + 4 * t), 1)], None, ALU.max))
                nc.vector.reciprocal(stat(H_INV + t), den).then_inc(s_("ml_d"), 1)
            values_by_token("ml", i)
            head_lo("ml", i, n0)
        step.leave(4)

        def mix(name, n):
            c0, ra, _, _, g0, _ = BASE[name]
            for h in range(2):
                for kh in range(4):
                    c = c0 + 4 * h + kh
                    split(c + 1)
                for t in range(T):
                    wait_tok(dve, t, g0 + 2 * h + 1, c0 + 4 * h + 3)
                    dve.wait_ge(a_free[t], ra + 2 * h + 1)
                    y, tmp = Y[:, t, 512 * h:512 * h + 512], xtmp[:, t % 2, :]
                    if n == 0:
                        tt(y, GATE[:, t, :], A[t][:], ALU.mult).then_inc(a_free[t], 1)
                    else:
                        tt(tmp, GATE[:, t, :], A[t][:], ALU.mult).then_inc(a_free[t], 1)
                        dve.wait_ge(a_free[t], ra + 2 * h + 2)
                        tt(y, y, tmp, ALU.add).then_inc(s_("mixed"), 1)

        mix("mix0", 0)
        c0, ra, rb, n0, _, f0 = BASE["ret"]
        dve.wait_ge(s_("decay_in"), 16)
        with dve.Fori(0, 4) as i:
            step.enter(i, 0)
            for j in range(2):
                split(c0 + j + 1, 4, i)
                dve.wait_ge(chunk_done, c0 + j + 1 + i * 4)
                nc.vector.tensor_copy((L_Q, L_K)[j][:, 1, :], B[1][:]).then_inc(b_free[1], 1)
            split(c0 + 3, 4, i)
            split(c0 + 4, 4, i)
            for j in range(T):
                n = S - j * P
                dve.wait_ge(s_("ret_s"), T * i + j + 1)
                decay = DECAY[:, ds(i, 1), 0:n].rearrange("p a n -> p (a n)")
                tt(L_A[:, j, 0:n], A[j][:, 0:n], decay, ALU.mult).then_inc(a_free[j], 1)
            values_by_token("ret", i)
            head_lo("ret", i, n0)
        mix("mix1", 1)
        c0 = BASE["dv"][0]
        for c in range(c0, c0 + 4):
            split(c + 1)
        c0, ra, rb, n0, _, f0 = BASE["diff"]
        dve.wait_ge(s_("alibi_in"), 16)
        with dve.Fori(0, 4) as i:
            step.enter(i, 2 * 4 * 3)
            for j in range(2):
                split(c0 + j + 1, 2, i)
                dve.wait_ge(chunk_done, c0 + j + 1 + i * 2)
                ts((F_Q, F_K)[j][:, 1, :], B[1][:], DIFF_SCALE if j == 0 else 1.0, None, ALU.mult).then_inc(b_free[1], 1)
            for h in range(2):
                ts(slopeR[:], ALIBI, st[:, ds(i * 2 + (SLOPE + h), 1)], None, ALU.mult).then_inc(s_("diff_b"), 1)

                def row_max(q):
                    for e in range(2):
                        u = 2 * q + e
                        dve.wait_ge(s_("diff_s"), 16 * i + 8 * h + u + 1)
                        nc.vector.tensor_reduce(stat(NM + u), A[u % 4][:, 0:(q + 1) * P], AX.X, ALU.max,
                                                negate=True).then_inc(s_("diff_m"), 1)

                row_max(0)
                for q in range(T):
                    n = (q + 1) * P
                    if q + 1 < T:
                        row_max(q + 1)
                    for e in range(2):
                        u = 2 * q + e
                        dve.wait_ge(a_free[u % 4], ra + 2 * h + u // 4 + 1 + 4 * i)
                    then(nc.vector.reciprocal(stat(RINV + 2 * q, 2), stat(SUM + 2 * q, 2)))
                    then(tt(stat(RINV + 2 * q + 1), stat(RINV + 2 * q + 1), stat(LAM + 2), ALU.mult))
                    if q >= 2:
                        dve.wait_ge(s_("diff_t"), 8 * i + 4 * h + q - 1)
                    then(ts(F_A[:, q % 2, 0:n], F_P[:, 1, 0:n], stat(RINV + 2 * q + 1), None, ALU.mult))
                    stt(F_A[:, q % 2, 0:n], F_P[:, 0, 0:n], stat(RINV + 2 * q), F_A[:, q % 2, 0:n], ALU.mult, ALU.add).then_inc(s_("diff_p"), 1)
                b = (rb + h) % 2
                dve.wait_ge(s_("diff_r"), 2 * i + h + 1)
                for q in range(T):
                    x = ts(F_H[:, tok(q)], B[b][:, tok(q)], stat(H_R + q), None, ALU.mult)
                x.then_inc(b_free[b], 1)
                u = (n0 + 5 * h + 4) % 2
                dve.wait_ge(s_("diff_hi"), 2 * i + h + 1)
                stt(YL[:, ds(i * 2 + h, 1), :].rearrange("p a n -> p (a n)"), C[u][:], vec[:, SUBLN:SUBLN + 1],
                    f32(YH[:, ds(i * 2 + h, 1), :]).rearrange("p a n -> p (a n)"), ALU.mult, ALU.subtract).then_inc(c_free[u], 1)
        step.leave(4)
        mix("mix2", 2)
        lo_transposed("yt", BASE["yt"][3], XH, XL)
        c0 = BASE["wout"][0]
        for c in range(c0, c0 + 4):
            split(c + 1)

        def add_normed(name, gb, after):
            dve.wait_ge(gb_in, gb)
            for t in range(T):
                dve.wait_ge(s_(name + "_r"), t + 1)
                then(stt(Y[:, t, :], Y[:, t, :], stat(RS + 4 + t), GB[:, 0, :], ALU.mult, ALU.mult))
                tt(X[:, t, :], X[:, t, :], Y[:, t, :], ALU.add).then_inc(s_(after), 1)

        add_normed("out", 4 * 32 + 16, "post_x")
        lo_transposed("post", BASE["wout"][3], XH, XL, NG2)
        c, ra, rb, _, g0, f0 = BASE["ffn"]
        use, done, silus = rb // 2, 0, 0
        dve.wait_ge(s_("ffn_0"), 1)
        for n, tiles in enumerate((8, 8, 6)):
            with dve.Fori(0, tiles // 2) as i:
                split(c + 1, 2, i)
                split(c + 2, 2, i)
                for m in range(2):
                    if m == 0:
                        dve.wait_ge(feat_done, f0 + 2 + i * 2)
                    else:
                        dve.wait_ge(chunk_done, c + 2 + i * 2)
                    dve.wait_ge(b_free[m], use + 1 + i * 2)
                    tt(PROD_T[:, m, :], SILU_T[:, m, :], B[m][:], ALU.mult).then_inc(b_free[m], 1)
                    dve.wait_ge(s_("ffn_hi"), done + m + 1 + i * 2)
                    tt(YL[:, ds(i * 2 + m, 1), :].rearrange("p a n -> p (a n)"), PROD_T[:, m, :],
                       f32(YH[:, ds(i * 2 + m, 1), :]).rearrange("p a n -> p (a n)"), ALU.subtract).then_inc(s_("ffn_y"), 1)
            c, f0, use, done = c + tiles, f0 + tiles, use + tiles, done + tiles
            for h in range(2):
                split(c + 1)
                split(c + 2)
                for t in range(T):
                    wait_tok(dve, t, g0 + 2 * n + h, c + 1)
                    y = Y[:, t, 512 * h:512 * h + 512]
                    tt(y, y, A[t][:], ALU.add).then_inc(a_free[t], 1)
                c += 2
        add_normed("fin", 4 * 32 + 32, "fin_x")

    @block.gpsimd
    def _(pool):
        step = Tally(pool_step)
        tt, ts = nc.gpsimd.tensor_tensor, nc.gpsimd.tensor_scalar

        def then(x):
            step.then(pool, x)

        then(nc.gpsimd.memset(st[:], 0.0))
        for at, value in ((NEGHALF, -0.5), (EPSILON, RMS_EPS), (PER_DIM, 1.0 / 128)):
            then(nc.gpsimd.memset(stat(at, T), value))

        def flat(v):
            return v.rearrange("(a n) -> a n", a=1)

        for dst, src in (
                (ident[:], a["c_ident"]), (CAUSAL_T, a["c_causal"]), (FUTURE_T, a["c_future"]),
                (cosT[:], a["c_cos"]), (sinT[:], a["c_sin"]), (RELB, a["rel_bias"]), (ONEHOT, a["c_onehot"]),
                (WINDOW_T, a["c_window"]), (stat(SLOPE, 8), a["c_slope"]),
                (SINK_T, a["swa_sinks"].broadcast_to([P, 16])),
                (LAMB_T.rearrange("p a n -> p (a n)"),
                 a["diff_lambda_2"].rearrange("a l n -> a (l n)").broadcast_to([P, 256])),
                (GATEB[0:4, :], a["mlstm_gate_bias_2"][0].rearrange("g h -> h g"))):
            pool.dma_start(dst, src, allow_slow_non_contiguous=True).then_inc(consts_in, 16)
        pool.wait_ge(rows_zero, 1)
        vectors = []
        for n in range(4):
            for at, name in ((ln_g(n), "_g"), (ln_b(n), "_b")):
                v = a[("ln_mix", "ln_mlp")[n % 2] + name][n // 2]
                vectors.append((at, KD, 0, v.rearrange("(k p) -> k p", p=P)))
        for at, n in ((NG0, 0), (NG2, 2)):
            vectors.append((at, KD, 0, a["norm_gains_2"][0, n].rearrange("(k p) -> k p", p=P)))
        vectors.append((GQ, 3, 0, a["mla_g_q"][0].rearrange("(k p) -> k p", p=P)))
        vectors.append((GKV, 2, 0, a["mla_g_kv"][0].rearrange("(k p) -> k p", p=P)))
        vectors.append((SUBLN, 1, 0, a["diff_subln_2"][0].rearrange("(k p) -> k p", p=P)))
        vectors.append((0, 64, 1, a["mlstm_conv_2"][0].rearrange("j (k p) -> (j k) p", p=P)))
        assert len(vectors) == ROWS_N
        for at, n, m, src in vectors:
            pool.dma_start(ROWS_T[at:at + n, m, :], src).then_inc(rows_in, 16)

        def load_gb(*vs):
            for n, v in enumerate(vs):
                pool.dma_start(GB[:, n, :], flat(v).broadcast_to([P, D])).then_inc(gb_in, 16)

        load_gb(a["ln_mix_g"][0], a["ln_mix_b"][0])

        def power(dst, src, n, width, eps, signal):
            then(ts(stat(dst, n), stat(src, n), 1.0 / width, eps, ALU.mult, ALU.add))
            tt(stat(dst, n), stat(dst, n), stat(NEGHALF, n), ALU.pow).then_inc(signal, 1)

        for n, width in enumerate((QR, KVR)):
            for t in range(T):
                pool.wait_ge(s_("in_ss"), 4 * n + t + 1)
                power(RS + 4 * n + t, SS + 4 * n + t, 1, width, RMS_EPS, s_("in_r"))
        pool.wait_ge(consts_done, 1)
        pool.dma_start(scr, HEADS_T.unsqueeze(1).broadcast_to([16, P, 3 * P])).then_inc(s_("toeplitz_out"), 16)

        def layer_norm(ln):
            for t in range(T):
                pool.wait_ge(s_(ln + "_st"), t + 1)
                then(ts(stat(RS + t), stat(MV + 2 * t + 1), LN_EPS, None, ALU.add))
                then(tt(stat(RS + t), stat(RS + t), stat(NEGHALF), ALU.pow))
                then(ts(stat(NMR + t), stat(MV + 2 * t), -1.0, None, ALU.mult))
                tt(stat(NMR + t), stat(NMR + t), stat(RS + t), ALU.mult).then_inc(s_(ln + "_r"), 1)

        def gains(ln, n, ahead):
            pool.wait_ge(gb_in, 32 * n + 32)
            for t in range(T):
                pool.wait_ge(s_(ln + "_n"), t + 1)
                then(tt(X[:, t, :], Y[:, t, :], GB[:, 0, :], ALU.mult))
                x = tt(X[:, t, :], X[:, t, :], GB[:, 1, :], ALU.add)
                if ahead:
                    then(x)
                else:
                    x.then_inc(s_(ln + "_x"), 1)
            if ahead:
                pool.wait_ge(s_(ln + "_t"), KD)
                for t in range(T):
                    ts(Y[:, t, :], X[:, t, :], ALPHA, None, ALU.mult).then_inc(s_(ln + "_y"), 1)

        layer_norm("ln0")
        gains("ln0", 0, True)
        load_gb(a["ln_mlp_g"][0], a["ln_mlp_b"][0])
        layer_norm("ln1")
        gains("ln1", 1, False)
        pool.wait_ge(s_("ln1_x"), T)
        load_gb(a["ln_mix_g"][1], a["ln_mix_b"][1])
        pool.wait_ge(s_("toeplitz_out"), 16)
        for g in range(SWA_KV):
            if g >= 2:
                pool.wait_ge(s_("swa_m"), 4 * (g - 1))
            for e in range(2):
                rows = bass.AP(scr.tensor, (4 * g + e) * 3 * P * P + P - 1, [[3 * P - 1, P], [2 * 3 * P * P, 2], [1, 2 * P]])
                pool.dma_start(W_B[:, g % 2, 2 * e:2 * e + 2, :], rows).then_inc(s_("bias_in%d" % (g % 2)), 16)
        layer_norm("ln2")
        gains("ln2", 2, True)
        load_gb(a["ln_mlp_g"][1], a["ln_mlp_b"][1])
        layer_norm("ln3")

        def rms(name, dst, src, width):
            for t in range(T):
                pool.wait_ge(s_(name + "_ss"), t + 1)
                power(dst + t, src + t, 1, width, RMS_EPS, s_(name + "_r"))

        rms("pre", RS, SS, D)
        load_gb(a["norm_gains_2"][0, 1])

        def heads_rms(name):
            with pool.Fori(0, 4) as i:
                step.enter(i, T)
                for t in range(T):
                    pool.wait_ge(s_(name + "_ss"), T * i + t + 1)
                    then(tt(stat(H_R + t), stat(H_SS + t), stat(EPSILON), ALU.add))
                    tt(stat(H_R + t), stat(H_R + t), stat(NEGHALF), ALU.pow).then_inc(s_(name + "_r"), 1)
            step.leave(4)

        heads_rms("ml")
        pool.wait_ge(chunk_done, BASE["mix0"][0] + 1)
        pool.dma_start(DECAY, a["c_decay"]).then_inc(s_("decay_in"), 16)
        heads_rms("ret")
        pool.wait_ge(s_("mixed"), 8)
        pool.dma_start(ALIBI, a["c_alibi"]).then_inc(s_("alibi_in"), 16)
        with pool.Fori(0, 4) as i:
            step.enter(i, 4)
            for h in range(2):
                pool.wait_ge(s_("diff_ss"), 2 * i + h + 1)
                then(tt(stat(H_R, T), stat(H_SS, T), stat(PER_DIM, T), ALU.mult))
                then(tt(stat(H_R, T), stat(H_R, T), stat(EPSILON, T), ALU.add))
                tt(stat(H_R, T), stat(H_R, T), stat(NEGHALF, T), ALU.pow).then_inc(s_("diff_r"), 1)
        step.leave(4)
        rms("out", RS + 4, SS, D)
        pool.wait_ge(s_("post_x"), T)
        load_gb(a["norm_gains_2"][0, 3])
        rms("post", RS, SS, D)
        pool.wait_ge(s_("post_t"), KD)
        for t in range(T):
            x = nc.gpsimd.memset(Y[:, t, :], 0.0)
        x.then_inc(s_("ffn_0"), 1)
        rms("fin", RS + 4, SS, D)

    ctx.close()


def kernel(**inputs):
    import concourse.bacc as bacc
    from concourse import mybir
    from concourse.bass_utils import run_bass_kernel_spmd

    nc = bacc.Bacc("TRN2", target_bir_lowering=False, num_devices=1)
    arrays, aps = {}, {}
    for name, value in {**inputs, **constants()}.items():
        v = np.ascontiguousarray(value)
        arrays["in_" + name] = v
        aps[name] = nc.dram_tensor("in_" + name, v.shape, mybir.dt.from_np(v.dtype), kind="ExternalInput").ap()
    out = nc.dram_tensor("out", (1, S, D), mybir.dt.float32, kind="ExternalOutput").ap()
    build(nc, aps, out)
    return run_bass_kernel_spmd(nc, [arrays], core_ids=[0]).results[0]["out"]
```

```python
import numpy as np
from contextlib import ExitStack

P = 128
S = 512
T = S // P
D = 1024
KD = D // P
CH = 2048

MLA_HEADS, NOPE, ROPE, VDIM, QR, KVR = 8, 128, 64, 128, 384, 256
SWA_KV, SWA_DH, WINDOW, BUCKETS = 4, 64, 128, 32
SWA_G = 4
D_FF = 4 * D
FFN = 2816
FT = FFN // P
ALPHA = 4 ** 0.25
LN_EPS, RMS_EPS = 1e-5, 1e-6
MLA_SCALE = (NOPE + ROPE) ** -0.5
BIG = float(2.0 ** 100)
DIFF_SCALE = 64 ** -0.5
LAM_INIT = 0.2

PLAN = [
    ("xt", 0, 1, 2, 2, 0, 0),
    ("in", 4, 2, 2, 7, 1, 0),
    ("pair", 8, 12, 32, 32, 4, 0),
    ("wo0", 4, 3, 2, 2, 2, 0),
    ("mlp0", 32, 9, 34, 2, 8, 16),
    ("kv", 3, 1, 4, 0, 1, 2),
    ("swa", 4, 8, 24, 32, 0, 4),
    ("ot", 0, 1, 2, 2, 0, 0),
    ("wo1", 4, 3, 2, 2, 2, 0),
    ("mlp1", 32, 8, 32, 0, 8, 16),
    ("pre", 0, 1, 2, 2, 0, 0),
    ("if", 1, 0, 2, 2, 0, 1),
    ("ml", 16, 16, 32, 8, 8, 8),
    ("mix0", 8, 4, 0, 0, 4, 0),
    ("ret", 16, 12, 32, 8, 8, 8),
    ("mix1", 8, 4, 0, 0, 4, 0),
    ("dv", 4, 2, 0, 0, 2, 0),
    ("diff", 8, 16, 24, 40, 0, 8),
    ("mix2", 8, 4, 0, 0, 4, 0),
    ("yt", 0, 1, 2, 2, 0, 0),
    ("wout", 4, 3, 2, 2, 2, 0),
    ("ffn", 34, 6, 44, 0, 6, 22),
]
BASE, _at = {}, [0] * 6
for _name, *_n in PLAN:
    BASE[_name] = tuple(_at)
    _at = [a + b for a, b in zip(_at, _n)]
CHUNKS = _at[0]


def constants():
    f = np.float32
    i, j = np.arange(P)[:, None], np.arange(P)[None, :]
    half = ROPE // 2
    inv = (f(10000.0) ** (-np.arange(half, dtype=f) / f(half))).astype(f)
    ang = (np.arange(S, dtype=f)[:, None] * inv[None, :]).astype(f).astype(np.float64)
    freq = np.arange(P) % half
    sign = np.where(np.arange(P) % ROPE < half, -1.0, 1.0)
    jj = np.arange(S)[None, :] - (S - P)
    alibi = -np.abs(i - jj).astype(np.float64)
    alibi = np.where((jj >= 0) & (jj // 64 > i // 64), -BIG, alibi)
    h = np.arange(4, dtype=np.float64)
    log_gamma = np.log(1.0 - 2.0 ** (-5.0 - h))
    rel = np.arange(S)[None, :] - i
    decay = np.where(rel[None] >= 0, np.exp(log_gamma[:, None, None] * np.maximum(rel, 0)[None]), 0.0) / 16.0
    dist = 255 - np.arange(3 * P)
    ok = (dist >= 0) & (dist < WINDOW)
    n = np.clip(dist, 0, None)
    nf = np.maximum(n, 1).astype(f)
    large = 16 + (np.log(nf / f(16)) / f(np.log(8.0)) * f(16)).astype(np.int32)
    bucket = np.where(n < 16, n, np.minimum(large, BUCKETS - 1))
    onehot = (ok[None, :] & (bucket[None, :] == np.arange(BUCKETS)[:, None]))
    return {
        "c_ident": np.eye(P, dtype=f),
        "c_causal": np.where(j > i, -BIG, 0.0).astype(f),
        "c_future": np.where(j < i, BIG, 0.0).astype(f),
        "c_cos": np.cos(ang).T[freq].astype(f),
        "c_sin": (np.sin(ang).T[freq] * sign[:, None]).astype(f),
        "c_alibi": alibi.astype(f),
        "c_slope": np.broadcast_to(2.0 ** -np.arange(1.0, 9.0), (P, 8)).astype(f).copy(),
        "c_decay": np.ascontiguousarray(decay.transpose(1, 0, 2)).astype(f),
        "c_onehot": onehot.astype(f),
        "c_window": np.broadcast_to(np.where(ok, 0.0, -BIG), (16, 3 * P)).astype(f).copy(),
    }


class Tally:

    def __init__(self, sem):
        self.sem, self.base, self.k, self.i, self.per = sem, 0, 0, 0, 0

    def enter(self, i, per):
        self.base, self.k, self.i, self.per = self.base + self.k, 0, i, per

    def leave(self, n):
        assert self.k == self.per, (self.k, self.per)
        self.base, self.k, self.i, self.per = self.base + n * self.per, 0, 0, 0

    def value(self):
        return self.base + self.k + self.i * self.per

    def then(self, engine, instruction):
        self.k += 1
        instruction.then_inc(self.sem, 1)
        engine.wait_ge(self.sem, self.value())


def build(nc, a, out):
    import concourse.bass as bass
    from concourse import mybir

    F32, F32R = mybir.dt.float32, mybir.dt.float32r
    ALU, ACT, AX = mybir.AluOpType, mybir.ActivationFunctionType, mybir.AxisListType
    ds = bass.ds
    ctx = ExitStack()

    def sb(name, shape, dt=F32):
        return ctx.enter_context(nc.sbuf_tensor(name, shape, dt))

    def sem(name):
        return ctx.enter_context(nc.semaphore(name))

    X = sb("X", [P, T, D])
    Y = sb("Y", [P, T, D])
    XH, XL = sb("XH", [P, KD, S], F32R), sb("XL", [P, KD, S], F32R)
    YH, YL = sb("YH", [P, KD, S], F32R), sb("YL", [P, KD, S], F32R)
    RAW = [sb(f"RAW{s}", [P, CH]) for s in range(2)]
    WH = [sb(f"WH{s}", [P, CH], F32R) for s in range(2)]
    WL = [sb(f"WL{s}", [P, CH], F32R) for s in range(2)]
    GB = sb("GB", [P, 2, D])
    ident, identR = sb("ident", [P, P]), sb("identR", [P, P], F32R)
    ones = sb("ones", [P, P])
    causalR, futureR = sb("causalR", [P, P], F32R), sb("futureR", [P, P], F32R)
    slopes = sb("slopes", [P, 2, S], F32R)
    vec = sb("vec", [P, 112])
    st = sb("st", [P, 256])
    xtmp = sb("xtmp", [P, 2, S])
    ar = sb("ar", [P, 10240])
    scr = nc.dram_tensor("toeplitz", (16, P, 3 * P), F32, kind="Internal").ap()

    A = [ctx.enter_context(nc.psum_tensor(f"A{t}", [P, S], F32)) for t in range(4)]
    B = [ctx.enter_context(nc.psum_tensor(f"B{m}", [P, S], F32)) for m in range(2)]
    C = [ctx.enter_context(nc.psum_tensor(f"C{m}", [P, S], F32)) for m in range(2)]

    def cut(at, *shape):
        n = int(np.prod(shape))
        assert at + n <= 10240
        v = ar[:, at:at + n]
        if len(shape) == 2:
            v = v.rearrange("p (a b) -> p a b", a=shape[0])
        if len(shape) == 3:
            v = v.rearrange("p (a b c) -> p a b c", a=shape[0], b=shape[1])
        return v

    def grid(t, k, n, at=0):
        return t[:, at:at + k * n].rearrange("p (k n) -> p k n", k=k)

    def f32(ap):
        return ap.bitcast(F32)

    def tok(t):
        return slice(t * P, (t + 1) * P)

    def ln_b(n):
        return 8 * n
    NG0, NG2, GQ, GKV, SUBLN, CONV = 24, 32, 40, 43, 45, 48
    GATEB = st[:, 184:186]

    raw_in = [sem(f"raw_in{s}") for s in range(2)]
    raw_more = [sem(f"raw_more{s}") for s in range(2)]
    hi_ready, lo_ready = sem("hi_ready"), sem("lo_ready")
    chunk_done = sem("chunk_done")
    tok_done = sem("tok_done")
    feat_done = sem("feat_done")
    a_free = [sem(f"a_free{t}") for t in range(4)]
    b_free = [sem(f"b_free{m}") for m in range(2)]
    c_free = [sem(f"c_free{m}") for m in range(2)]
    dve_step, pool_step = sem("dve_step"), sem("pool_step")
    ident_in, consts_in = sem("ident_in"), sem("consts_in")
    x_in = [sem(f"x_in{t}") for t in range(T)]
    rows_in, rows_zero = sem("rows_in"), sem("rows_zero")
    consts_done, masks_done = sem("consts_done"), sem("masks_done")
    gb_in = sem("gb_in")
    stage_sems = {}

    def s_(name):
        if name not in stage_sems:
            stage_sems[name] = sem(name)
        return stage_sems[name]

    def slot(c):
        return c % 2

    def c_all_free(pe, n):
        pe.wait_ge(c_free[0], (n + 1) // 2)
        pe.wait_ge(c_free[1], n // 2)

    def eight_banks(a, b, c, a_first):
        four = [(A[t], a_free[t], a) for t in range(4)]
        rest = [(B[m], b_free[m], b // 2) for m in range(2)] + [(C[m], c_free[m], (c + 1 - m) // 2) for m in range(2)]
        return four + rest if a_first else rest + four

    def banks_of(name):
        phase, a, b, first = {"xt": ("xt", 0, 0, True), "ln0": ("wo0", 2, 0, False), "ln1": ("mlp0", 8, 32, False),
                              "ot": ("ot", 0, 0, True), "ln2": ("wo1", 2, 0, False), "pre": ("pre", 0, 0, False),
                              "yt": ("yt", 0, 0, True), "post": ("wout", 2, 0, False)}[name]
        _, ra, rb, n0, _, _ = BASE[phase]
        return eight_banks(ra + a, rb + b, n0, first)

    def wait_tok(e, t, g, c):
        if t < 3:
            e.wait_ge(tok_done, 3 * g + t + 1)
        else:
            e.wait_ge(chunk_done, c + 1)

    def wait_feat(e, m, f, c):
        if m == 0:
            e.wait_ge(feat_done, f + 1)
        else:
            e.wait_ge(chunk_done, c + 1)

    cosT, sinT = xtmp[:, 0, :], xtmp[:, 1, :]
    RELB, ONEHOT, WINDOW_T, HEADS_T = (ar[0:32, 4300:4316], ar[0:32, 4320:4704], ar[0:16, 4704:5088], Y[0:16, T - 1, 0:3 * P])
    CAUSAL_T, FUTURE_T, SINK_T, LAMB_T = cut(5500, P), cut(5628, P), cut(5760, 16), cut(5780, 4, 64)
    ROWS_T, LAMP_T = cut(4000, 2, P), cut(6040, 2, 64)
    M_QN, M_KN, M_QR, M_V = cut(0, 2, S), cut(1024, 2, S), cut(2048, S), cut(2560, T, 256)
    M_P, M_PT, M_T, M_KR = cut(3584, 2, 1280), cut(6144, T, S), cut(8192, 2, S), cut(9216, S)
    C_N = cut(0, T, QR + KVR)
    R_T, SQ_T = cut(0, 2, S), cut(1024, 2, S)
    W_K = [cut(9216, 2, S), xtmp[:]]
    W_V, W_Q, W_KG = cut(0, T, 256), cut(1024, 2, 2, S), cut(3072, 2, S)
    W_B, W_S, W_PT = cut(4096, 2, 4, 256), cut(6144, 2, 4, 256), cut(8192, 2, S)
    G_I, G_F, G_T, G_L = cut(0, S), cut(512, S), cut(1024, S), cut(1536, S)
    G_B, G_U, G_EM, G_0, G_M = cut(2048, S), cut(2560, S), cut(3072, S), cut(3584, S), cut(9232, S)
    L_Q, L_K, L_V, L_A = cut(0, 2, S), cut(1024, 2, S), cut(2048, T, 258), cut(3080, T, S)
    L_H, L_O, L_M = cut(5128, T, 256), cut(6152, T, 256), cut(7176, S)
    L_PRE, L_ACC, DECAY = cut(7688, 2, 516), cut(8720, S), cut(7176, 4, S)
    F_V, F_Q, F_K, F_A = cut(0, T, D), cut(4096, 2, S), cut(5120, 2, S), cut(6144, 2, S)
    F_P = [cut(7168, 2, S), GB[:, 0, :].rearrange("p (e n) -> p e n", e=2)]
    F_PT, F_H, ALIBI = cut(8192, T, S), xtmp[:, 0, :], xtmp[:, 1, :]
    GATE = cut(5128, T, S)
    SQUARES = cut(4096, T, D)
    SILU_T, PROD_T = cut(0, 2, S), cut(1024, 2, S)
    SS, RS, MV, ST6, NMR = 0, 8, 16, 24, 72
    NM, SUM, RINV = 76, 84, 92
    W_MAX, W_NEG, W_SUM, W_ES, W_DEN, W_INV, NEGSINK, LAM = 100, 108, 116, 124, 132, 140, 148, 164
    NEGHALF, EPSILON = 168, 172
    U_COL, EM_COL, H_DEN, H_INV, H_SS, H_R, SLOPE = 192, 208, 224, 228, 232, 236, 240

    def stat(at, n=1):
        return st[:, at:at + n]

    CONSTS_N, ROWS_N = 11, 9

    block = ctx.enter_context(nc.Block())

    @block.sync
    def _(sp):
        def load_x(t):
            sp.dma_start(X[:, t, :], a["x"][0, tok(t), :]).then_inc(x_in[t], 16)

        sp.dma_start(ident[:], a["c_ident"]).then_inc(ident_in, 16)
        def load(c, s, *pieces):
            if not isinstance(c, int) or c >= 2:
                sp.wait_ge(lo_ready, c - 1)
            for dst, src in pieces[:-1]:
                sp.dma_start(dst, src).then_inc(raw_more[s], 16)
            dst, src = pieces[-1]
            sp.dma_start(dst, src).then_inc(raw_in[s], 16)

        def rows(w):
            return w.rearrange("(k p) n -> p k n", p=P)

        def load_tokens(c0, w, halves=2):
            for h in range(halves):
                for kh in range(2):
                    c = c0 + 2 * h + kh
                    load(c, slot(c), (grid(RAW[slot(c)], 4, 512), rows(w)[:, 4 * kh:4 * kh + 4, 512 * h:512 * h + 512]))

        def load_mlp(c0, up, down):
            with sp.Fori(0, 4) as i:
                for j in range(4):
                    s = slot(c0 + j)
                    load(c0 + j + 8 * i, s, (grid(RAW[s], 8, 256), rows(up)[:, :, ds(i * 1024 + 256 * j, 256)]))
                for j in range(4, 8):
                    h, kh, s = (j - 4) // 2, j % 2, slot(c0 + j)
                    load(c0 + j + 8 * i, s, (grid(RAW[s], 4, 512), rows(down)[:, ds(i * 8 + 4 * kh, 4), 512 * h:512 * h + 512]))

        w_in = rows(a["mla_w_in"][0])
        for kh in range(2):
            load_x(2 * kh)
            load_x(2 * kh + 1)
            load(kh, slot(kh), (grid(RAW[kh], 4, QR), w_in[:, 4 * kh:4 * kh + 4, 0:QR]))
        for kh in range(2):
            g, w, r0 = grid(RAW[kh], 4, 512), w_in[:, 4 * kh:4 * kh + 4, :], QR + KVR
            half = ROPE // 2
            load(2 + kh, slot(2 + kh),
                 (g[:, :, 256:320], w[:, :, r0:r0 + ROPE]), (g[:, :, 320:384], w[:, :, r0:r0 + ROPE]),
                 *[(g[:, :, 384 + half * q:384 + half * q + half],
                    w[:, :, r0 + half * (1 - q % 2):r0 + half * (1 - q % 2) + half]) for q in range(4)],
                 (g[:, :, 0:KVR], w[:, :, QR:QR + KVR]))
        c0 = BASE["pair"][0]
        w_uv = a["mla_w_uv"][0].rearrange("(k p) h v -> p k (h v)", p=P)
        w_uk = a["mla_w_uk"][0].rearrange("(k p) h v -> p k (h v)", p=P)
        w_uq = a["mla_w_uq"][0].rearrange("(k p) h v -> p k (h v)", p=P)
        with sp.Fori(0, 4) as i:
            s = slot(c0)
            load(c0 + 2 * i, s, (grid(RAW[s], 2, 256), w_uv[:, :, ds(i * 256, 256)]))
            s = slot(c0 + 1)
            g, hw, half = grid(RAW[s], 3, 512), NOPE + ROPE, ROPE // 2
            load(c0 + 1 + 2 * i, s,
                 *[(g[:, :, 128 * h:128 * h + 128], w_uq[:, :, ds(i * (2 * hw) + hw * h, NOPE)]) for h in range(2)],
                 *[(g[:, :, 256 + 64 * h:256 + 64 * h + 64], w_uq[:, :, ds(i * (2 * hw) + hw * h + NOPE, ROPE)]) for h in range(2)],
                 *[(g[:, :, 384 + 64 * h + half * q:384 + 64 * h + half * q + half],
                    w_uq[:, :, ds(i * (2 * hw) + hw * h + NOPE + half * (1 - q), half)]) for h in range(2) for q in range(2)],
                 (grid(RAW[s], 2, 256, 1536), w_uk[:, :, ds(i * 256, 256)]))
        load_tokens(BASE["wo0"][0], a["mla_w_o"][0])
        load_mlp(BASE["mlp0"][0], a["mlp_w_up"][0], a["mlp_w_down"][0])
        c0, w_kv = BASE["kv"][0], rows(a["kv_w_shared"])
        s = slot(c0)
        load(c0, s, (grid(RAW[s], 8, 256), w_kv[:, :, 0:256]))
        s = slot(c0 + 1)
        g = grid(RAW[s], 8, 256)
        load(c0 + 1, s, *[(g[:, :, 128 * j + 64 * e:128 * j + 64 * e + 64],
                           w_kv[:, :, 128 * j + 64 * (1 - e):128 * j + 64 * (1 - e) + 64]) for j in range(2) for e in range(2)])
        s = slot(c0 + 2)
        load(c0 + 2, s, (grid(RAW[s], 8, 256), w_kv[:, :, 256:512]))
        c0 = BASE["swa"][0]
        with sp.Fori(0, 2) as i:
            for u in range(2):
                s = slot(c0 + u)
                load(c0 + u + 2 * i, s, (grid(RAW[s], 8, 256), rows(a["swa_w_q"][0])[:, :, ds(i * 512 + 256 * u, 256)]))
        load_tokens(BASE["wo1"][0], a["swa_w_o"][0])
        load_mlp(BASE["mlp1"][0], a["mlp_w_up"][1], a["mlp_w_down"][1])
        w = rows(a["w_in_2"][0])
        OFF = dict(mq=0, mk=D, mv=2 * D, mo=3 * D, gate_if=4 * D, dq=4 * D + 8, dk=5 * D + 8, dv=6 * D + 8,
                   rq=7 * D + 8, rk=8 * D + 8, rv=9 * D + 8, rg=10 * D + 8, gates=11 * D + 8)
        c0 = BASE["if"][0]
        load(c0, slot(c0), (grid(RAW[slot(c0)], 8, 256), w[:, :, OFF["gate_if"]:OFF["gate_if"] + 256]))

        def load_heads(c0, names):
            with sp.Fori(0, 4) as i:
                for j, name in enumerate(names):
                    s = slot(c0 + j)
                    load(c0 + j + 4 * i, s, (grid(RAW[s], 8, 256), w[:, :, ds(i * 256 + OFF[name], 256)]))

        def load_mix(c0, n, w_o):
            for h in range(2):
                for kh in range(2):
                    c = c0 + 4 * h + kh
                    at = OFF["gates"] + n * D + 512 * h
                    load(c, slot(c), (grid(RAW[slot(c)], 4, 512), w[:, 4 * kh:4 * kh + 4, at:at + 512]))
                for kh in range(2):
                    c = c0 + 4 * h + 2 + kh
                    load(c, slot(c), (grid(RAW[slot(c)], 4, 512), rows(w_o)[:, 4 * kh:4 * kh + 4, 512 * h:512 * h + 512]))

        load_heads(BASE["ml"][0], ("mq", "mk", "mv", "mo"))
        load_mix(BASE["mix0"][0], 0, a["w_mlstm_out_2"][0])
        load_heads(BASE["ret"][0], ("rq", "rk", "rv", "rg"))
        load_mix(BASE["mix1"][0], 2, a["w_ret_out_2"][0])
        load_tokens(BASE["dv"][0], a["w_in_2"][0][:, OFF["dv"]:OFF["dv"] + D])
        c0 = BASE["diff"][0]
        with sp.Fori(0, 4) as i:
            for u, name in enumerate(("dq", "dk")):
                s = slot(c0 + u)
                load(c0 + u + 2 * i, s, (grid(RAW[s], 8, 256), w[:, :, ds(i * 256 + OFF[name], 256)]))
        load_mix(BASE["mix2"][0], 1, a["w_diff_out_2"][0])
        load_tokens(BASE["wout"][0], a["w_out_2"][0])
        c0, w_up, w_down = BASE["ffn"][0], rows(a["w_ffn_in_2"][0]), rows(a["w_ffn_out_2"][0])

        def load_down(c0, k0, nk):
            for h in range(2):
                for kh in range(2):
                    c, n = c0 + 2 * h + kh, min(4, nk - 4 * kh)
                    load(c, slot(c), (grid(RAW[slot(c)], n, 512), w_down[:, k0 + 4 * kh:k0 + 4 * kh + n, 512 * h:512 * h + 512]))

        for n, tiles in enumerate((8, 8, 6)):
            c = c0 + 12 * n
            with sp.Fori(0, tiles // 2) as i:
                for u in range(2):
                    load(c + u + 2 * i, slot(c + u),
                         (grid(RAW[slot(c + u)], 8, 256), w_up[:, :, ds(i * 256 + (8 * n * P + FFN * u), 256)]))
            load_down(c + tiles, 8 * n, tiles)
        for t in range(T):
            sp.wait_ge(s_("fin_x"), t + 1)
            sp.dma_start(out[0, tok(t), :], X[:, t, :]).then_inc(s_("stored"), 16)
        sp.wait_ge(s_("stored"), 16 * T)

    @block.tensor
    def _(pe):
        def mm(dst, l, r, first, last):
            return nc.tensor.matmul(dst, l, r, start=first, stop=last)

        def mm3(dst, lh, ll, rh, rl, first, last):
            mm(dst, lh, rh, first, False)
            mm(dst, lh, rl, False, False)
            return mm(dst, ll, rh, False, last)

        def tokens(c, s, xh, xl, k0, nk, n, rnd, first=True, last=True, ready=None):
            pe.wait_ge(lo_ready, c + 1)
            wh, wl = grid(WH[s], nk, n), grid(WL[s], nk, n)
            for t in range(T):
                if first:
                    pe.wait_ge(a_free[t], rnd)
                for j in range(nk):
                    k = k0 + j
                    if ready and t == 0:
                        ready(k)
                    m = mm3(A[t][:, 0:n], xh[:, k, tok(t)], xl[:, k, tok(t)], wh[:, j, :], wl[:, j, :],
                            first and j == 0, last and j == nk - 1)
                if t == T - 1:
                    m.then_inc(chunk_done, 1)
                elif last:
                    m.then_inc(tok_done, 1)

        def tokens_full(c0, r0, xh, xl, ready=None):
            for h in range(2):
                for kh in range(2):
                    c = c0 + 2 * h + kh
                    tokens(c, slot(c), xh, xl, 4 * kh, 4, 512, r0 + h, kh == 0, kh == 1, None if h else ready)

        def features(c, s, xh, xl, use, use1=None, ready=None):
            pe.wait_ge(lo_ready, c + 1)
            wh, wl = grid(WH[s], KD, 256), grid(WL[s], KD, 256)
            for m in range(2):
                pe.wait_ge(b_free[m], use1 if m and use1 is not None else use)
                for k in range(KD):
                    if ready and m == 0:
                        ready(k)
                    r = mm3(B[m][:], wh[:, k, tok(m)], wl[:, k, tok(m)], xh[:, k, :], xl[:, k, :], k == 0, k == KD - 1)
                r.then_inc(feat_done if m == 0 else chunk_done, 1)

        def transposed(name, src):
            for k, (bank, free, n) in enumerate(banks_of(name)):
                pe.wait_ge(free, n)
                for t in range(T):
                    r = nc.tensor.transpose(bank[:, tok(t)], src[:, t, tok(k)], ident[:])
                r.then_inc(s_(name + "_t"), 1)

        def transposed_tiles(name, src, done):
            banks = banks_of(name)
            order = [(t, k) for t in range(T - 1) for k in range(KD - 1)] + [(t, KD - 1) for t in range(T - 1)]
            order += [(T - 1, k) for k in range(KD)]
            for t, k in order:
                bank, free, n = banks[k]
                if k == 0:
                    pe.wait_ge(*done(t))
                if t == 0 and n:
                    pe.wait_ge(free, n)
                r = nc.tensor.transpose(bank[:, tok(t)], src[:, t, tok(k)], ident[:])
                if t == T - 1:
                    r.then_inc(s_(name + "_t"), 1)

        def ready_of(name):
            banks = banks_of(name)

            def ready(k):
                _, free, n = banks[k]
                pe.wait_ge(free, n + 1)

            return ready

        pe.wait_ge(ident_in, 16)
        transposed_tiles("xt", X, lambda t: (x_in[t], 16))
        _, ra, rb, n0, _, _ = BASE["in"]
        for kh in range(2):
            tokens(kh, slot(kh), XH, XL, 4 * kh, 4, QR, ra, kh == 0, kh == 1, ready_of("xt"))
        for kh in range(2):
            c, s = 2 + kh, slot(2 + kh)
            pe.wait_ge(lo_ready, c + 1)
            wh, wl = grid(WH[s], 4, 512), grid(WL[s], 4, 512)
            for t in range(T):
                if kh == 0:
                    pe.wait_ge(a_free[t], ra + 1)
                for j in range(4):
                    k = 4 * kh + j
                    r = mm3(A[t][:, 0:KVR], XH[:, k, tok(t)], XL[:, k, tok(t)], wh[:, j, 0:KVR], wl[:, j, 0:KVR],
                            k == 0, k == 7)
                if kh == 1:
                    r.then_inc(s_("in_kv"), 1)
            for m in range(2):
                for j in range(4):
                    k, cols = 4 * kh + j, slice(256 + P * m, 384 + P * m)
                    r = mm3(B[m][:], wh[:, j, cols], wl[:, j, cols], XH[:, k, :], XL[:, k, :], k == 0, k == 7)
                if m == 1:
                    r.then_inc(chunk_done, 1)
                elif kh == 1:
                    r.then_inc(s_("in_kv"), 1)
        pe.wait_ge(rows_in, ROWS_N * 16)
        pe.wait_ge(consts_in, CONSTS_N * 16)
        for m in range(2):
            r = nc.tensor.transpose(C[n0 % 2][:, tok(m)], ROWS_T[:, m, :], ident[:])
        r.then_inc(s_("vec_t"), 1)
        mm(C[(n0 + 1) % 2][0:16, 0:3 * P], RELB, ONEHOT, True, True).then_inc(s_("vec_t"), 1)
        for k in range(5):
            u = n0 + 2 + k
            pe.wait_ge(c_free[u % 2], u // 2)
            for t in range(T):
                pe.wait_ge(a_free[t], ra + (1 if k < 3 else 2))
                r = nc.tensor.transpose(C[u % 2][:, tok(t)], C_N[:, t, tok(k)], ident[:])
            r.then_inc(s_("in_t"), 1)
        c_all_free(pe, n0 + 7)
        pe.wait_ge(masks_done, 1)
        pe.wait_ge(consts_done, 1)
        c0, ra, rb, n0, _, _ = BASE["pair"]
        pe.wait_ge(s_("kr_ready"), 1)
        with pe.Fori(0, 4) as i:
            c = c0 + 2 * i
            tokens(c, slot(c0), YH, YL, 3, 2, 256, ra + 3 * i)
            s = slot(c0 + 1)
            pe.wait_ge(lo_ready, c + 2)
            qh, ql = grid(WH[s], 3, 512), grid(WL[s], 3, 512)
            kh, kl = grid(WH[s], 2, 256, 1536), grid(WL[s], 2, 256, 1536)
            for u, (wh, wl, at, x0, nk) in enumerate((
                    (qh, ql, 0, 0, 3), (qh, ql, 128, 0, 3), (kh, kl, 0, 3, 2), (kh, kl, 128, 3, 2),
                    (qh, ql, 256, 0, 3), (qh, ql, 384, 0, 3))):
                b = u % 2
                pe.wait_ge(b_free[b], (rb + u) // 2 + 4 * i)
                for k in range(nk):
                    r = mm3(B[b][:], wh[:, k, at:at + P], wl[:, k, at:at + P], YH[:, x0 + k, :], YL[:, x0 + k, :], k == 0, k == nk - 1)
                r.then_inc(chunk_done if u == 5 else s_("pair_f"), 1)
            for b in range(2):
                pe.wait_ge(b_free[b], rb // 2 + 4 * i + 2)

            def without_position(h, q):
                n = (q + 1) * P
                pe.wait_ge(a_free[q], ra + 3 * i + 1 + h)
                mm(A[q][:, 0:n], M_QN[:, h, tok(q)], M_KN[:, h, 0:n], True, False)
                mm(A[q][:, n - P:n], identR[:], causalR[:], False, False)

            def with_position(h, q):
                n, rows = (q + 1) * P, slice(64 * h, 64 * h + 64)
                mm(A[q][:, 0:n], M_QR[rows, tok(q)], M_KR[rows, 0:n], False, True).then_inc(s_("pair_s"), 1)

            for q in range(T):
                without_position(0, q)
            pe.wait_ge(s_("qr_ready"), i + 1)
            for q in range(T):
                with_position(0, q)
            for q in range(T):
                without_position(1, q)
                with_position(1, q)
            for h in range(2):
                for q in range(T):
                    u = n0 + 4 * h + q
                    pe.wait_ge(c_free[u % 2], u // 2 + 4 * i)
                    pe.wait_ge(s_("pair_p"), 8 * i + 4 * h + q + 1)
                    for k in range(q + 1):
                        at = q * (q + 1) // 2 * P + k * P
                        r = nc.tensor.transpose(C[u % 2][:, tok(k)], M_P[:, h, at:at + P], ident[:])
                    r.then_inc(s_("pair_t"), 1)
                for b in range(2):
                    pe.wait_ge(c_free[b], (n0 + 4 * h + 4 + 1 - b) // 2 + 4 * i)
                pe.wait_ge(b_free[h], rb // 2 + 4 * i + 3)
                for k in range(T):
                    r = mm(B[h][:, k * P:S], M_V[:, k, tok(h)], M_PT[:, k, k * P:S], k == 0, k == T - 1)
                r.then_inc(s_("pair_o"), 1)

        def b_all_free(n):
            pe.wait_ge(b_free[0], (n + 1) // 2)
            pe.wait_ge(b_free[1], n // 2)

        b_all_free(BASE["wo0"][2])
        tokens_full(BASE["wo0"][0], BASE["wo0"][1], XH, XL)

        transposed_tiles("ln0", Y, lambda t: (s_("ln0_g"), t + 1))

        def mlp(name, before):
            c0, ra, rb, _, _, _ = BASE[name]
            with pe.Fori(0, 4) as i:
                c = c0 + 8 * i
                for j in range(4):
                    features(c + j, slot(c0 + j), XH, XL, rb // 2 + 4 * i + j, None, None if j else ready_of(before))
                for h in range(2):
                    for kh in range(2):
                        j = 4 + 2 * h + kh
                        pe.wait_ge(s_(name + "_y"), 8 * i + 4 * kh + 4)
                        tokens(c + j, slot(c0 + j), YH, YL, 4 * kh, 4, 512, ra + 2 * i + h, kh == 0, kh == 1)

        mlp("mlp0", "ln0")
        transposed_tiles("ln1", Y, lambda t: (s_("ln1_g"), t + 1))
        c0, ra, rb, _, _, _ = BASE["kv"]
        for u in range(2):
            features(c0 + u, slot(c0 + u), XH, XL, rb // 2 + u, None, None if u else ready_of("ln1"))
        tokens(c0 + 2, slot(c0 + 2), XH, XL, 0, 8, 256, ra)
        c0, ra, rb, n0, _, _ = BASE["swa"]
        for t in range(T):
            pe.wait_ge(a_free[t], BASE["kv"][1] + 1)
        with pe.Fori(0, 2) as i:
            for u in range(2):
                features(c0 + u + 2 * i, slot(c0 + u), XH, XL, rb // 2 + u + 2 * i)
        with pe.Fori(0, 2) as i:
            def block_scores(j):
                u, n, bank = j // T, j % T, 2 * (j % 2)
                w, k_at = (2 * P if n else P), max(n - 1, 0) * P
                if n == 0:
                    pe.wait_ge(s_("swa_k"), 2 * i + u + 1)
                for e in range(2):
                    pe.wait_ge(a_free[bank + e], ra + j // 2 + 4 * i)
                for q in range(2):
                    for e in range(2):
                        rows = slice(64 * e, 64 * e + 64)
                        r = mm(A[bank + e][:, 256 * q:256 * q + w], W_Q[rows, u, q, tok(n)], W_KG[rows, u, k_at:k_at + w], True, True)
                        if q == 1:
                            r.then_inc(s_("swa_s"), 1)

            block_scores(0)
            block_scores(1)
            for j in range(2 * T):
                u, n, z = j // T, j % T, j % 2
                pe.wait_ge(s_("swa_p"), 8 * i + j + 1)
                for kb in range(2):
                    pe.wait_ge(c_free[kb], (n0 + 1 - kb) // 2 + j + 8 * i)
                    todo = [(h, kb) for h in range(4)] if n else [(2 * kb, 0), (2 * kb + 1, 0)]
                    for x, (h, blk) in enumerate(todo):
                        r = nc.tensor.transpose(C[kb][:, tok(x)], W_S[:, z, h, blk * P:blk * P + P], ident[:])
                    r.then_inc(s_("swa_t"), 1)
                if j + 2 < 2 * T:
                    block_scores(j + 2)
                for kb in range(2):
                    pe.wait_ge(c_free[kb], (n0 + 1 - kb) // 2 + j + 1 + 8 * i)
                pe.wait_ge(b_free[z], rb // 2 + 4 + j // 2 + 4 * i)
                blocks = (0, 1) if n else (1,)
                for h in range(4):
                    for kb in blocks:
                        r = mm(B[z][:, 64 * h:64 * h + 64], W_PT[:, kb, tok(h)],
                               W_V[:, n - 1 + kb, ds(i * 128 + 64 * u, 64)], kb == blocks[0], kb == 1)
                r.then_inc(s_("swa_o"), 1)
        b_all_free(BASE["ot"][2])
        transposed("ot", Y)
        tokens_full(BASE["wo1"][0], BASE["wo1"][1], YH, YL, ready_of("ot"))
        transposed_tiles("ln2", Y, lambda t: (s_("ln2_g"), t + 1))
        mlp("mlp1", "ln2")
        transposed_tiles("pre", Y, lambda t: (s_("pre_n"), t + 1))
        c0, _, rb, n0, _, _ = BASE["if"]
        s = slot(c0)
        pe.wait_ge(lo_ready, c0 + 1)
        wh, wl = grid(WH[s], KD, 256), grid(WL[s], KD, 256)
        for m in range(2):
            pe.wait_ge(b_free[m], rb // 2)
            for k in range(KD):
                cols = slice(4 * m, 4 * m + P)
                if m == 0:
                    ready_of("pre")(k)
                r = mm3(B[m][:], wh[:, k, cols], wl[:, k, cols], XH[:, k, :], XL[:, k, :], k == 0, k == KD - 1)
            r.then_inc(feat_done if m == 0 else chunk_done, 1)
        features(BASE["ml"][0], slot(BASE["ml"][0]), XH, XL, BASE["ml"][2] // 2)
        for m, src in enumerate((G_U, G_EM)):
            b = (n0 + m) % 2
            pe.wait_ge(c_free[b], (n0 + m) // 2)
            pe.wait_ge(s_("if_g"), 1)
            for t in range(T):
                r = nc.tensor.transpose(C[b][:, tok(t)], src[:, tok(t)], ident[:])
            r.then_inc(s_("if_t"), 1)

        def head_transposed(name, i, n0, src):
            pe.wait_ge(s_(name + "_h"), T * i + T)
            for m in range(2):
                b = (n0 + m) % 2
                pe.wait_ge(c_free[b], (n0 + m) // 2 + i)
                for t in range(T):
                    r = nc.tensor.transpose(C[b][:, tok(t)], src[:, t, tok(m)], ident[:])
                r.then_inc(s_(name + "_t"), 1)

        def decayed_values(name, i, rounds, rb, at, v, width):
            for t in range(T):
                pe.wait_ge(a_free[t], rounds)
                b, u = t % 2, rb + 4 + t
                pe.wait_ge(b_free[b], u // 2 + 4 * i)
                for j in range(t + 1):
                    r = mm(B[b][:, 0:width], at[:, j, (t - j) * P:(t - j) * P + P], v[:, j, 0:width], j == 0, j == t)
                r.then_inc(s_(name + "_o"), 1)

        def scores(name, i, r, q, k):
            for j in range(T):
                n = S - j * P
                pe.wait_ge(a_free[j], r)
                for m in range(2):
                    x = mm(A[j][:, 0:n], k[:, m, tok(j)], q[:, m, j * P:S], m == 0, m == 1)
                x.then_inc(s_(name + "_s"), 1)

        def gate_chunk(name, h, kh):
            c0, ra, _, _, _, _ = BASE[name]
            c = c0 + 4 * h + kh
            tokens(c, slot(c), XH, XL, 4 * kh, 4, 512, ra + 2 * h, kh == 0, kh == 1)

        c0, ra, rb, n0, _, _ = BASE["ml"]

        def after_head(name, mix_name, i, ahead):
            c0, _, rb, n0, _, _ = BASE[name]
            if ahead:
                features(c0 + 4 * i + 4, slot(c0), XH, XL, rb // 2 + 4 * i + 4)
            else:
                gate_chunk(mix_name, 0, 0)
            head_transposed(name, i, n0, L_H)

        def mlstm_head(i, ahead):
            c = c0 + 4 * i
            features(c + 1, slot(c0 + 1), XH, XL, rb // 2 + 4 * i + 1)
            for j in range(2):
                tokens(c + 2 + j, slot(c0 + 2 + j), XH, XL, 0, KD, 256, ra + 4 * i + j)
            pe.wait_ge(s_("ml_m"), i + 1)
            for j in range(T):
                n = S - j * P
                pe.wait_ge(a_free[j], ra + 4 * i + 2)
                if n > P:
                    mm(A[j][:, P:n], ones[:], L_M[:, (j + 1) * P:S], True, True)
                mm(A[j][:, 0:P], ones[:], L_M[:, tok(j)], True, False)
                mm(A[j][:, 0:P], identR[:], futureR[:], False, True).then_inc(s_("ml_w"), 1)
            pe.wait_ge(s_("ml_qk"), 4 * i + 4)
            scores("ml", i, ra + 4 * i + 3, L_Q, L_K)
            decayed_values("ml", i, ra + 4 * i + 4, rb, L_A, L_V, 257)
            after_head("ml", "mix0", i, ahead)

        with pe.Fori(0, 3) as i:
            mlstm_head(i, True)
        mlstm_head(3, False)

        def mix(name, begun):
            c0, ra, _, n0, _, _ = BASE[name]
            for h in range(2):
                for kh in range(2):
                    if 2 * h + kh >= begun:
                        gate_chunk(name, h, kh)
                if h == 0:
                    c_all_free(pe, n0)
                for kh in range(2):
                    c = c0 + 4 * h + 2 + kh
                    tokens(c, slot(c), YH, YL, 4 * kh, 4, 512, ra + 2 * h + 1, kh == 0, kh == 1)

        mix("mix0", 1)
        c0, ra, rb, n0, _, _ = BASE["ret"]

        def retention_head(i, ahead):
            c = c0 + 4 * i
            features(c + 1, slot(c0 + 1), XH, XL, rb // 2 + 4 * i + 1)
            for j in range(2):
                tokens(c + 2 + j, slot(c0 + 2 + j), XH, XL, 0, KD, 256, ra + 3 * i + j)
            for b in range(2):
                pe.wait_ge(b_free[b], rb // 2 + 4 * i + 2)
            scores("ret", i, ra + 3 * i + 2, L_Q, L_K)
            decayed_values("ret", i, ra + 3 * i + 3, rb, L_A, L_V, 256)
            after_head("ret", "mix1", i, ahead)

        features(c0, slot(c0), XH, XL, rb // 2)
        with pe.Fori(0, 3) as i:
            retention_head(i, True)
        retention_head(3, False)
        mix("mix1", 1)
        tokens_full(BASE["dv"][0], BASE["dv"][1], XH, XL)
        c0, ra, rb, n0, _, _ = BASE["diff"]
        for t in range(T):
            pe.wait_ge(a_free[t], BASE["dv"][1] + 2)
        def diff_scores(i, h, q):
            n = (q + 1) * P
            if q == 0:
                pe.wait_ge(s_("diff_b"), 2 * i + h + 1)
            for e in range(2):
                u, rows = 2 * q + e, slice(64 * e, 64 * e + 64)
                pe.wait_ge(a_free[u % 4], ra + 2 * h + u // 4 + 4 * i)
                mm(A[u % 4][:, 0:n], identR[:], slopes[:, h, S - n:S], True, False)
                mm(A[u % 4][:, 0:n], F_Q[rows, h, tok(q)], F_K[rows, h, 0:n], False, True).then_inc(s_("diff_s"), 1)

        def diff_weights(i, h, q):
            u = n0 + 5 * h + q
            pe.wait_ge(c_free[u % 2], u // 2 + 5 * i)
            pe.wait_ge(s_("diff_p"), 8 * i + 4 * h + q + 1)
            for k in range(q + 1):
                r = nc.tensor.transpose(C[u % 2][:, tok(k)], F_A[:, q % 2, tok(k)], ident[:])
            r.then_inc(s_("diff_t"), 1)

        def diff_use(i, h):
            next_heads = 2 if h and not isinstance(i, int) else 0
            return rb // 2 + 2 + 3 * i + next_heads

        def diff_values(i, h):
            for b in range(2):
                pe.wait_ge(c_free[b], (n0 + 5 * h + 4 + 1 - b) // 2 + 5 * i)
            pe.wait_ge(b_free[h], diff_use(i, h))
            for q in range(T):
                for k in range(q + 1):
                    r = mm(B[h][:, tok(q)], F_PT[:, k, tok(q)], F_V[:, k, ds(i * 256 + P * h, P)], k == 0, k == q)
            r.then_inc(s_("diff_o"), 1)

        def diff_by_feature(i, h):
            u = n0 + 5 * h + 4
            pe.wait_ge(b_free[h], diff_use(i, h) + 1)
            pe.wait_ge(c_free[u % 2], u // 2 + 5 * i)
            for t in range(T):
                r = nc.tensor.transpose(C[u % 2][:, tok(t)], F_H[:, tok(t)], ident[:])
            r.then_inc(s_("diff_ht"), 1)

        def diff_pair(i, ahead):
            for q in (0, 1):
                diff_weights(i, 0, q)
                diff_scores(i, 1, q)
            for q in (2, 3):
                diff_weights(i, 0, q)
            diff_scores(i, 1, 2)
            diff_values(i, 0)
            diff_scores(i, 1, 3)
            if ahead:
                features(c0 + 2 + 2 * i, slot(c0), XH, XL, rb // 2 + 3 + 3 * i, rb // 2 + 2 + 3 * i)
            else:
                gate_chunk("mix2", 0, 0)
            diff_by_feature(i, 0)
            for q in (0, 1):
                diff_weights(i, 1, q)
            if ahead:
                features(c0 + 3 + 2 * i, slot(c0 + 1), XH, XL, rb // 2 + 4 + 3 * i, rb // 2 + 3 + 3 * i)
            for q in (2, 3):
                diff_weights(i, 1, q)
                if ahead:
                    for b in range(2):
                        pe.wait_ge(b_free[b], rb // 2 + 5 - b + 3 * i)
                    diff_scores(i + 1, 0, q - 2)
            if ahead:
                diff_scores(i + 1, 0, 2)
            diff_values(i, 1)
            if ahead:
                diff_scores(i + 1, 0, 3)
            else:
                gate_chunk("mix2", 0, 1)
            diff_by_feature(i, 1)

        for j in range(2):
            features(c0 + j, slot(c0 + j), XH, XL, rb // 2 + j)
        for b in range(2):
            pe.wait_ge(b_free[b], rb // 2 + 2)
        for q in range(T):
            diff_scores(0, 0, q)
        with pe.Fori(0, 3) as i:
            diff_pair(i, True)
        diff_pair(3, False)
        mix("mix2", 2)
        pe.wait_ge(s_("mixed"), 16)
        transposed("yt", Y)
        tokens_full(BASE["wout"][0], BASE["wout"][1], XH, XL, ready_of("yt"))
        transposed_tiles("post", Y, lambda t: (s_("post_n"), t + 1))
        c, ra, rb, _, _, _ = BASE["ffn"]
        use, done = rb // 2, 0
        for n, tiles in enumerate((8, 8, 6)):
            with pe.Fori(0, tiles // 2) as i:
                for j in range(2):
                    features(c + j + 2 * i, slot(c + j), XH, XL, use + j + 2 * i, None, None if n or j else ready_of("post"))
            c, use, done = c + tiles, use + tiles, done + tiles
            for h in range(2):
                for kh in range(2):
                    nk = min(4, tiles - 4 * kh)
                    pe.wait_ge(s_("ffn_y"), done - tiles + 4 * kh + nk)
                    tokens(c, slot(c), YH, YL, 4 * kh, nk, 512, ra + 2 * n + h, kh == 0, kh == 1)
                    c += 1

    @block.scalar
    def _(act):
        def split(c, per=0, i=0, more=None):
            if c >= CHUNKS:
                return
            s = slot(c)
            act.wait_ge(raw_in[s], 16 * (c // 2 + 1) + i * (16 * (per // 2)))
            if more is not None:
                act.wait_ge(raw_more[s], more)
            if c >= 2:
                act.wait_ge(chunk_done, c - 1 + i * per)
            n = 4 * QR if c < 2 else CH
            nc.scalar.activation(WH[s][:, 0:n], RAW[s][:, 0:n], ACT.Copy).then_inc(hi_ready, 1)

        def copy(dst, src, scale=1.0):
            return nc.scalar.activation(dst, src, ACT.Copy, scale=scale)

        def hi_transposed(name, dst, g=None, b=None):
            for k, (bank, _, _) in enumerate(banks_of(name)):
                act.wait_ge(s_(name + "_t"), k + 1)
                if b is not None:
                    x = nc.scalar.activation(dst[:, k, :], bank[:], ACT.Identity, bias=vec[:, b + k:b + k + 1])
                else:
                    x = copy(dst[:, k, :], bank[:], 1.0 if g is None else vec[:, g + k:g + k + 1])
                x.then_inc(s_(name + "_hi"), 1)

        act.wait_ge(ident_in, 16)
        copy(identR[:], ident[:]).then_inc(masks_done, 1)
        split(0)
        hi_transposed("xt", XH)
        split(1)
        split(2, more=16 * 6)

        act.wait_ge(s_("st_zero"), 1)

        def latents(n, wait, at, width):
            for t in range(T):
                wait(t)
                nc.scalar.activation(C_N[:, t, at:at + width], A[t][:, 0:width], ACT.Square, scale=width ** -0.5,
                                     accum_out=stat(SS + 4 * n + t)).then_inc(s_("in_ss"), 1)
            for t in range(T):
                act.wait_ge(s_("in_r"), 4 * n + t + 1)
                nc.scalar.activation(C_N[:, t, at:at + width], A[t][:, 0:width], ACT.Copy,
                                     scale=stat(RS + 4 * n + t)).then_inc(a_free[t], 1)

        latents(0, lambda t: wait_tok(act, t, 0, 1), 0, QR)
        split(3, more=16 * 6)
        split(4)
        act.wait_ge(s_("lam_dot"), 1)
        nc.scalar.activation(stat(LAM, 2), stat(LAM, 2), ACT.Exp).then_inc(s_("lam_exp"), 1)
        latents(1, lambda t: act.wait_ge(s_("in_kv"), t + 1), QR, KVR)
        act.wait_ge(consts_done, 1)
        for k in range(5):
            act.wait_ge(s_("in_t"), k + 1)
            g = (GQ + k) if k < 3 else (GKV + k - 3)
            nc.scalar.activation(YH[:, k, :], C[(BASE["in"][3] + 2 + k) % 2][:], ACT.Copy,
                                 scale=vec[:, g:g + 1]).then_inc(s_("in_hi"), 1)
        c0, ra, rb, n0, g0, _ = BASE["pair"]
        def pair(i, ahead):
            for t in range(T):
                if t < 3:
                    act.wait_ge(tok_done, 3 * g0 + t + 1 + i * 3)
                else:
                    act.wait_ge(chunk_done, c0 + 1 + i * 2)
                copy(M_V[:, t, :], A[t][:, 0:256]).then_inc(a_free[t], 1)
            split(c0 + 2, 2, i)
            act.wait_ge(s_("pair_f"), 5 * i + 1)
            copy(M_QN[:, 0, :], B[0][:]).then_inc(b_free[0], 1)
            act.wait_ge(s_("pair_f"), 5 * i + 3)
            copy(M_KN[:, 0, :], B[0][:], MLA_SCALE).then_inc(b_free[0], 1)
            for h in range(2):
                for q in range(T):
                    n, at = (q + 1) * P, q * (q + 1) // 2 * P
                    act.wait_ge(s_("pair_m"), 8 * i + 4 * h + q + 1)
                    nc.scalar.activation(M_P[:, h, at:at + n], A[q][:, 0:n], ACT.Exp, bias=stat(NM + 4 * h + q),
                                         accum_out=stat(SUM + 4 * h + q)).then_inc(a_free[q], 1)
            for h in range(2):
                for q in range(T):
                    u = (n0 + 4 * h + q) % 2
                    act.wait_ge(s_("pair_t"), 8 * i + 4 * h + q + 1)
                    copy(M_PT[:, 0:q + 1, tok(q)], C[u][:, 0:(q + 1) * P].rearrange("p (k n) -> p k n", n=P)).then_inc(c_free[u], 1)
                if h == 0 and ahead:
                    split(c0 + 3, 2, i, more=16 * 6 + 256 + i * 128)
                elif h == 0:
                    split(BASE["wo0"][0] + 1)
                act.wait_ge(s_("pair_o"), 2 * i + h + 1)
                copy(XH[:, ds(i * 2 + h, 1), :].rearrange("p a n -> p (a n)"), B[h][:]).then_inc(s_("pair_hi"), 1)

        split(c0 + 1, more=16 * 6 + 128)
        with act.Fori(0, 3) as i:
            pair(i, True)
        pair(3, False)

        def splits(c0, n):
            for c in range(c0, c0 + n):
                split(c + 1)

        def normalize(name, t):
            act.wait_ge(s_(name + "_r"), t + 1)
            nc.scalar.activation(Y[:, t, :], Y[:, t, :], ACT.Identity, scale=stat(RS + t),
                                 bias=stat(NMR + t)).then_inc(s_(name + "_n"), 1)

        splits(BASE["wo0"][0] + 1, 3)
        for t in range(T):
            normalize("ln0", t)
        hi_transposed("ln0", XH, b=ln_b(0))

        def mlp(name):
            c0, _, _, _, _, f0 = BASE[name]
            with act.Fori(0, 4) as i:
                for j in range(4):
                    split(c0 + j + 1, 8, i)
                    for m in range(2):
                        if m == 0:
                            act.wait_ge(feat_done, f0 + j + 1 + i * 4)
                        else:
                            act.wait_ge(chunk_done, c0 + j + 1 + i * 8)
                        nc.scalar.activation(R_T[:, m, :], B[m][:], ACT.Relu).then_inc(b_free[m], 1)
                        act.wait_ge(s_(name + "_sq"), 8 * i + 2 * j + m + 1)
                        copy(YH[:, 2 * j + m, :], SQ_T[:, m, :]).then_inc(s_(name + "_hi"), 1)
                for j in range(4, 8):
                    split(c0 + j + 1, 8, i)

        mlp("mlp0")
        for t in range(T):
            normalize("ln1", t)
        hi_transposed("ln1", XH, b=ln_b(1))
        c0, _, _, _, g0, f0 = BASE["kv"]
        for u in range(2):
            split(c0 + u + 1, more=16 * 6 + 512 + 48 if u == 0 else None)
            wait_feat(act, 0, f0 + u, c0 + u)
            copy(W_K[u][:, 0, :], B[0][:]).then_inc(b_free[0], 1)
        split(c0 + 3)
        for t in range(T):
            wait_tok(act, t, g0, c0 + 2)
            copy(W_V[:, t, :], A[t][:, 0:256]).then_inc(a_free[t], 1)
        c0, ra, rb, n0, _, f0 = BASE["swa"]
        act.wait_ge(s_("ln1_x"), T)
        with act.Fori(0, 2) as i:
            for u in range(2):
                split(c0 + u + 1, 2, i)
                act.wait_ge(feat_done, f0 + u + 1 + i * 2)
                copy(Y[:, 0:2, ds(i * 512 + 256 * u, 256)], B[0][:].rearrange("p (a n) -> p a n", a=2),
                     SWA_DH ** -0.5).then_inc(b_free[0], 1)
        with act.Fori(0, 2) as i:
            def block_exp(j):
                w, z = (2 * P if j % T else P), j % 2
                act.wait_ge(s_("swa_m"), 8 * i + j + 1)
                for h in range(4):
                    nc.scalar.activation(W_S[:, z, h, 0:w], W_S[:, z, h, 0:w], ACT.Exp, bias=stat(W_NEG + 4 * z + h),
                                         accum_out=stat(W_SUM + 4 * z + h))
                nc.scalar.activation(stat(W_ES + 4 * z, 4), stat(W_ES + 4 * z, 4), ACT.Exp).then_inc(s_("swa_p"), 1)

            block_exp(0)
            for j in range(2 * T):
                act.wait_ge(s_("swa_t"), 16 * i + 2 * j + 1)
                dst = W_PT[:, 0, :] if j % T else W_PT[:, 1, 0:256]
                copy(dst, C[0][:, 0:512 if j % T else 256]).then_inc(c_free[0], 1)
                if j + 1 < 2 * T:
                    block_exp(j + 1)
        hi_transposed("ot", YH)
        splits(BASE["wo1"][0], 4)
        for t in range(T):
            normalize("ln2", t)
        hi_transposed("ln2", XH, b=ln_b(2))
        mlp("mlp1")

        def mean_square(name, t):
            act.wait_ge(s_(name + "_x"), t + 1)
            nc.scalar.activation(Y[:, t, :], X[:, t, :], ACT.Square, scale=D ** -0.5,
                                 accum_out=stat(H_SS + t)).then_inc(s_(name + "_ss"), 1)

        def over_root(name, t):
            act.wait_ge(s_(name + "_r"), t + 1)
            copy(Y[:, t, :], X[:, t, :], stat(H_R + t)).then_inc(s_(name + "_n"), 1)

        def then_rms(name, first):
            for t in range(T + 2):
                if t < T:
                    first(t)
                if 1 <= t <= T:
                    mean_square(name, t - 1)
                if t >= 2:
                    over_root(name, t - 2)

        then_rms("pre", lambda t: normalize("ln3", t))
        hi_transposed("pre", XH, g=NG0)
        split(BASE["if"][0] + 1)
        act.wait_ge(s_("if_abs"), 1)
        nc.scalar.activation(G_L, G_T, ACT.Exp, scale=-1.0).then_inc(s_("if_e"), 1)
        split(BASE["ml"][0] + 1)
        act.wait_ge(s_("if_e"), 1)
        nc.scalar.activation(G_L, G_L, ACT.Ln, bias=1.0).then_inc(s_("if_l"), 1)
        c0, ra, rb, n0, g0, f0 = BASE["ml"]

        def head_rms(name, i, inv):
            for t in range(T):
                if inv:
                    act.wait_ge(s_(name + "_d"), T * i + t + 1)
                    nc.scalar.activation(L_H[:, t, :], B[t % 2][:, 0:256], ACT.Copy, scale=stat(H_INV + t)).then_inc(b_free[t % 2], 1)
                else:
                    act.wait_ge(s_(name + "_o"), T * i + t + 1)
                    copy(L_H[:, t, :], B[t % 2][:, 0:256]).then_inc(b_free[t % 2], 1)
                u = BASE[name][2] + 4 + t
                act.wait_ge(b_free[t % 2], u // 2 + 1 + i * 4)
                nc.scalar.activation(xtmp[:, t // 2, 256 * (t % 2):256 * (t % 2) + 256], L_H[:, t, :], ACT.Square, scale=256 ** -0.5,
                                     accum_out=stat(H_SS + t)).then_inc(s_(name + "_ss"), 1)

        def head_hi(name, i, n0):
            for m in range(2):
                act.wait_ge(s_(name + "_t"), 2 * i + m + 1)
                copy(YH[:, ds(i * 2 + m, 1), :].rearrange("p a n -> p (a n)"), C[(n0 + m) % 2][:]).then_inc(s_(name + "_hi"), 1)

        def head_tokens(name, i, j, gi, dst, func):
            for t in range(T):
                if t < 3:
                    act.wait_ge(tok_done, 3 * (g0 + gi) + t + 1 + i * 6)
                else:
                    act.wait_ge(chunk_done, c0 + j + 1 + i * 4)
                nc.scalar.activation(dst[:, t, 0:256], A[t][:, 0:256], func).then_inc(a_free[t], 1)

        act.wait_ge(s_("ml_zero"), 1)

        def before_conv(i, j):
            for m in range(2):
                if m == 0:
                    act.wait_ge(feat_done, f0 + j + 1 + i * 2)
                else:
                    act.wait_ge(chunk_done, c0 + j + 1 + i * 4)
                copy(L_PRE[:, m, 3:3 + S], B[m][:]).then_inc(b_free[m], 1)

        def after_conv(i, j):
            for m in range(2):
                act.wait_ge(s_("ml_conv"), 4 * i + 2 * j + m + 1)
                nc.scalar.activation((L_Q, L_K)[j][:, m, :], L_ACC, ACT.Silu).then_inc(s_("ml_qk"), 1)

        def mlstm_head(i, ahead):
            before_conv(i, 1)
            split(c0 + 3, 4, i)
            head_tokens("ml", i, 2, 0, L_V, ACT.Copy)
            after_conv(i, 1)
            split(c0 + 4, 4, i)
            head_tokens("ml", i, 3, 1, L_O, ACT.Sigmoid)
            for j in range(T):
                n = S - j * P
                act.wait_ge(s_("ml_w"), T * i + j + 1)
                nc.scalar.activation(L_A[:, j, 0:n], A[j][:, 0:n], ACT.Exp, scale=-1.0,
                                     bias=st[:, ds(i + (U_COL + 4 * j), 1)]).then_inc(a_free[j], 1)
            split(c0 + 5, 4, i)
            head_rms("ml", i, True)
            if ahead:
                before_conv(i + 1, 0)
            split(c0 + 6, 4, i)
            if ahead:
                after_conv(i + 1, 0)
            head_hi("ml", i, n0)

        act.wait_ge(s_("if_m"), 1)
        nc.scalar.activation(G_EM, G_EM, ACT.Exp, scale=-1.0).then_inc(s_("if_g"), 1)
        before_conv(0, 0)
        split(c0 + 2)
        after_conv(0, 0)
        with act.Fori(0, 3) as i:
            mlstm_head(i, True)
        mlstm_head(3, False)

        def mix(name, split_to):
            c0, _, _, _, g0, _ = BASE[name]
            for h in range(2):
                for kh in range(4):
                    j = 4 * h + kh
                    if j + 1 > split_to:
                        split(c0 + j + 1)
                    if kh == 1:
                        for t in range(T):
                            wait_tok(act, t, g0 + 2 * h, c0 + j)
                            nc.scalar.activation(GATE[:, t, :], A[t][:], ACT.Sigmoid).then_inc(a_free[t], 1)

        mix("mix0", 2)
        c0, ra, rb, n0, g0, f0 = BASE["ret"]

        def retention_part(i, j):
            act.wait_ge(feat_done, f0 + j + 1 + i * 2)
            copy((L_Q, L_K)[j][:, 0, :], B[0][:]).then_inc(b_free[0], 1)

        def retention_head(i, ahead):
            retention_part(i, 1)
            split(c0 + 3, 4, i)
            head_tokens("ret", i, 2, 0, L_V, ACT.Copy)
            split(c0 + 4, 4, i)
            head_tokens("ret", i, 3, 1, L_O, ACT.Silu)
            split(c0 + 5, 4, i)
            head_rms("ret", i, False)
            if ahead:
                retention_part(i + 1, 0)
            split(c0 + 6, 4, i)
            head_hi("ret", i, n0)

        split(c0 + 1)
        retention_part(0, 0)
        split(c0 + 2)
        with act.Fori(0, 3) as i:
            retention_head(i, True)
        retention_head(3, False)
        mix("mix1", 2)
        c0, _, _, _, g0, _ = BASE["dv"]
        for h in range(2):
            split(c0 + 2 * h + 1)
            split(c0 + 2 * h + 2)
            for t in range(T):
                wait_tok(act, t, g0 + h, c0 + 2 * h + 1)
                copy(F_V[:, t, 512 * h:512 * h + 512], A[t][:]).then_inc(a_free[t], 1)
        c0, ra, rb, n0, _, f0 = BASE["diff"]

        def diff_exp(i, h, q):
            n = (q + 1) * P
            if h or q >= 2:
                act.wait_ge(s_("diff_p"), 8 * i + 4 * h + q - 1)
            for e in range(2):
                u = 2 * q + e
                act.wait_ge(s_("diff_m"), 16 * i + 8 * h + u + 1)
                nc.scalar.activation(F_P[q % 2][:, e, 0:n], A[u % 4][:, 0:n], ACT.Exp, bias=stat(NM + u),
                                     accum_out=stat(SUM + u)).then_inc(a_free[u % 4], 1)

        def diff_weights(i, h, q):
            u = (n0 + 5 * h + q) % 2
            act.wait_ge(s_("diff_t"), 8 * i + 4 * h + q + 1)
            copy(F_PT[:, 0:q + 1, tok(q)], C[u][:, 0:(q + 1) * P].rearrange("p (k n) -> p k n", n=P)).then_inc(c_free[u], 1)

        def diff_squares(i, h):
            act.wait_ge(s_("diff_o"), 2 * i + h + 1)
            for q in range(T):
                x = nc.scalar.activation(F_H[:, tok(q)], B[h][:, tok(q)], ACT.Square, scale=128 ** -0.5,
                                         accum_out=stat(H_SS + q))
            x.then_inc(s_("diff_ss"), 1)

        def diff_hi(i, h):
            act.wait_ge(s_("diff_ht"), 2 * i + h + 1)
            u = (n0 + 5 * h + 4) % 2
            y = YH[:, ds(i * 2 + h, 1), :].rearrange("p a n -> p (a n)")
            nc.scalar.activation(y, C[u][:], ACT.Copy, scale=vec[:, SUBLN:SUBLN + 1]).then_inc(s_("diff_hi"), 1)

        def diff_features(i, j):
            act.wait_ge(feat_done, f0 + j + 1 + i * 2)
            copy((F_Q, F_K)[j][:, 0, :], B[0][:], DIFF_SCALE if j == 0 else 1.0).then_inc(b_free[0], 1)

        def diff_pair(i, ahead):
            for q in range(T):
                if q:
                    diff_exp(i, (q + 2) // T, (q + 2) % T)
                diff_weights(i, 0, q)
            diff_exp(i, 1, 2)
            diff_squares(i, 0)
            diff_exp(i, 1, 3)
            if ahead:
                split(c0 + 3, 2, i)
                diff_features(i + 1, 0)
            else:
                split(BASE["mix2"][0] + 1)
            diff_hi(i, 0)
            for q in (0, 1):
                diff_weights(i, 1, q)
            if ahead:
                split(c0 + 4, 2, i)
                diff_features(i + 1, 1)
            for q in (2, 3):
                diff_weights(i, 1, q)
                if ahead:
                    diff_exp(i + 1, 0, q - 2)
            if not ahead:
                split(BASE["mix2"][0] + 2)
            diff_squares(i, 1)
            if ahead:
                diff_exp(i + 1, 0, 2)
            diff_hi(i, 1)

        for j in range(2):
            split(c0 + j + 1)
            diff_features(0, j)
        for q in (0, 1, 2):
            diff_exp(0, 0, q)
        with act.Fori(0, 3) as i:
            diff_pair(i, True)
        diff_pair(3, False)
        mix("mix2", 2)
        hi_transposed("yt", XH)
        c0, ra, _, _, g0, _ = BASE["wout"]

        def product_out(h, t):
            wait_tok(act, t, g0 + h, c0 + 2 * h + 1)
            nc.scalar.activation(SQUARES[:, t, 512 * h:512 * h + 512], A[t][:], ACT.Square, scale=D ** -0.5,
                                 accum_out=stat(SS + 4 * h + t))
            copy(Y[:, t, 512 * h:512 * h + 512], A[t][:]).then_inc(a_free[t], 1)

        for h in range(2):
            split(c0 + 2 * h + 1)
            split(c0 + 2 * h + 2)
            if h == 0:
                for t in range(T):
                    product_out(0, t)
        then_rms("post", lambda t: product_out(1, t))
        hi_transposed("post", XH, g=NG2)
        c, ra, rb, _, _, f0 = BASE["ffn"]
        use = rb // 2
        for n, tiles in enumerate((8, 8, 6)):
            with act.Fori(0, tiles // 2) as i:
                split(c + 1, 2, i)
                for m in range(2):
                    if m == 0:
                        act.wait_ge(feat_done, f0 + 1 + i * 2)
                    else:
                        act.wait_ge(chunk_done, c + 1 + i * 2)
                    nc.scalar.activation(SILU_T[:, m, :], B[m][:], ACT.Silu).then_inc(b_free[m], 1)
                split(c + 2, 2, i)
                for m in range(2):
                    act.wait_ge(b_free[m], use + 2 + i * 2)
                    copy(YH[:, ds(i * 2 + m, 1), :].rearrange("p a n -> p (a n)"), PROD_T[:, m, :]).then_inc(s_("ffn_hi"), 1)
            c, f0, use = c + tiles, f0 + tiles, use + tiles
            for j in range(4):
                split(c + 1)
                c += 1
        for h in range(2):
            for t in range(T):
                act.wait_ge(a_free[t], ra + 5 + h)
                nc.scalar.activation(SQUARES[:, t, 512 * h:512 * h + 512], Y[:, t, 512 * h:512 * h + 512], ACT.Square,
                                     scale=D ** -0.5, accum_out=stat(SS + 4 * h + t)).then_inc(s_("fin_ss"), 1)

    @block.vector
    def _(dve):
        step = Tally(dve_step)
        tt, stt, ts = nc.vector.tensor_tensor, nc.vector.scalar_tensor_tensor, nc.vector.tensor_scalar

        def then(x):
            step.then(dve, x)

        def split(c, per=0, i=0):
            if c >= CHUNKS:
                return
            s = slot(c)
            dve.wait_ge(hi_ready, c + 1 + i * per)
            n = 4 * QR if c < 2 else CH
            tt(WL[s][:, 0:n], RAW[s][:, 0:n], f32(WH[s][:, 0:n]), ALU.subtract).then_inc(lo_ready, 1)

        def lo_transposed(name, hi, lo, g=None, b=None):
            for k, (bank, free, _) in enumerate(banks_of(name)):
                dve.wait_ge(s_(name + "_hi"), k + 1)
                if g is None and b is None:
                    x = tt(lo[:, k, :], bank[:], f32(hi[:, k, :]), ALU.subtract)
                else:
                    at, op = (g, ALU.mult) if b is None else (b, ALU.add)
                    x = stt(lo[:, k, :], bank[:], vec[:, at + k:at + k + 1], f32(hi[:, k, :]), op, ALU.subtract)
                x.then_inc(free, 1)

        nc.vector.memset(ROWS_T, 0.0).then_inc(rows_zero, 1)
        nc.vector.memset(ones[:], 1.0)
        split(0)
        lo_transposed("xt", XH, XL)
        split(1)
        split(2)
        split(3)
        split(4)
        dve.wait_ge(consts_in, CONSTS_N * 16)
        nc.vector.tensor_copy(causalR[:], CAUSAL_T)
        nc.vector.tensor_copy(futureR[:], FUTURE_T)
        for g in range(SWA_KV):
            ts(stat(NEGSINK + 4 * g, 4).rearrange("p (e q) -> p e q", e=2),
               SINK_T[:, 4 * g:4 * g + 4].rearrange("p (q e) -> p e q", e=2), -1.0, None, ALU.mult)
        then(tt(LAMP_T, LAMB_T.rearrange("p (a b) n -> p a b n", b=2)[:, :, 0, :],
                LAMB_T.rearrange("p (a b) n -> p a b n", b=2)[:, :, 1, :], ALU.mult))
        nc.vector.tensor_reduce(stat(LAM, 2), LAMP_T, AX.X, ALU.add).then_inc(s_("lam_dot"), 1)
        dve.wait_ge(s_("lam_exp"), 1)
        then(tt(stat(LAM + 2), stat(LAM + 1), stat(LAM), ALU.subtract))
        then(ts(stat(LAM + 2), stat(LAM + 2), -LAM_INIT, None, ALU.add))
        _, _, rb, n0, _, _ = BASE["in"]
        for m, table in enumerate((cosT, sinT)):
            if m == 0:
                dve.wait_ge(s_("in_kv"), 5)
            else:
                dve.wait_ge(chunk_done, 4)
            x = stt(M_T[:, m, :], B[m][:], MLA_SCALE, table, ALU.mult, ALU.mult)
            x.then_inc(b_free[m], 1)
        for m in range(2):
            dve.wait_ge(b_free[m], rb // 2 + 1)
        tt(M_KR, M_T[:, 0, :], M_T[:, 1, :], ALU.add).then_inc(s_("kr_ready"), 1)
        dve.wait_ge(s_("vec_t"), 2)
        then(nc.vector.tensor_copy(vec[:, 0:CONV], C[n0 % 2][:, 0:CONV]))
        nc.vector.tensor_copy(vec[:, CONV:CONV + 64], C[n0 % 2][:, P:P + 64]).then_inc(c_free[n0 % 2], 1)
        tt(HEADS_T, C[(n0 + 1) % 2][0:16, 0:3 * P], WINDOW_T, ALU.add).then_inc(c_free[(n0 + 1) % 2], 1)
        ts(vec[:, SUBLN:SUBLN + 1], vec[:, SUBLN:SUBLN + 1], 1.0 - LAM_INIT, None, ALU.mult).then_inc(consts_done, 1)
        for k in range(5):
            u = (n0 + 2 + k) % 2
            g = (GQ + k) if k < 3 else (GKV + k - 3)
            dve.wait_ge(s_("in_hi"), k + 1)
            stt(YL[:, k, :], C[u][:], vec[:, g:g + 1], f32(YH[:, k, :]), ALU.mult, ALU.subtract).then_inc(c_free[u], 1)
        c0, ra, rb, n0, _, _ = BASE["pair"]
        def pair(i, ahead):
            split(c0 + 2, 2, i)
            dve.wait_ge(s_("pair_f"), 5 * i + 2)
            nc.vector.tensor_copy(M_QN[:, 1, :], B[1][:]).then_inc(b_free[1], 1)
            dve.wait_ge(s_("pair_f"), 5 * i + 4)
            ts(M_KN[:, 1, :], B[1][:], MLA_SCALE, None, ALU.mult).then_inc(b_free[1], 1)
            dve.wait_ge(s_("pair_f"), 5 * i + 5)
            tt(M_T[:, 0, :], B[0][:], cosT, ALU.mult).then_inc(b_free[0], 1)
            dve.wait_ge(chunk_done, c0 + 2 + 2 * i)
            tt(M_T[:, 1, :], B[1][:], sinT, ALU.mult).then_inc(b_free[1], 1)
            for m in range(2):
                dve.wait_ge(b_free[m], rb // 2 + 3 + 4 * i)
            tt(M_QR, M_T[:, 0, :], M_T[:, 1, :], ALU.add).then_inc(s_("qr_ready"), 1)

            def row_max(h, q):
                dve.wait_ge(s_("pair_s"), 8 * i + 4 * h + q + 1)
                nc.vector.tensor_reduce(stat(NM + 4 * h + q), A[q][:, 0:(q + 1) * P], AX.X, ALU.max,
                                        negate=True).then_inc(s_("pair_m"), 1)

            def normalized(h, q):
                n, at = (q + 1) * P, q * (q + 1) // 2 * P
                dve.wait_ge(a_free[q], ra + 2 + h + 3 * i)
                then(nc.vector.reciprocal(stat(RINV + 4 * h + q), stat(SUM + 4 * h + q)))
                ts(M_P[:, h, at:at + n], M_P[:, h, at:at + n], stat(RINV + 4 * h + q), None, ALU.mult).then_inc(s_("pair_p"), 1)

            for q in range(T):
                row_max(0, q)
            for q in range(T):
                normalized(0, q)
                row_max(1, q)
            for q in range(T):
                normalized(1, q)
            if ahead:
                split(c0 + 3, 2, i)
            else:
                split(BASE["wo0"][0] + 1)
            for h in range(2):
                dve.wait_ge(s_("pair_hi"), 2 * i + h + 1)
                tt(XL[:, ds(i * 2 + h, 1), :].rearrange("p a n -> p (a n)"), B[h][:],
                   f32(XH[:, ds(i * 2 + h, 1), :]).rearrange("p a n -> p (a n)"), ALU.subtract).then_inc(b_free[h], 1)

        split(c0 + 1)
        with dve.Fori(0, 3) as i:
            step.enter(i, 8)
            pair(i, True)
        step.leave(3)
        pair(3, False)

        def half_moments(t, h):
            return nc.vector.bn_stats(stat(ST6 + 12 * t + 6 * h, 6), Y[:, t, 512 * h:512 * h + 512])

        def moments(ln, t):
            then(half_moments(t, 1))
            nc.vector.bn_aggr(stat(MV + 2 * t, 2), stat(ST6 + 12 * t, 12)).then_inc(s_(ln + "_st"), 1)

        def gain(ln, n, t):
            dve.wait_ge(s_(ln + "_n"), t + 1)
            if t == 0:
                dve.wait_ge(gb_in, 32 * n + 32)
            x = tt(Y[:, t, :], Y[:, t, :], GB[:, 0, :], ALU.mult)
            if n < 3:
                x.then_inc(s_(ln + "_g"), 1)
            else:
                then(x)
                tt(X[:, t, :], Y[:, t, :], GB[:, 1, :], ALU.add).then_inc(s_("pre_x"), 1)

        def norm_steps(ln, n, t):
            moments(ln, t)
            if t >= 1:
                gain(ln, n, t - 1)
            if t == T - 1:
                gain(ln, n, t)

        def residual(name, ln, n):
            c0, ra, _, _, g0, _ = BASE[name]
            for h in range(2):
                if h or n:
                    split(c0 + 2 * h + 1)
                split(c0 + 2 * h + 2)
                for t in range(T):
                    wait_tok(dve, t, g0 + h, c0 + 2 * h + 1)
                    stt(Y[:, t, 512 * h:512 * h + 512], X[:, t, 512 * h:512 * h + 512], ALPHA, A[t][:], ALU.mult, ALU.add).then_inc(a_free[t], 1)
                    dve.wait_ge(a_free[t], ra + h + 1)
                    if h == 0:
                        half_moments(t, 0)
                    else:
                        norm_steps(ln, n, t)

        dve.wait_ge(s_("toeplitz_out"), 16)
        residual("wo0", "ln0", 0)
        lo_transposed("ln0", XH, XL, b=ln_b(0))

        def mlp(name, before, ln, n):
            c0, ra, rb, _, g0, f0 = BASE[name]
            for t in range(T):
                dve.wait_ge(s_(before + "_y"), t + 1)

            def group(i, last):
                for j in range(4):
                    split(c0 + j + 1, 8, i)
                    for m in range(2):
                        n8 = 8 * i + 2 * j + m
                        dve.wait_ge(b_free[m], rb // 2 + j + 1 + i * 4)
                        tt(SQ_T[:, m, :], R_T[:, m, :], R_T[:, m, :], ALU.mult).then_inc(s_(name + "_sq"), 1)
                        dve.wait_ge(s_(name + "_hi"), n8 + 1)
                        tt(YL[:, 2 * j + m, :], SQ_T[:, m, :], f32(YH[:, 2 * j + m, :]), ALU.subtract).then_inc(s_(name + "_y"), 1)
                for h in range(2):
                    split(c0 + 4 + 2 * h + 1, 8, i)
                    split(c0 + 4 + 2 * h + 2, 8, i)
                    for t in range(T):
                        if t < 3:
                            dve.wait_ge(tok_done, 3 * (g0 + h) + t + 1 + i * 6)
                        else:
                            dve.wait_ge(chunk_done, c0 + 6 + 2 * h + i * 8)
                        y = Y[:, t, 512 * h:512 * h + 512]
                        tt(y, y, A[t][:], ALU.add).then_inc(a_free[t], 1)
                        if last:
                            dve.wait_ge(a_free[t], ra + 7 + h)
                            if h == 0:
                                half_moments(t, 0)
                            else:
                                norm_steps(ln, n, t)

            with dve.Fori(0, 3) as i:
                group(i, False)
            group(3, True)

        mlp("mlp0", "ln0", "ln1", 1)
        lo_transposed("ln1", XH, XL, b=ln_b(1))
        c0, _, _, _, _, f0 = BASE["kv"]
        for u in range(2):
            split(c0 + u + 1)
            wait_feat(dve, 1, f0 + u, c0 + u)
            nc.vector.tensor_copy(W_K[u][:, 1, :], B[1][:]).then_inc(b_free[1], 1)
        split(c0 + 3)
        c0, ra, rb, n0, _, f0 = BASE["swa"]
        dve.wait_ge(s_("ln1_x"), T)
        with dve.Fori(0, 2) as i:
            for u in range(2):
                split(c0 + u + 1, 2, i)
                dve.wait_ge(chunk_done, c0 + u + 1 + i * 2)
                ts(Y[:, 2:4, ds(i * 512 + 256 * u, 256)], B[1][:].rearrange("p (a n) -> p a n", a=2), SWA_DH ** -0.5, None,
                   ALU.mult).then_inc(b_free[1], 1)
        with dve.Fori(0, 2) as i:
            step.enter(i, 2 * T * 4)

            def block_max(j):
                u, n, z, bank = j // T, j % T, j % 2, 2 * (j % 2)
                w = 2 * P if n else P
                if n == 0:
                    dve.wait_ge(s_("bias_in%d" % u), 32 * i + 32)
                for e in range(2):
                    dve.wait_ge(s_("swa_s"), 16 * i + 2 * j + e + 1)
                    tt(W_S[:, z, 2 * e:2 * e + 2, 0:w],
                       A[bank + e][:].rearrange("p (q n) -> p q n", q=2)[:, :, 0:w],
                       W_B[:, u, 2 * e:2 * e + 2, 256 - w:256], ALU.add).then_inc(a_free[bank + e], 1)
                for e in range(2):
                    dve.wait_ge(a_free[bank + e], ra + j // 2 + 1 + 4 * i)
                then(nc.vector.tensor_reduce(stat(W_MAX + 4 * z, 4), W_S[:, z, :, 0:w], AX.X, ALU.max, negate=True))
                sink = st[:, ds(i * 8 + (NEGSINK + 4 * u), 4)]
                then(tt(stat(W_NEG + 4 * z, 4), stat(W_MAX + 4 * z, 4), sink, ALU.min))
                tt(stat(W_ES + 4 * z, 4), stat(W_NEG + 4 * z, 4), sink, ALU.subtract).then_inc(s_("swa_m"), 1)

            def block_out(j):
                u, n, z = j // T, j % T, j % 2
                dve.wait_ge(s_("swa_o"), 8 * i + j + 1)
                y = Y[:, n, ds(i * 512 + 256 * u, 256)].rearrange("p (q e d) -> p e q d", q=2, e=2)
                inv = stat(W_INV + 4 * z, 4).rearrange("p (e q) -> p e q", e=2).unsqueeze(3).broadcast_to([P, 2, 2, 64])
                tt(y, B[z][:, 0:256].rearrange("p (e q d) -> p e q d", e=2, q=2), inv, ALU.mult).then_inc(b_free[z], 1)

            block_max(0)
            block_max(1)
            for j in range(2 * T):
                z = j % 2
                dve.wait_ge(s_("swa_p"), 8 * i + j + 1)
                then(tt(stat(W_DEN + 4 * z, 4), stat(W_SUM + 4 * z, 4), stat(W_ES + 4 * z, 4), ALU.add))
                then(nc.vector.reciprocal(stat(W_INV + 4 * z, 4), stat(W_DEN + 4 * z, 4)))
                dve.wait_ge(s_("swa_t"), 16 * i + 2 * j + 2)
                dst = W_PT[:, 1, :] if j % T else W_PT[:, 1, 256:512]
                nc.vector.tensor_copy(dst, C[1][:, 0:512 if j % T else 256]).then_inc(c_free[1], 1)
                if j >= 1:
                    block_out(j - 1)
                if j + 2 < 2 * T:
                    block_max(j + 2)
            block_out(2 * T - 1)
        step.leave(2)
        lo_transposed("ot", YH, YL)
        residual("wo1", "ln2", 2)
        lo_transposed("ln2", XH, XL, b=ln_b(2))
        mlp("mlp1", "ln2", "ln3", 3)
        lo_transposed("pre", XH, XL, g=NG0)
        c0, _, _, _, _, f0 = BASE["if"]
        split(c0 + 1)
        nc.vector.memset(L_PRE, 0.0).then_inc(s_("ml_zero"), 1)
        then(nc.vector.memset(G_0, 0.0))
        wait_feat(dve, 0, f0, c0)
        ts(G_I, B[0][:], GATEB[:, 0:1], None, ALU.add).then_inc(b_free[0], 1)
        wait_feat(dve, 1, f0, c0)
        ts(G_F, B[1][:], GATEB[:, 1:2], None, ALU.add).then_inc(b_free[1], 1)
        dve.wait_ge(b_free[1], BASE["if"][2] // 2 + 1)
        stt(G_T, G_F, -1.0, G_F, ALU.mult, ALU.max).then_inc(s_("if_abs"), 1)
        split(BASE["ml"][0] + 1)
        dve.wait_ge(s_("if_l"), 1)
        then(stt(G_F, G_F, 0.0, G_L, ALU.min, ALU.subtract))
        then(nc.vector.tensor_tensor_scan(G_B, G_F, G_0, 0.0, ALU.add, ALU.add))
        dve.wait_ge(b_free[0], BASE["if"][2] // 2 + 1)
        then(tt(G_U, G_I, G_B, ALU.subtract))
        then(nc.vector.tensor_tensor_scan(G_M, G_U, G_U, 0.0, ALU.max, ALU.max))
        tt(G_EM, G_B, G_M, ALU.add).then_inc(s_("if_m"), 1)

        def values_by_token(name, i):
            for t in range(T):
                dve.wait_ge(s_(name + "_r"), T * i + t + 1)
                stt(L_H[:, t, :], L_H[:, t, :], stat(H_R + t), L_O[:, t, :], ALU.mult, ALU.mult).then_inc(s_(name + "_h"), 1)

        def head_lo(name, i, n0):
            for m in range(2):
                u = (n0 + m) % 2
                dve.wait_ge(s_(name + "_hi"), 2 * i + m + 1)
                tt(YL[:, ds(i * 2 + m, 1), :].rearrange("p a n -> p (a n)"), C[u][:],
                   f32(YH[:, ds(i * 2 + m, 1), :]).rearrange("p a n -> p (a n)"), ALU.subtract).then_inc(c_free[u], 1)

        c0, ra, rb, n0, _, f0 = BASE["ml"]
        dve.wait_ge(s_("ml_zero"), 1)

        def convolution(i, j):
            for m in range(2):
                dve.wait_ge(b_free[m], rb // 2 + 1 + j + 4 * i)
                if j or m or not isinstance(i, int):
                    dve.wait_ge(s_("ml_qk"), 4 * i + 2 * j + m)
                tap = [vec[:, ds(i * 2 + (CONV + 16 * q + 8 * j + m), 1)] for q in range(4)]
                then(ts(L_ACC, L_PRE[:, m, 0:S], tap[0], None, ALU.mult))
                then(stt(L_ACC, L_PRE[:, m, 1:1 + S], tap[1], L_ACC, ALU.mult, ALU.add))
                then(stt(L_ACC, L_PRE[:, m, 2:2 + S], tap[2], L_ACC, ALU.mult, ALU.add))
                stt(L_ACC, L_PRE[:, m, 3:3 + S], tap[3], L_ACC, ALU.mult, ALU.add).then_inc(s_("ml_conv"), 1)

        def mlstm_head(i, ahead):
            ts(L_M, G_M, ident[:, ds(i, 1)], None, ALU.mult).then_inc(s_("ml_m"), 1)
            split(c0 + 3, 4, i)
            convolution(i, 1)
            split(c0 + 4, 4, i)
            for j in range(T):
                n = S - j * P
                dve.wait_ge(s_("ml_s"), T * i + j + 1)
                dve.wait_ge(a_free[j], ra + 3 + 4 * i)
                stt(L_A[:, j, 0:n], A[j][:, 0:n], 1.0 / 16.0, L_A[:, j, 0:n], ALU.mult, ALU.mult).then_inc(a_free[j], 1)
            split(c0 + 5, 4, i)
            for t in range(T):
                dve.wait_ge(s_("ml_o"), T * i + t + 1)
                den = stat(H_DEN + t)
                then(nc.vector.tensor_copy(den, B[t % 2][:, 256:257]))
                then(stt(den, den, -1.0, den, ALU.mult, ALU.max))
                then(ts(den, den, st[:, ds(i + (EM_COL + 4 * t), 1)], None, ALU.max))
                nc.vector.reciprocal(stat(H_INV + t), den).then_inc(s_("ml_d"), 1)
            values_by_token("ml", i)
            split(c0 + 6, 4, i)
            if ahead:
                convolution(i + 1, 0)
            head_lo("ml", i, n0)

        split(c0 + 2)
        convolution(0, 0)
        for m, at in enumerate((U_COL, EM_COL)):
            u = (BASE["if"][3] + m) % 2
            dve.wait_ge(s_("if_t"), m + 1)
            nc.vector.tensor_copy(stat(at, 16).rearrange("p (t h) -> p t h", t=T),
                                  C[u][:].rearrange("p (t n) -> p t n", t=T)[:, :, 0:4]).then_inc(c_free[u], 1)
        then(nc.vector.memset(L_V[:, :, 256:258], 1.0))
        with dve.Fori(0, 3) as i:
            step.enter(i, 4 * 3 + 4 * 3)
            mlstm_head(i, True)
        step.leave(3)
        mlstm_head(3, False)

        def mix(name, n, split_to):
            c0, ra, _, _, g0, _ = BASE[name]
            for h in range(2):
                for kh in range(4):
                    j = 4 * h + kh
                    if j + 1 > split_to:
                        split(c0 + j + 1)
                for t in range(T):
                    wait_tok(dve, t, g0 + 2 * h + 1, c0 + 4 * h + 3)
                    dve.wait_ge(a_free[t], ra + 2 * h + 1)
                    y, tmp = Y[:, t, 512 * h:512 * h + 512], xtmp[:, t % 2, :]
                    if n == 0:
                        tt(y, GATE[:, t, :], A[t][:], ALU.mult).then_inc(a_free[t], 1)
                    else:
                        tt(tmp, GATE[:, t, :], A[t][:], ALU.mult).then_inc(a_free[t], 1)
                        dve.wait_ge(a_free[t], ra + 2 * h + 2)
                        tt(y, y, tmp, ALU.add).then_inc(s_("mixed"), 1)

        mix("mix0", 0, 2)
        c0, ra, rb, n0, _, f0 = BASE["ret"]
        dve.wait_ge(s_("decay_in"), 16)

        def retention_part(i, j):
            dve.wait_ge(chunk_done, c0 + j + 1 + i * 4)
            nc.vector.tensor_copy((L_Q, L_K)[j][:, 1, :], B[1][:]).then_inc(b_free[1], 1)

        def retention_head(i, ahead):
            retention_part(i, 1)
            split(c0 + 3, 4, i)
            split(c0 + 4, 4, i)
            for j in range(T):
                n = S - j * P
                dve.wait_ge(s_("ret_s"), T * i + j + 1)
                decay = DECAY[:, ds(i, 1), 0:n].rearrange("p a n -> p (a n)")
                tt(L_A[:, j, 0:n], A[j][:, 0:n], decay, ALU.mult).then_inc(a_free[j], 1)
            split(c0 + 5, 4, i)
            values_by_token("ret", i)
            if ahead:
                retention_part(i + 1, 0)
            split(c0 + 6, 4, i)
            head_lo("ret", i, n0)

        split(c0 + 1)
        retention_part(0, 0)
        split(c0 + 2)
        with dve.Fori(0, 3) as i:
            retention_head(i, True)
        retention_head(3, False)
        mix("mix1", 1, 2)
        c0 = BASE["dv"][0]
        for c in range(c0, c0 + 4):
            split(c + 1)
        c0, ra, rb, n0, _, f0 = BASE["diff"]
        dve.wait_ge(s_("alibi_in"), 16)
        def diff_slope(i, h):
            ts(slopes[:, h, :], ALIBI, st[:, ds(i * 2 + (SLOPE + h), 1)], None, ALU.mult).then_inc(s_("diff_b"), 1)

        def diff_features(i, j):
            dve.wait_ge(chunk_done, c0 + j + 1 + i * 2)
            ts((F_Q, F_K)[j][:, 1, :], B[1][:], DIFF_SCALE if j == 0 else 1.0, None, ALU.mult).then_inc(b_free[1], 1)

        def diff_max(i, h, q):
            for e in range(2):
                u = 2 * q + e
                dve.wait_ge(s_("diff_s"), 16 * i + 8 * h + u + 1)
                nc.vector.tensor_reduce(stat(NM + u), A[u % 4][:, 0:(q + 1) * P], AX.X, ALU.max,
                                        negate=True).then_inc(s_("diff_m"), 1)

        def diff_weights(i, h, q):
            n = (q + 1) * P
            for e in range(2):
                u = 2 * q + e
                dve.wait_ge(a_free[u % 4], ra + 2 * h + u // 4 + 1 + 4 * i)
            then(nc.vector.reciprocal(stat(RINV + 2 * q, 2), stat(SUM + 2 * q, 2)))
            if not (isinstance(i, int) and i == 0) or h or q >= 2:
                dve.wait_ge(s_("diff_t"), 8 * i + 4 * h + q - 1)
            then(ts(F_A[:, q % 2, 0:n], F_P[q % 2][:, 1, 0:n], stat(RINV + 2 * q + 1), stat(LAM + 2), ALU.mult, ALU.mult))
            stt(F_A[:, q % 2, 0:n], F_P[q % 2][:, 0, 0:n], stat(RINV + 2 * q), F_A[:, q % 2, 0:n], ALU.mult, ALU.add).then_inc(s_("diff_p"), 1)

        def diff_norm(i, h):
            dve.wait_ge(s_("diff_r"), 2 * i + h + 1)
            for q in range(T):
                x = ts(F_H[:, tok(q)], B[h][:, tok(q)], stat(H_R + q), None, ALU.mult)
            x.then_inc(b_free[h], 1)

        def diff_lo(i, h):
            u = (n0 + 5 * h + 4) % 2
            dve.wait_ge(s_("diff_hi"), 2 * i + h + 1)
            stt(YL[:, ds(i * 2 + h, 1), :].rearrange("p a n -> p (a n)"), C[u][:], vec[:, SUBLN:SUBLN + 1],
                f32(YH[:, ds(i * 2 + h, 1), :]).rearrange("p a n -> p (a n)"), ALU.mult, ALU.subtract).then_inc(c_free[u], 1)

        def diff_pair(i, ahead):
            for q in range(1, T):
                diff_weights(i, 0, q)
                diff_max(i, (q + 2) // T, (q + 2) % T)
            diff_max(i, 1, 2)
            diff_weights(i, 1, 0)
            diff_norm(i, 0)
            diff_max(i, 1, 3)
            diff_weights(i, 1, 1)
            if ahead:
                for h in range(2):
                    diff_slope(i + 1, h)
                split(c0 + 3, 2, i)
                diff_features(i + 1, 0)
            else:
                split(BASE["mix2"][0] + 1)
            diff_lo(i, 0)
            for q in (2, 3):
                diff_weights(i, 1, q)
            if ahead:
                split(c0 + 4, 2, i)
                diff_features(i + 1, 1)
                for q in (0, 1):
                    diff_max(i + 1, 0, q)
                diff_weights(i + 1, 0, 0)
            else:
                split(BASE["mix2"][0] + 2)
            diff_norm(i, 1)
            if ahead:
                diff_max(i + 1, 0, 2)
            diff_lo(i, 1)

        for h in range(2):
            diff_slope(0, h)
        for j in range(2):
            split(c0 + j + 1)
            diff_features(0, j)
        for q in (0, 1):
            diff_max(0, 0, q)
        diff_weights(0, 0, 0)
        diff_max(0, 0, 2)
        with dve.Fori(0, 3) as i:
            step.enter(i, 2 * T * 2)
            diff_pair(i, True)
        step.leave(3)
        diff_pair(3, False)
        mix("mix2", 2, 2)
        lo_transposed("yt", XH, XL)
        c0 = BASE["wout"][0]
        for c in range(c0, c0 + 4):
            split(c + 1)

        def add_normed(name, gb, t, after):
            if t == 0:
                dve.wait_ge(gb_in, gb)
            dve.wait_ge(s_(name + "_r"), t + 1)
            then(stt(Y[:, t, :], Y[:, t, :], stat(RS + t), GB[:, 0, :], ALU.mult, ALU.mult))
            tt(X[:, t, :], X[:, t, :], Y[:, t, :], ALU.add).then_inc(s_(after), 1)

        for t in range(T):
            add_normed("out", 4 * 32 + 16, t, "post_x")
        lo_transposed("post", XH, XL, g=NG2)
        c, ra, rb, _, g0, f0 = BASE["ffn"]
        use, done, silus = rb // 2, 0, 0
        for n, tiles in enumerate((8, 8, 6)):
            with dve.Fori(0, tiles // 2) as i:
                split(c + 1, 2, i)
                split(c + 2, 2, i)
                for m in range(2):
                    if m == 0:
                        dve.wait_ge(feat_done, f0 + 2 + i * 2)
                    else:
                        dve.wait_ge(chunk_done, c + 2 + i * 2)
                    dve.wait_ge(b_free[m], use + 1 + i * 2)
                    tt(PROD_T[:, m, :], SILU_T[:, m, :], B[m][:], ALU.mult).then_inc(b_free[m], 1)
                    dve.wait_ge(s_("ffn_hi"), done + m + 1 + i * 2)
                    tt(YL[:, ds(i * 2 + m, 1), :].rearrange("p a n -> p (a n)"), PROD_T[:, m, :],
                       f32(YH[:, ds(i * 2 + m, 1), :]).rearrange("p a n -> p (a n)"), ALU.subtract).then_inc(s_("ffn_y"), 1)
            c, f0, use, done = c + tiles, f0 + tiles, use + tiles, done + tiles
            for h in range(2):
                split(c + 1)
                split(c + 2)
                for t in range(T):
                    wait_tok(dve, t, g0 + 2 * n + h, c + 1)
                    y = Y[:, t, 512 * h:512 * h + 512]
                    if n == 0:
                        nc.vector.tensor_copy(y, A[t][:]).then_inc(a_free[t], 1)
                    else:
                        tt(y, y, A[t][:], ALU.add).then_inc(a_free[t], 1)
                    if n == 2 and h == 1 and t >= 1:
                        add_normed("fin", 4 * 32 + 32, t - 1, "fin_x")
                c += 2
        add_normed("fin", 4 * 32 + 32, T - 1, "fin_x")

    @block.gpsimd
    def _(pool):
        step = Tally(pool_step)
        tt, ts = nc.gpsimd.tensor_tensor, nc.gpsimd.tensor_scalar

        def then(x):
            step.then(pool, x)

        nc.gpsimd.memset(st[:], 0.0).then_inc(s_("st_zero"), 1)
        pool.wait_ge(s_("st_zero"), 1)
        for at, value in ((NEGHALF, -0.5), (EPSILON, RMS_EPS)):
            then(nc.gpsimd.memset(stat(at, T), value))

        def flat(v):
            return v.rearrange("(a n) -> a n", a=1)

        for dst, src in (
                (CAUSAL_T, a["c_causal"]), (FUTURE_T, a["c_future"]),
                (cosT, a["c_cos"]), (sinT, a["c_sin"]), (RELB, a["rel_bias"]), (ONEHOT, a["c_onehot"]),
                (WINDOW_T, a["c_window"]), (stat(SLOPE, 8), a["c_slope"]),
                (SINK_T, a["swa_sinks"].broadcast_to([P, 16])),
                (LAMB_T.rearrange("p a n -> p (a n)"),
                 a["diff_lambda_2"].rearrange("a l n -> a (l n)").broadcast_to([P, 256])),
                (GATEB[0:4, :], a["mlstm_gate_bias_2"][0].rearrange("g h -> h g"))):
            pool.dma_start(dst, src, allow_slow_non_contiguous=True).then_inc(consts_in, 16)
        pool.wait_ge(rows_zero, 1)
        vectors = []
        for n in range(3):
            v = a[("ln_mix_b", "ln_mlp_b")[n % 2]][n // 2]
            vectors.append((ln_b(n), KD, 0, v.rearrange("(k p) -> k p", p=P)))
        for at, n in ((NG0, 0), (NG2, 2)):
            vectors.append((at, KD, 0, a["norm_gains_2"][0, n].rearrange("(k p) -> k p", p=P)))
        vectors.append((GQ, 3, 0, a["mla_g_q"][0].rearrange("(k p) -> k p", p=P)))
        vectors.append((GKV, 2, 0, a["mla_g_kv"][0].rearrange("(k p) -> k p", p=P)))
        vectors.append((SUBLN, 1, 0, a["diff_subln_2"][0].rearrange("(k p) -> k p", p=P)))
        vectors.append((0, 64, 1, a["mlstm_conv_2"][0].rearrange("j (k p) -> (j k) p", p=P)))
        assert len(vectors) == ROWS_N
        for at, n, m, src in vectors:
            pool.dma_start(ROWS_T[at:at + n, m, :], src).then_inc(rows_in, 16)

        def load_gb(*vs):
            for n, v in enumerate(vs):
                pool.dma_start(GB[:, n, :], flat(v).broadcast_to([P, D])).then_inc(gb_in, 16)

        load_gb(a["ln_mix_g"][0], a["ln_mix_b"][0])

        def over_root(dst, src, eps, signal):
            then(ts(stat(dst), stat(src), eps, None, ALU.add))
            tt(stat(dst), stat(dst), stat(NEGHALF), ALU.pow).then_inc(signal, 1)

        for n in range(2):
            for t in range(T):
                pool.wait_ge(s_("in_ss"), 4 * n + t + 1)
                over_root(RS + 4 * n + t, SS + 4 * n + t, RMS_EPS, s_("in_r"))
        pool.wait_ge(consts_done, 1)
        pool.dma_start(scr, HEADS_T.unsqueeze(1).broadcast_to([16, P, 3 * P])).then_inc(s_("toeplitz_out"), 16)

        def layer_norm(ln, t):
            pool.wait_ge(s_(ln + "_st"), t + 1)
            then(ts(stat(RS + t), stat(MV + 2 * t + 1), LN_EPS, None, ALU.add))
            then(tt(stat(RS + t), stat(RS + t), stat(NEGHALF), ALU.pow))
            ts(stat(NMR + t), stat(MV + 2 * t), stat(RS + t), -1.0, ALU.mult, ALU.mult).then_inc(s_(ln + "_r"), 1)

        def layer_norms(ln, ahead):
            for t in range(T):
                layer_norm(ln, t)
            for t in range(T):
                pool.wait_ge(s_(ln + "_g"), t + 1)
                x = tt(X[:, t, :], Y[:, t, :], GB[:, 1, :], ALU.add)
                if ahead:
                    then(x)
                else:
                    x.then_inc(s_(ln + "_x"), 1)
            if ahead:
                pool.wait_ge(s_(ln + "_t"), KD)
                for t in range(T):
                    ts(Y[:, t, :], X[:, t, :], ALPHA, None, ALU.mult).then_inc(s_(ln + "_y"), 1)

        layer_norms("ln0", True)
        load_gb(a["ln_mlp_g"][0], a["ln_mlp_b"][0])
        layer_norms("ln1", False)
        pool.wait_ge(s_("ln1_x"), T)
        load_gb(a["ln_mix_g"][1], a["ln_mix_b"][1])
        pool.wait_ge(s_("toeplitz_out"), 16)
        rb = BASE["swa"][2]
        for g in range(SWA_KV):
            for m in range(2):
                pool.wait_ge(b_free[m], rb // 2 + g + 1)
            if g >= 2:
                pool.wait_ge(s_("swa_s"), 8 * (g - 1))
            then(nc.gpsimd.tensor_copy(W_Q[:, g % 2].rearrange("p q (a n) -> p (q a) n", a=2), Y[:, :, 256 * g:256 * g + 256]))
            for e in range(2):
                rows = slice(64 * e, 64 * e + 64)
                x = nc.gpsimd.tensor_copy(W_KG[rows, g % 2, :], W_K[int(e != g % 2)][rows, g // 2, :])
                if e == 0:
                    then(x)
            x.then_inc(s_("swa_k"), 1)
            pool.wait_ge(s_("swa_k"), g + 1)
            if g >= 2:
                pool.wait_ge(s_("swa_m"), 4 * (g - 1))
            for e in range(2):
                rows = bass.AP(scr.tensor, (4 * g + e) * 3 * P * P + P - 1, [[3 * P - 1, P], [2 * 3 * P * P, 2], [1, 2 * P]])
                pool.dma_start(W_B[:, g % 2, 2 * e:2 * e + 2, :], rows).then_inc(s_("bias_in%d" % (g % 2)), 16)
        layer_norms("ln2", True)
        load_gb(a["ln_mlp_g"][1], a["ln_mlp_b"][1])
        for t in range(T + 2):
            if t < T:
                layer_norm("ln3", t)
            if t >= 2:
                pool.wait_ge(s_("pre_ss"), t - 1)
                over_root(H_R + t - 2, H_SS + t - 2, RMS_EPS, s_("pre_r"))

        def heads_rms(name):
            with pool.Fori(0, 4) as i:
                step.enter(i, T)
                for t in range(T):
                    pool.wait_ge(s_(name + "_ss"), T * i + t + 1)
                    then(tt(stat(H_R + t), stat(H_SS + t), stat(EPSILON), ALU.add))
                    tt(stat(H_R + t), stat(H_R + t), stat(NEGHALF), ALU.pow).then_inc(s_(name + "_r"), 1)
            step.leave(4)

        heads_rms("ml")
        pool.wait_ge(chunk_done, BASE["mix0"][0] + 1)
        pool.dma_start(DECAY, a["c_decay"]).then_inc(s_("decay_in"), 16)
        heads_rms("ret")
        pool.wait_ge(s_("mixed"), 8)
        pool.dma_start(ALIBI, a["c_alibi"]).then_inc(s_("alibi_in"), 16)
        with pool.Fori(0, 4) as i:
            step.enter(i, 2)
            for h in range(2):
                pool.wait_ge(s_("diff_ss"), 2 * i + h + 1)
                then(tt(stat(H_R, T), stat(H_SS, T), stat(EPSILON, T), ALU.add))
                tt(stat(H_R, T), stat(H_R, T), stat(NEGHALF, T), ALU.pow).then_inc(s_("diff_r"), 1)
        step.leave(4)
        pool.wait_ge(s_("mixed"), 16)
        load_gb(a["norm_gains_2"][0, 1])

        def root_of_halves(name, wait, t):
            wait(t)
            then(tt(stat(SS + t), stat(SS + t), stat(SS + 4 + t), ALU.add))
            over_root(RS + t, SS + t, RMS_EPS, s_(name + "_r"))

        ra = BASE["wout"][1]
        for t in range(T + 1):
            if t < T:
                root_of_halves("out", lambda t: pool.wait_ge(a_free[t], ra + 2), t)
            if t >= 1:
                pool.wait_ge(s_("post_ss"), t)
                over_root(H_R + t - 1, H_SS + t - 1, RMS_EPS, s_("post_r"))
        pool.wait_ge(s_("post_x"), T)
        load_gb(a["norm_gains_2"][0, 3])
        for t in range(T):
            root_of_halves("fin", lambda t: pool.wait_ge(s_("fin_ss"), T + t + 1), t)

    ctx.close()


def kernel(**inputs):
    import concourse.bacc as bacc
    from concourse import mybir
    from concourse.bass_utils import run_bass_kernel_spmd

    nc = bacc.Bacc("TRN2", target_bir_lowering=False, num_devices=1)
    arrays, aps = {}, {}
    for name, value in {**inputs, **constants()}.items():
        v = np.ascontiguousarray(value)
        arrays["in_" + name] = v
        aps[name] = nc.dram_tensor("in_" + name, v.shape, mybir.dt.from_np(v.dtype), kind="ExternalInput").ap()
    out = nc.dram_tensor("out", (1, S, D), mybir.dt.float32, kind="ExternalOutput").ap()
    build(nc, aps, out)
    return run_bass_kernel_spmd(nc, [arrays], core_ids=[0]).results[0]["out"]
```
